# Optimizing a Trainium2 kernel written in Bass

```python
import jax, jax.numpy as jnp
from jax import lax
import numpy as np
import math

D_MODEL = 1024
BATCH = 1
SEQ = 256
DEPTH = 2

MLA_HEADS = 8
MLA_NOPE = 64
MLA_ROPE = 32
MLA_V = 64
Q_LORA = 384
KV_LORA = 256
ROPE_BASE = 10000.0
DSA_HEADS = 8
DSA_DIM = 64
IDX_HEADS = 8
IDX_DIM = 32
TOPK_MAX = 256
D_MIX = MLA_HEADS * MLA_V + DSA_HEADS * DSA_DIM
N_EXPERTS = 16
N_GROUPS = 4
EXPERTS_PER_GROUP = N_EXPERTS // N_GROUPS
TOP_K_EXPERTS = 2
GROUP_SCORE_K = 2
D_FF_EXPERT = 512
ALPHA = (2.0 * DEPTH) ** 0.25
BETA = (8.0 * DEPTH) ** -0.25
Q_BLOCK = 128
LN_EPS = 1e-5
RMS_EPS = 1e-6

SPLIT_SIZES = (Q_LORA, KV_LORA, MLA_ROPE, DSA_HEADS * DSA_DIM, DSA_DIM, DSA_DIM,
               IDX_HEADS * IDX_DIM, IDX_DIM, IDX_HEADS)
SPLIT_POINTS = tuple(int(v) for v in np.cumsum(SPLIT_SIZES)[:-1])
IN_COLS = int(sum(SPLIT_SIZES))
DSA_V_START = int(sum(SPLIT_SIZES[:5]))


def layer_norm(x, g, b):
    xf = x.astype(jnp.float32)
    mu = jnp.mean(xf, axis=-1, keepdims=True)
    var = jnp.mean(jnp.square(xf - mu), axis=-1, keepdims=True)
    y = (xf - mu) * lax.rsqrt(var + LN_EPS) * g.astype(jnp.float32) + b.astype(jnp.float32)
    return y.astype(x.dtype)

def rms_norm(x, g):
    xf = x.astype(jnp.float32)
    y = xf * lax.rsqrt(jnp.mean(jnp.square(xf), axis=-1, keepdims=True) + RMS_EPS)
    return (y * g.astype(jnp.float32)).astype(x.dtype)

def rope(x, pos):
    half = x.shape[-1] // 2
    inv = ROPE_BASE ** (-jnp.arange(half, dtype=jnp.float32) / half)
    ang = pos[:, None] * inv[None, :]
    cos = jnp.cos(ang)[None, :, None, :]
    sin = jnp.sin(ang)[None, :, None, :]
    xf = x.astype(jnp.float32)
    x1, x2 = xf[..., :half], xf[..., half:]
    return jnp.concatenate([x1 * cos - x2 * sin, x1 * sin + x2 * cos], axis=-1).astype(x.dtype)

def sweep_query_blocks(block_fn, seq_len):
    starts = jnp.arange(seq_len // Q_BLOCK, dtype=jnp.int32) * Q_BLOCK
    out = lax.map(block_fn, starts)
    nb, b, qb, h, d = out.shape
    return jnp.transpose(out, (1, 0, 2, 3, 4)).reshape(b, nb * qb, h * d)

def mla_group(qa, kva, kr, q_norm_g, w_q_up, kv_norm_g, w_uk, w_uv, pos):
    B, T, _ = qa.shape
    q = (rms_norm(qa, q_norm_g) @ w_q_up).reshape(B, T, MLA_HEADS, MLA_NOPE + MLA_ROPE)
    q = jnp.concatenate([q[..., :MLA_NOPE], rope(q[..., MLA_NOPE:], pos)], axis=-1)
    c_kv = rms_norm(kva, kv_norm_g)
    k_nope = (c_kv @ w_uk).reshape(B, T, MLA_HEADS, MLA_NOPE)
    v = (c_kv @ w_uv).reshape(B, T, MLA_HEADS, MLA_V)
    k_rope = rope(kr[:, :, None, :], pos)
    k = jnp.concatenate([k_nope, jnp.broadcast_to(k_rope, (B, T, MLA_HEADS, MLA_ROPE))], axis=-1)
    scale = (MLA_NOPE + MLA_ROPE) ** -0.5
    key_idx = jnp.arange(T, dtype=jnp.int32)

    def block(start):
        qb = lax.dynamic_slice_in_dim(q, start, Q_BLOCK, axis=1)
        s = jnp.einsum('bthd,bshd->bhts', qb, k).astype(jnp.float32) * scale
        tq = start + jnp.arange(Q_BLOCK, dtype=jnp.int32)
        s = jnp.where(key_idx[None, :] <= tq[:, None], s, -jnp.inf)
        p = jax.nn.softmax(s, axis=-1).astype(v.dtype)
        return jnp.einsum('bhts,bshd->bthd', p, v)

    return sweep_query_blocks(block, T)

def dsa_group(dq, dk, dv, iq, ik, iw, slopes, n_keep):
    B, T, _ = dq.shape
    q = dq.reshape(B, T, DSA_HEADS, DSA_DIM)
    iq = iq.reshape(B, T, IDX_HEADS, IDX_DIM)
    iw = iw * (IDX_HEADS ** -0.5)
    key_idx = jnp.arange(T, dtype=jnp.int32)
    scale = DSA_DIM ** -0.5
    gather = jax.vmap(lambda arr, idx: arr[idx])

    def block(start):
        qb = lax.dynamic_slice_in_dim(q, start, Q_BLOCK, axis=1)
        iqb = lax.dynamic_slice_in_dim(iq, start, Q_BLOCK, axis=1)
        iwb = lax.dynamic_slice_in_dim(iw, start, Q_BLOCK, axis=1)
        tq = start + jnp.arange(Q_BLOCK, dtype=jnp.int32)
        rel = jax.nn.relu(jnp.einsum('bthd,bsd->bths', iqb, ik) * (IDX_DIM ** -0.5))
        score = jnp.einsum('bths,bth->bts', rel, iwb).astype(jnp.float32)
        score = jnp.where(key_idx[None, None, :] <= tq[None, :, None], score, -jnp.inf)
        _, sel = lax.top_k(score, n_keep)
        k_sel = gather(dk, sel)
        v_sel = gather(dv, sel)
        dist = (tq[None, :, None] - sel).astype(jnp.float32)
        s = jnp.einsum('bthd,btkd->bhtk', qb, k_sel).astype(jnp.float32) * scale
        s = s - slopes[None, :, None, None] * dist[:, None, :, :]
        s = jnp.where((dist >= 0.0)[:, None, :, :], s, -jnp.inf)
        p = jax.nn.softmax(s, axis=-1).astype(v_sel.dtype)
        return jnp.einsum('bhtk,btkd->bthd', p, v_sel)

    return sweep_query_blocks(block, T)

def hybrid_mixer(h, w_in, q_norm_g, w_q_up, kv_norm_g, w_uk, w_uv, w_o, pos, slopes, n_keep):
    proj = h @ w_in
    qa, kva, kr, dq, dk, dv, iq, ik, iw = jnp.split(proj, SPLIT_POINTS, axis=-1)
    out_a = mla_group(qa, kva, kr, q_norm_g, w_q_up, kv_norm_g, w_uk, w_uv, pos)
    out_b = dsa_group(dq, dk, dv, iq, ik, iw, slopes, n_keep)
    return jnp.concatenate([out_a, out_b], axis=-1) @ w_o

def grouped_moe(h, router_w, router_bias, w_gate, w_up, w_down):
    B, T, D = h.shape
    xt = h.reshape(B * T, D)
    aff = jax.nn.sigmoid((xt @ router_w).astype(jnp.float32))
    biased = aff + router_bias.astype(jnp.float32)
    grouped = biased.reshape(-1, N_GROUPS, EXPERTS_PER_GROUP)
    group_score = jnp.sum(lax.top_k(grouped, GROUP_SCORE_K)[0], axis=-1)
    g_sel = jnp.argmax(group_score, axis=-1)
    in_group = (jnp.arange(N_EXPERTS) // EXPERTS_PER_GROUP)[None, :] == g_sel[:, None]
    _, e_idx = lax.top_k(jnp.where(in_group, biased, -jnp.inf), TOP_K_EXPERTS)
    wts = jnp.take_along_axis(aff, e_idx, axis=-1)
    wts = wts / jnp.sum(wts, axis=-1, keepdims=True)
    gates = jnp.sum(jax.nn.one_hot(e_idx, N_EXPERTS, dtype=jnp.float32) * wts[..., None], axis=1)
    hg = jnp.einsum('nd,edf->nef', xt, w_gate)
    hu = jnp.einsum('nd,edf->nef', xt, w_up)
    act = jax.nn.silu(hg) * hu * gates[:, :, None].astype(hg.dtype)
    out = jnp.einsum('nef,efd->nd', act, w_down)
    return out.reshape(B, T, D)

def first_inputs(seed: int = 0) -> dict:
    key = jax.random.key(seed)
    ks = jax.random.split(key, 20)
    f32 = jnp.float32
    nrm = lambda k, shape, s: jax.random.normal(k, shape, f32) * s
    col_scale = np.ones((IN_COLS,), np.float32)
    col_scale[DSA_V_START:DSA_V_START + DSA_DIM] = BETA
    w_in = nrm(ks[1], (DEPTH, D_MODEL, IN_COLS), D_MODEL ** -0.5) * jnp.asarray(col_scale)
    return {
        'x': jax.random.normal(ks[0], (BATCH, SEQ, D_MODEL), f32),
        'w_in': w_in,
        'q_norm_g': 1.0 + nrm(ks[2], (DEPTH, Q_LORA), 0.02),
        'w_q_up': nrm(ks[3], (DEPTH, Q_LORA, MLA_HEADS * (MLA_NOPE + MLA_ROPE)), Q_LORA ** -0.5),
        'kv_norm_g': 1.0 + nrm(ks[4], (DEPTH, KV_LORA), 0.02),
        'w_uk': nrm(ks[5], (DEPTH, KV_LORA, MLA_HEADS * MLA_NOPE), KV_LORA ** -0.5),
        'w_uv': nrm(ks[6], (DEPTH, KV_LORA, MLA_HEADS * MLA_V), BETA * KV_LORA ** -0.5),
        'w_o': nrm(ks[7], (DEPTH, D_MIX, D_MODEL), BETA * D_MIX ** -0.5),
        'ln1_g': 1.0 + nrm(ks[8], (DEPTH, D_MODEL), 0.02),
        'ln1_b': nrm(ks[9], (DEPTH, D_MODEL), 0.02),
        'router_w': nrm(ks[10], (D_MODEL, N_EXPERTS), D_MODEL ** -0.5),
        'router_bias': nrm(ks[11], (N_EXPERTS,), 0.01),
        'w_gate': nrm(ks[12], (DEPTH, N_EXPERTS, D_MODEL, D_FF_EXPERT), BETA * D_MODEL ** -0.5),
        'w_up': nrm(ks[13], (DEPTH, N_EXPERTS, D_MODEL, D_FF_EXPERT), BETA * D_MODEL ** -0.5),
        'w_down': nrm(ks[14], (DEPTH, N_EXPERTS, D_FF_EXPERT, D_MODEL), BETA * D_FF_EXPERT ** -0.5),
        'ln2_g': 1.0 + nrm(ks[15], (DEPTH, D_MODEL), 0.02),
        'ln2_b': nrm(ks[16], (DEPTH, D_MODEL), 0.02),
    }

def first_block(x, w_in, q_norm_g, w_q_up, kv_norm_g, w_uk, w_uv, w_o, ln1_g, ln1_b,
              router_w, router_bias, w_gate, w_up, w_down, ln2_g, ln2_b):
    T = x.shape[1]
    pos = jnp.arange(T, dtype=jnp.float32)
    n_keep = min(TOPK_MAX, T // 4)
    slopes = 2.0 ** (-8.0 * jnp.arange(1, DSA_HEADS + 1, dtype=jnp.float32) / DSA_HEADS)
    for l in range(DEPTH):
        mix = hybrid_mixer(x, w_in[l], q_norm_g[l], w_q_up[l], kv_norm_g[l], w_uk[l], w_uv[l],
                           w_o[l], pos, slopes, n_keep)
        x = layer_norm(ALPHA * x + mix, ln1_g[l], ln1_b[l])
        ffn = grouped_moe(x, router_w, router_bias, w_gate[l], w_up[l], w_down[l])
        x = layer_norm(ALPHA * x + ffn, ln2_g[l], ln2_b[l])
    return x


N_A_LAYERS = DEPTH // 2
N_B_LAYERS = DEPTH - N_A_LAYERS
HG_HEADS = 8
HG_DIM = D_MODEL // HG_HEADS
HG_CHUNK = 32
SW_Q_HEADS = 16
SW_KV_HEADS = 4
SW_HEAD_DIM = D_MODEL // SW_Q_HEADS
SW_GROUP = SW_Q_HEADS // SW_KV_HEADS
SW_WINDOW = 128
REL_BUCKETS = 32
REL_MAX_DIST = 128
FFN_DIM = 2816
CONV_WIDTH = 3
ALPHA_2 = (2.0 * DEPTH) ** 0.25
BETA_2 = (8.0 * DEPTH) ** -0.25


def layer_norm_2(x, g, b):
    xf = x.astype(jnp.float32)
    mu = xf.mean(-1, keepdims=True)
    var = jnp.square(xf - mu).mean(-1, keepdims=True)
    y = (xf - mu) * lax.rsqrt(var + LN_EPS) * g.astype(jnp.float32) + b.astype(jnp.float32)
    return y.astype(x.dtype)

def hgrn2_chunkwise(q, k, v, log_f):
    B, S, H, Dk = q.shape
    Dv = v.shape[-1]
    n = S // HG_CHUNK

    def chunks(a):
        return a.reshape(B, n, HG_CHUNK, H, a.shape[-1]).transpose(1, 0, 3, 2, 4)

    qc, kc, vc = chunks(q), chunks(k), chunks(v)
    bc = jnp.cumsum(chunks(log_f), axis=3)
    causal = jnp.tril(jnp.ones((HG_CHUNK, HG_CHUNK), dtype=bool))[:, :, None]

    def step(state, inp):
        q_, k_, v_, b_ = inp
        o_inter = jnp.einsum('bhtk,bhkv->bhtv', q_ * jnp.exp(b_), state)
        diff = b_[:, :, :, None, :] - b_[:, :, None, :, :]
        decay = jnp.where(causal, jnp.exp(jnp.minimum(diff, 0.0)), 0.0)
        scores = jnp.einsum('bhtsk,bhsk->bhts', q_[:, :, :, None, :] * decay, k_)
        o = o_inter + jnp.einsum('bhts,bhsv->bhtv', scores, v_)
        b_last = b_[:, :, -1, :]
        k_dec = k_ * jnp.exp(b_last[:, :, None, :] - b_)
        state = jnp.exp(b_last)[..., None] * state + jnp.einsum('bhsk,bhsv->bhkv', k_dec, v_)
        return state, o

    state0 = jnp.zeros((B, H, Dk, Dv), jnp.float32)
    _, o = lax.scan(step, state0, (qc, kc, vc, bc))
    return o.transpose(1, 0, 3, 2, 4).reshape(B, S, H, Dv)

def hgrn2_mixer(h, w_in, lower_bound, g_norm_w, w_out):
    B, S, D = h.shape
    q, f, i, g = jnp.split(h @ w_in, 4, axis=-1)

    def heads(a):
        return a.reshape(B, S, HG_HEADS, HG_DIM).astype(jnp.float32)

    lb = lower_bound.astype(jnp.float32).reshape(HG_HEADS, HG_DIM)
    fg = lb + (1.0 - lb) * jax.nn.sigmoid(heads(f))
    o = hgrn2_chunkwise(jax.nn.silu(heads(q)), 1.0 - fg, heads(i), jnp.log(fg))
    o = o * lax.rsqrt(jnp.mean(jnp.square(o), -1, keepdims=True) + RMS_EPS)
    o = o * g_norm_w.astype(jnp.float32) * jax.nn.silu(heads(g))
    return o.reshape(B, S, D).astype(h.dtype) @ w_out

def t5_causal_bucket(dist):
    exact = REL_BUCKETS // 2
    d = jnp.maximum(dist, 1).astype(jnp.float32)
    log_b = exact + (jnp.log(d / exact) / math.log(REL_MAX_DIST / exact)
                     * (REL_BUCKETS - exact)).astype(jnp.int32)
    return jnp.where(dist < exact, dist, jnp.minimum(log_b, REL_BUCKETS - 1))

def banded_bias_and_mask(rel_table, n_blocks):
    t = jnp.arange(SW_WINDOW)[:, None] + SW_WINDOW
    s = jnp.arange(2 * SW_WINDOW)[None, :]
    dist = t - s
    bias = rel_table[t5_causal_bucket(jnp.maximum(dist, 0))].transpose(2, 0, 1)
    band = (dist >= 0) & (dist < SW_WINDOW)
    has_prev = (jnp.arange(n_blocks) > 0)[:, None, None]
    mask = band[None] & (has_prev | (s >= SW_WINDOW)[None])
    return bias, mask

def swa_sink_mixer(h, k, v, w_q, sinks, bias, mask, w_out):
    B, S, D = h.shape
    nb = S // SW_WINDOW
    q = (h @ w_q).reshape(B, nb, SW_WINDOW, SW_KV_HEADS, SW_GROUP, SW_HEAD_DIM)

    def with_prev(a):
        ab = a.reshape(B, nb, SW_WINDOW, SW_KV_HEADS, SW_HEAD_DIM)
        prev = jnp.pad(ab, ((0, 0), (1, 0), (0, 0), (0, 0), (0, 0)))[:, :-1]
        return jnp.concatenate([prev, ab], axis=2)

    kk, vv = with_prev(k), with_prev(v)
    scale = SW_HEAD_DIM ** -0.5
    logits = jnp.einsum('bntgrd,bnsgd->bngrts', q, kk).astype(jnp.float32) * scale
    logits = logits + bias.astype(jnp.float32).reshape(SW_KV_HEADS, SW_GROUP, SW_WINDOW, 2 * SW_WINDOW)
    logits = jnp.where(mask[None, :, None, None], logits, -jnp.inf)
    sink = sinks.astype(jnp.float32).reshape(1, 1, SW_KV_HEADS, SW_GROUP, 1)
    m = jnp.maximum(logits.max(-1), sink)
    p = jnp.exp(logits - m[..., None])
    denom = p.sum(-1) + jnp.exp(sink - m)
    o = jnp.einsum('bngrts,bnsgd->bntgrd', p, vv.astype(jnp.float32))
    o = o / jnp.moveaxis(denom, -1, 2)[..., None]
    return o.reshape(B, S, D).astype(h.dtype) @ w_out

def conv_ffn(h, w_in, conv_w, conv_b, w_out):
    u = h @ w_in
    C = u.shape[-1]
    u = lax.conv_general_dilated(u, conv_w[:, None, :], window_strides=(1,),
                                 padding=[(CONV_WIDTH - 1, 0)],
                                 dimension_numbers=('NWC', 'WIO', 'NWC'),
                                 feature_group_count=C) + conv_b
    a, b = jnp.split(u, 2, axis=-1)
    return (jax.nn.silu(a) * b) @ w_out

def second_inputs(seed: int = 0) -> dict:
    key = jax.random.key(seed)
    ks = jax.random.split(key, 24)
    D, F = D_MODEL, FFN_DIM
    kv_dim = SW_KV_HEADS * SW_HEAD_DIM
    nrm = jax.random.normal

    x = nrm(ks[0], (BATCH, SEQ, D), jnp.float32)

    hgrn_w_in = nrm(ks[1], (N_A_LAYERS, D, 4 * D), jnp.float32) * D ** -0.5
    hgrn_w_in = hgrn_w_in.at[..., 2 * D:3 * D].multiply(BETA_2)
    hgrn_lb_logits = nrm(ks[2], (N_A_LAYERS + 1, D), jnp.float32) * 0.5
    hgrn_gnorm_w = 1.0 + 0.02 * nrm(ks[3], (N_A_LAYERS, HG_DIM), jnp.float32)
    hgrn_w_out = nrm(ks[4], (N_A_LAYERS, D, D), jnp.float32) * D ** -0.5 * BETA_2

    swa_w_q = nrm(ks[5], (N_B_LAYERS, D, D), jnp.float32) * D ** -0.5
    swa_sinks = nrm(ks[6], (N_B_LAYERS, SW_Q_HEADS), jnp.float32) * 0.5
    swa_w_out = nrm(ks[7], (N_B_LAYERS, D, D), jnp.float32) * D ** -0.5 * BETA_2
    shared_w_kv = nrm(ks[8], (D, 2 * kv_dim), jnp.float32) * D ** -0.5
    shared_w_kv = shared_w_kv.at[:, kv_dim:].multiply(BETA_2)
    rel_bias = nrm(ks[9], (REL_BUCKETS, SW_Q_HEADS), jnp.float32) * 0.5

    ffn_w_in = nrm(ks[10], (DEPTH, D, 2 * F), jnp.float32) * D ** -0.5 * BETA_2
    ffn_conv_w = nrm(ks[11], (DEPTH, CONV_WIDTH, 2 * F), jnp.float32) * CONV_WIDTH ** -0.5
    ffn_conv_b = nrm(ks[12], (DEPTH, 2 * F), jnp.float32) * 0.02
    ffn_w_out = nrm(ks[13], (DEPTH, F, D), jnp.float32) * F ** -0.5 * BETA_2

    ln_mix_g = 1.0 + 0.02 * nrm(ks[14], (DEPTH, D), jnp.float32)
    ln_mix_b = 0.02 * nrm(ks[15], (DEPTH, D), jnp.float32)
    ln_ffn_g = 1.0 + 0.02 * nrm(ks[16], (DEPTH, D), jnp.float32)
    ln_ffn_b = 0.02 * nrm(ks[17], (DEPTH, D), jnp.float32)

    return {"x": x, "hgrn_w_in": hgrn_w_in, "hgrn_lb_logits": hgrn_lb_logits,
            "hgrn_gnorm_w": hgrn_gnorm_w, "hgrn_w_out": hgrn_w_out,
            "swa_w_q": swa_w_q, "swa_sinks": swa_sinks, "swa_w_out": swa_w_out,
            "shared_w_kv": shared_w_kv, "rel_bias": rel_bias,
            "ffn_w_in": ffn_w_in, "ffn_conv_w": ffn_conv_w, "ffn_conv_b": ffn_conv_b,
            "ffn_w_out": ffn_w_out, "ln_mix_g": ln_mix_g, "ln_mix_b": ln_mix_b,
            "ln_ffn_g": ln_ffn_g, "ln_ffn_b": ln_ffn_b}

def second_block(x, hgrn_w_in, hgrn_lb_logits, hgrn_gnorm_w, hgrn_w_out,
              swa_w_q, swa_sinks, swa_w_out, shared_w_kv, rel_bias,
              ffn_w_in, ffn_conv_w, ffn_conv_b, ffn_w_out,
              ln_mix_g, ln_mix_b, ln_ffn_g, ln_ffn_b):
    B, S, D = x.shape
    n_blocks = S // SW_WINDOW
    lower_bounds = jnp.cumsum(jax.nn.softmax(hgrn_lb_logits.astype(jnp.float32), axis=0), axis=0)
    bias, mask = banded_bias_and_mask(rel_bias, n_blocks)

    h = x
    k_shared = v_shared = None
    for layer in range(DEPTH):
        if layer < N_A_LAYERS:
            mix = hgrn2_mixer(h, hgrn_w_in[layer], lower_bounds[layer],
                              hgrn_gnorm_w[layer], hgrn_w_out[layer])
        else:
            j = layer - N_A_LAYERS
            mix = swa_sink_mixer(h, k_shared, v_shared, swa_w_q[j], swa_sinks[j],
                                 bias, mask, swa_w_out[j])
        h = layer_norm_2(ALPHA_2 * h + mix, ln_mix_g[layer], ln_mix_b[layer])
        ff = conv_ffn(h, ffn_w_in[layer], ffn_conv_w[layer], ffn_conv_b[layer], ffn_w_out[layer])
        h = layer_norm_2(ALPHA_2 * h + ff, ln_ffn_g[layer], ln_ffn_b[layer])
        if layer == N_A_LAYERS - 1:
            k_flat, v_flat = jnp.split(h @ shared_w_kv, 2, axis=-1)
            k_shared = k_flat.reshape(B, S, SW_KV_HEADS, SW_HEAD_DIM)
            v_shared = v_flat.reshape(B, S, SW_KV_HEADS, SW_HEAD_DIM)
    return h


def setup_inputs(seed=0):
    out = dict(first_inputs(seed))
    for name, value in second_inputs(seed + 1).items():
        if name != "x":
            out[name + "_2"] = value
    return out


def reference(
    x, w_in, q_norm_g, w_q_up, kv_norm_g, w_uk, w_uv, w_o, ln1_g, ln1_b, router_w, router_bias,
    w_gate, w_up, w_down, ln2_g, ln2_b, hgrn_w_in_2, hgrn_lb_logits_2, hgrn_gnorm_w_2,
    hgrn_w_out_2, swa_w_q_2, swa_sinks_2, swa_w_out_2, shared_w_kv_2, rel_bias_2, ffn_w_in_2,
    ffn_conv_w_2, ffn_conv_b_2, ffn_w_out_2, ln_mix_g_2, ln_mix_b_2, ln_ffn_g_2, ln_ffn_b_2,
):
    x = first_block(
        x, w_in, q_norm_g, w_q_up, kv_norm_g, w_uk, w_uv, w_o, ln1_g, ln1_b, router_w,
        router_bias, w_gate, w_up, w_down, ln2_g, ln2_b,
    )
    return second_block(
        x, hgrn_w_in_2, hgrn_lb_logits_2, hgrn_gnorm_w_2, hgrn_w_out_2, swa_w_q_2, swa_sinks_2,
        swa_w_out_2, shared_w_kv_2, rel_bias_2, ffn_w_in_2, ffn_conv_w_2, ffn_conv_b_2,
        ffn_w_out_2, ln_mix_g_2, ln_mix_b_2, ln_ffn_g_2, ln_ffn_b_2,
    )


_drawn_inputs = setup_inputs


def setup_inputs(seed=0):
    import zlib

    import numpy as np

    out = dict(_drawn_inputs(seed))
    spreads = {}
    factors = {'q_norm_g': 8.0,
     'kv_norm_g': 8.0,
     'router_bias': 3.987,
     'hgrn_lb_logits_2': 4.801,
     'hgrn_gnorm_w_2': 30.892,
     'swa_sinks_2': 24.175,
     'rel_bias_2': 4.093,
     'ffn_conv_b_2': 8.0}
    for name, (base, spread) in spreads.items():
        noise = np.random.default_rng([zlib.crc32(name.encode()), seed]).standard_normal(out[name].shape)
        drawn = base * np.exp(spread * noise) if base else spread * noise
        out[name] = __import__('jax').numpy.asarray(drawn.astype(out[name].dtype))
    for name, factor in factors.items():
        out[name] = (out[name] * factor).astype(out[name].dtype)
    return out
```

```python
from contextlib import ExitStack

import numpy as np

import concourse.bass as bass
from concourse import mybir
from concourse.alu_op_type import AluOpType as ALU

F32 = mybir.dt.float32
I32 = mybir.dt.int32
U32 = mybir.dt.uint32
ACT = mybir.ActivationFunctionType
AX = mybir.AxisListType

P = 128
T = 256
NT = T // P
D = 1024
KD = D // P
DEPTH = 2
ALPHA = (2.0 * DEPTH) ** 0.25
LN_EPS, RMS_EPS = 1e-5, 1e-6
NEG = -1.0e30
PICKED = -3.0e38

Q_LORA, KV_LORA, ROPE, HEADS, HD, IDX_HEADS, IDX_DIM = 384, 256, 32, 8, 64, 8, 32
NOPE = 64
QK = NOPE + ROPE
C_QA = 0
C_KVA = C_QA + Q_LORA
C_KR = C_KVA + KV_LORA
C_DQ = C_KR + ROPE
C_DK = C_DQ + HEADS * HD
C_DV = C_DK + HD
C_IQ = C_DV + HD
C_IK = C_IQ + IDX_HEADS * IDX_DIM
C_IW = C_IK + IDX_DIM
IN_COLS = C_IW + IDX_HEADS
TOPK = T // 4
KEYS = [P * (t + 1) for t in range(NT)]
K0 = [0, P]
NK = sum(KEYS)
SLOPES = [2.0 ** (-8.0 * (h + 1) / HEADS) for h in range(HEADS)]

E, GROUPS, EPG, FF = 16, 4, 4, 512
CAP = 64
PAIRS = E // 2
MF = FF // P

HG_HEADS, HG_DIM = 8, 128
LEVELS = [1, 2, 4, 8, 16, 32, 64]
SWQ, SWKV, SWD = 16, 4, 64
FFN = 2816
CH = 2 * FFN // P
GC = FFN // P
NBUCKET, MAXDIST = 32, 128

NSLOT = 12
SLOT = 2048


class Use:

    def __init__(self, place, before):
        self.place, self.before, self.step, self.turns = place, before, 0, 1


class Ring:

    def __init__(self, size):
        self.size, self.count, self.at = size, [0] * size, 0
        self.open = None

    def take(self, place=None):
        if place is None:
            place = self.at % self.size
            self.at += 1
        u = Use(place, self.count[place])
        self.count[place] += 1
        if self.open is not None:
            self.open.append(u)
        return u

    def begin_loop(self):
        self.open = []
        self.start = list(self.count)

    def end_loop(self, turns):
        for u in self.open:
            u.step, u.turns = self.count[u.place] - self.start[u.place], turns
        for p in range(self.size):
            self.count[p] = self.start[p] + turns * (self.count[p] - self.start[p])
        self.open = None


def const_arrays():
    t = np.arange(T, dtype=np.float32)
    half = ROPE // 2
    inv = (10000.0 ** (-np.arange(half, dtype=np.float32) / half)).astype(np.float32)
    ang = (t[:, None] * inv[None, :]).astype(np.float32)
    rope = np.stack([np.cos(ang), np.sin(ang)], 1).astype(np.float32).reshape(NT, P, 2 * half)
    ident = np.eye(P, dtype=np.float32)
    before = np.triu(np.ones((P, P), np.float32), 1)
    q = np.arange(P)
    causal = np.zeros((P, NK), np.float32)
    for i in range(NT):
        s = np.arange(KEYS[i])
        causal[:, K0[i]:K0[i] + KEYS[i]] = np.where(s[None, :] <= (q + i * P)[:, None], 0.0, NEG)
    negdist = np.zeros((P, NK), np.float32)
    for i in range(NT):
        negdist[:, K0[i]:K0[i] + KEYS[i]] = np.arange(KEYS[i])[None, :] - (q + i * P)[:, None]
    rep = np.zeros((P, 2, P), np.float32)
    rep[:IDX_DIM, 0] = np.tile(np.eye(IDX_DIM), (1, P // IDX_DIM))
    rep[:HD, 1] = np.tile(np.eye(HD), (1, P // HD))
    rep[HD:, 1] = rep[:HD, 1]
    pos = np.tile(np.arange(CAP, dtype=np.float32), (P, 1))
    eidx = np.tile(np.arange(E, dtype=np.float32), (P, 1))
    gidx = np.tile(np.repeat(np.arange(GROUPS, dtype=np.float32), EPG), (P, 1))
    s, tt = np.arange(P)[:, None], np.arange(P)[None, :]
    levels = [(s == tt)]
    for m in LEVELS:
        levels.append((s // (2 * m) == tt // (2 * m)) & ((s // m) % 2 == 0) & ((tt // m) % 2 == 1))
    levels = np.stack(levels, 1).astype(np.int32)
    dist = q[:, None] + P - np.arange(2 * P)[None, :]
    band = np.where((dist >= 0) & (dist < P), 0.0, NEG).astype(np.float32)
    band = np.concatenate([band[:, P:], band], 1)
    d = 2 * P - 1 - np.arange(3 * P)
    exact = NBUCKET // 2
    safe = np.maximum(d, 1).astype(np.float32)
    logb = exact + (np.log(safe / np.float32(exact)) / np.float32(np.log(MAXDIST / exact)) * (NBUCKET - exact)).astype(np.int32)
    bucket = np.where(d < exact, np.maximum(d, 0), np.minimum(logb, NBUCKET - 1))
    pick = (bucket[None, :] == np.arange(NBUCKET)[:, None]).astype(np.float32)
    return {
        "c_ident": ident, "c_before": before,
        "c_rope": rope, "c_causal": causal, "c_negdist": negdist,
         "c_rep": rep, "c_pos": pos, "c_eidx": eidx, "c_gidx": gidx,
        "c_levels": levels, "c_band": band, "c_pick": pick,
    }



def plan():
    ring, banks = Ring(NSLOT), Ring(8)
    W, J, freed, order = {}, {}, {}, []

    def load(name, by):
        W[name] = ring.take()
        freed[name] = by
        order.append(name)

    def job(*name, bank=None):
        J[name] = banks.take(bank)

    job(0, "gains")
    plan_norm(job, 0, "in", False)
    for l in range(DEPTH):
        for n, by in (("f1", "dviw"), ("f2", "dviw"), ("iq", "iq"), ("a", "a"), ("b", "b"), ("c", "c"), ("d", "d"),
                      ("e", "e"), ("qup0", "q10"), ("qup1", "q11"), ("uk", "kn3"), ("uv", "v1")):
            load((l, n), (l, by))
        for n in range(4):
            load((l, f"wo{n}"), (l, "y11"))
        for n in ["ikdk", "iq", "dviw", "rep", "a"] + [f"idx{h}" for h in range(IDX_HEADS)] + ["b", "c", "ms", "d", "e",
                  "q00", "q01", "q10", "q11", "kn0", "kn1", "kn2", "kn3", "v0", "v1", "krT", "qT0", "qT1", "qT2", "qT3"]:
            job(l, n)
        plan_heads(job, l, 2 * HEADS)
        plan_norm(job, l, "y", True)
        for n in ("logit", "rank", "sgT0", "sgT1", "sgT2", "sgT3"):
            job(l, n)
        ring.begin_loop()
        banks.begin_loop()
        body = []
        quarters = [(m, i) for i in range(2) for m in "gu"]
        for q, (m, i) in enumerate(quarters):
            for e in range(2):
                load((l, f"{m}{e}{i}"), ("quarter_used", 2 * PAIRS * l + q + 1, 2) if q < 2 else (l, ("Hg", "Hu")[q - 2]))
                body.append(order.pop())
        for i in range(2):
            for e in range(2):
                load((l, f"w{e}{i}"), (l, "Y1"))
                body.append(order.pop())
        order.append((PAIRS, body))
        for n, b in (("G0", 0), ("G1", 1), ("Hg", 2), ("Hu", 3), ("A", 4), ("Y0", 5), ("Y1", 6),
                     ("M00", 7), ("M01", 4), ("M10", 7), ("M11", 4)):
            job(l, n, bank=b)
        ring.end_loop(PAIRS)
        banks.end_loop(PAIRS)
        plan_norm(job, l, "m", False)
    job(2, "lbT")
    for i in range(4):
        load((2, f"hq{i}"), (2, f"hq{i}"))
        job(2, f"hq{i}")
    for i in range(4):
        load((2, f"hf{i}"), (2, f"hf{i}"))
        job(2, f"hf{i}")
    for m in "iv":
        for h in range(2):
            for g in range(2):
                load((2, f"h{m}{h}{g}"), (2, f"h{m}1{h}"))
    for li in range(len(LEVELS) + 1):
        for s in range(2):
            for t in range(NT):
                job(2, f"L{li}{s}{t}")
        m, h, t = "iv"[li // 4], li % 4 // 2, li % 2
        job(2, f"h{m}{t}{h}")
    for s in range(2):
        job(2, f"X{s}")
    for t in range(NT):
        for s in range(2):
            job(2, f"R{t}{s}")
    for i in range(4):
        job(2, f"hoT{i}")
    for i in range(4):
        load((2, f"ho{i}"), (2, "y11"))
    plan_norm(job, 2, "y", True)
    for i in range(SWQ):
        job(2, f"rb{i}")
    plan_ffn(load, job, ring, banks, order, 2)
    load((3, "kv0"), (3, "kv0"))
    load((3, "kv1"), (3, "vv"))
    for n in ("kv0", "vv", "kR0", "kR1", "kR2", "kR3"):
        job(3, n)
    for i in range(4):
        load((3, f"sq{i}"), (3, f"sq{i}"))
        job(3, f"sq{i}")
    plan_heads(job, 3, SWQ)
    for i in range(4):
        load((3, f"so{i}"), (3, "y11"))
    plan_norm(job, 3, "y", True)
    plan_ffn(load, job, ring, banks, order, 3)
    return W, J, freed, order


def plan_ffn(load, job, ring, banks, order, l):
    job(l, "cw")
    ring.begin_loop()
    banks.begin_loop()
    body = []
    for j in range(2):
        for n in "ab":
            load((l, f"F{n}{j}"), (l, f"U{j}1"))
            body.append(order.pop())
        for c in range(2):
            job(l, f"U{j}{c}", bank=2 * j + c)
    order.append((FFN // 256 // 2, body))
    ring.end_loop(FFN // 256 // 2)
    banks.end_loop(FFN // 256 // 2)
    for n in "ab":
        load((l, f"F{n}2"), (l, "U21"))
    for c in range(2):
        job(l, f"U2{c}", bank=c)
    for i in range(GC // 2):
        load((l, f"Fw{i}"), ("down_used", (l - 2) * (GC // 2 - 1) + i + 1, 0) if i < GC // 2 - 1 else (l, "z11"))
    for n, b in (("00", 4), ("01", 5), ("10", 6), ("11", 7)):
        job(l, "z" + n, bank=b)
    if l < 3:
        plan_norm(job, l, "z", False)


def plan_heads(job, l, heads):
    for k in range(heads + 3):
        if k < heads:
            job(l, f"S{k}")
        if 0 <= k - 2 < heads:
            job(l, f"T{k - 2}")
        if 0 <= k - 3 < heads and (k - 3) % 2 == 0:
            job(l, f"O{(k - 3) // 2}")


def plan_norm(job, l, y, with_y):
    if with_y:
        for n in ("00", "01", "10", "11"):
            job(l, y + n)
    for n in ("00", "01", "10", "11"):
        job(l, y + "xT" + n)



def build(nc, io, out):
    W, J, freed, order = plan()
    with ExitStack() as ctx:
        def sb(name, shape, dt=F32):
            return ctx.enter_context(nc.sbuf_tensor(name, shape, dt))

        sems = {}

        def sem(name):
            if name not in sems:
                sems[name] = ctx.enter_context(nc.semaphore(name))
            return sems[name]

        bank_full = [sem(f"bank_full{b}") for b in range(8)]
        bank_free = [sem(f"bank_free{b}") for b in range(8)]
        slot_full = [sem(f"slot_full{s}") for s in range(NSLOT)]
        bank = [ctx.enter_context(nc.psum_tensor(f"bank{b}", [P, 512], F32)) for b in range(8)]

        slots = [sb(f"slot{s}", [P, SLOT]) for s in range(NSLOT)]
        x_tok = sb("x_tok", [P, NT, D])
        xT = sb("xT", [P, KD, T])
        res = sb("res", [P, NT, D])
        ln_gb = sb("ln_gb", [P, 2, D])
        ident = sb("ident", [P, P])
        ones = sb("ones", [P, P])
        rope_cs = sb("rope_cs", [P, NT, ROPE])
        tables = sb("tables", [P, (len(LEVELS) + 1) * P])
        causal, negdist, before = tables[:, 0:NK], tables[:, NK:2 * NK], tables[:, 2 * NK:2 * NK + P]
        levels = tables[:, :].bitcast(I32).rearrange("p (l t) -> p l t", t=P)
        rep = sb("rep", [P, 2, P])
        eps = sb("eps", [P, 2])
        gains = sb("gains", [P, 10])
        gain_rows = sb("gain_rows", [10, P])
        ln_stats = sb("ln_stats", [P, NT, 2, 6])
        ln_mv = sb("ln_mv", [P, NT, 2])
        ln_std = sb("ln_std", [P, NT])
        negmax = sb("negmax", [P, 2 * HEADS, NT])
        rowsum = sb("rowsum", [P, 2 * HEADS, NT])
        rinv = sb("rinv", [P, 2 * HEADS, NT])

        router = sb("router", [P, KD, E])
        rbias = sb("rbias", [P, E])
        pos = sb("pos", [P, CAP])
        eidx = sb("eidx", [P, E])
        gidx = sb("gidx", [P, E])
        aff = sb("aff", [P, NT, E])
        biased = sb("biased", [P, NT, E])
        chosen = sb("chosen", [P, NT, E])
        gates = sb("gates", [P, NT, E])
        rank = sb("rank", [P, NT, E])
        pairs2 = sb("pairs2", [P, NT * GROUPS, 6])
        gscore = sb("gscore", [P, NT, 8])
        best = sb("best", [P, NT, 8])
        besti = sb("besti", [P, NT, 8], U32)
        bestf = sb("bestf", [P, NT, 2])
        wsum = sb("wsum", [P, NT])
        most = sb("most", [P, 4])
        rounds = sb("rounds", [P, DEPTH], I32)

        lb_rows = sb("lb_rows", [16, P])
        lb = sb("lb", [P, 4, 8])
        gnorm = sb("gnorm", [P, P])
        hsum = sb("hsum", [P, NT * HG_HEADS])
        sinks = sb("sinks", [P, 2, SWQ])
        sinkexp = sb("sinkexp", [P, SWQ, NT])

        ARENA = 17450
        arena = sb("arena", [P, ARENA])

        def carve(spec):
            got, at = {}, 0
            for name, *shape in spec:
                n = int(np.prod(shape))
                v = arena[:, at:at + n]
                if len(shape) == 2:
                    v = v.rearrange("p (a b) -> p a b", a=shape[0])
                elif len(shape) == 3:
                    v = v.rearrange("p (a b c) -> p a b c", a=shape[0], b=shape[1])
                got[name] = v
                at += n
            assert at <= ARENA, (at, spec)
            return got

        A = carve([("ikdk", 2, T), ("ikdkT", 2, T), ("iqT", 2, T), ("dqT", 4, T), ("qaT", 3, T), ("kvaT", 2, T),
                   ("sq", 5, T), ("rstd", 2, T), ("q_tok", NT, HEADS * QK), ("rt", NT * HEADS, 2 * 16), ("krt", NT, ROPE), ("kr_tok", NT, QK),
                   ("qT", HEADS, T), ("kT", HEADS, T), ("v_tok", NT, HEADS * HD), ("dv", NT, HD), ("iw", NT, IDX_HEADS),
                   ("relu", 2, NK), ("work", NK), ("top8", NT, 8), ("msel", NK), ("bias", 2, NK),
                   ("prob", 3, NK), ("probT", 2, NK)])
        A["mixT"] = carve([("before", 5 * 2 + 0, T), ("mixT", 8, T)])["mixT"]

        B = carve([("S", NT, E * CAP), ("SG", NT, E * CAP), ("sgT", PAIRS, T), ("sgp", T), ("xe", KD, 2 * CAP),
                   ("silu", FF), ("act", FF), ("actT", MF, 2 * CAP), ("y", D)])

        C = carve([("Qt", HG_HEADS, T), ("Kt", HG_HEADS, T), ("SX", HG_HEADS, P), ("SA", HG_HEADS, NT * P), ("Pd", HG_HEADS, T), ("Sd", HG_HEADS, T),
                   ("Q", HG_HEADS, T), ("K", HG_HEADS, T), ("V", NT, D)])
        C["mixT"] = C["Qt"]
        C["O"] = C["Q"].rearrange("p h t -> p (h t)").rearrange("p (t n) -> p t n", t=NT)
        C["O2"] = C["K"].rearrange("p h t -> p (h t)").rearrange("p (t n) -> p t n", t=NT)
        F = carve([("gT", GC, T), ("conv", 4, T), ("gate", 2, T), ("cw_rows", 2, P), ("cw", 4, CH), ("cws", 2, 16), ("bias", SWQ, NK),
                   ("band", NK), ("rel", SWQ), ("pick", NK)])
        G = carve([("qT", 8, T), ("kraw", 2, T), ("kR", SWKV, T), ("v", NT, T), ("probT", 2, NK), ("prob", 3, NK)])
        G["bias"], G["mixT"] = F["bias"], carve([("skip", 64, 216), ("mixT", 8, T)])["mixT"]

        def slot(u, k, n):
            return slots[u.place][:, 0:k * n].rearrange("p (k n) -> p k n", k=k)

        def at(u, i, more=0):
            v = u.before + more
            return v if i is None or u.step == 0 else v + i * u.step

        def loaded(eng, name, i=None):
            u = W[name]
            v = 16 * (u.before + 1)
            eng.wait_ge(slot_full[u.place], v if i is None else v + i * (16 * u.step))
            return u

        def reuse(pe, name, i=None):
            u = J[name]
            if u.before > 0:
                pe.wait_ge(bank_free[u.place], at(u, i))
            return bank[u.place]

        def done(ins, name):
            ins.then_inc(bank_full[J[name].place], 1)

        def produced(eng, name, i=None):
            eng.wait_ge(bank_full[J[name].place], at(J[name], i, 1))
            return bank[J[name].place]

        def drained(ins, name):
            ins.then_inc(bank_free[J[name].place], 1)

        def evacuated(eng, name, i=None):
            eng.wait_ge(bank_free[J[name].place], at(J[name], i, 1))

        class Chain:

            def __init__(self, eng, name):
                self.eng, self.sem, self.n, self.base = eng, sem(name), 0, None

            def __call__(self, ins):
                self.n += 1
                ins.then_inc(self.sem, 1)
                self.eng.wait_ge(self.sem, self.n if self.base is None else self.base + self.n)

        out_banks = [6, 7, 2, 4]

        def over(l, name):
            return sem(f"over_{name}{l}")

        def more_rounds(eng, l):
            eng.wait_ge(sem("rounds_ready"), l + 1)
            return eng.value_load(rounds[0:1, l:l + 1], min_val=0, max_val=T // CAP - 1)

        block = ctx.enter_context(nc.Block())
        heads_before = {0: 0, 1: 2 * HEADS, 3: 4 * HEADS}

        def w_src(name, p=None):
            l, n = name
            win = io["w_in"]
            cols = {"f1": (C_DK, C_IQ), "f2": (C_IK, IN_COLS), "iq": (C_IQ, C_IK), "a": (0, 256), "b": (256, 512),
                    "c": (512, C_DQ), "d": (C_DQ, C_DQ + 256), "e": (C_DQ + 256, C_DK)}
            if l >= DEPTH:
                i = int(n[-1])
                if n[:2] in ("hq", "hf"):
                    o = (0 if n[1] == "q" else D) + 256 * i
                    return [(io["hgrn_w_in_2"][0, :, o:o + 256], KD, 256)]
                if n[:2] in ("hi", "hv"):
                    o = (2 if n[1] == "i" else 3) * D + 512 * int(n[2])
                    return [(io["hgrn_w_in_2"][0, 512 * i:512 * (i + 1), o:o + 512], 4, 512)]
                if n[:2] == "ho":
                    return [(io["hgrn_w_out_2"][0, 256 * i:256 * (i + 1), :], 2, 1024)]
                if n[:2] == "so":
                    return [(io["swa_w_out_2"][0, 256 * i:256 * (i + 1), :], 2, 1024)]
                if n[:2] == "sq":
                    return [(io["swa_w_q_2"][0, :, 256 * i:256 * (i + 1)], KD, 256)]
                if n[:2] == "kv":
                    return [(io["shared_w_kv_2"][:, 256 * i:256 * (i + 1)], KD, 256)]
                if n[:2] == "Fw":
                    i = int(n[2:])
                    return [(io["ffn_w_out_2"][l - DEPTH, 256 * i:256 * (i + 1), :], 2, 1024)]
                if n[0] == "F":
                    j = FFN // 256 - 1 if i == 2 else 2 * (0 if p is None else p) + i
                    o = FFN * (n[1] == "b") + 256 * j
                    x = slice(o, o + 256) if isinstance(o, int) else bass.ds(o, 256)
                    return [(io["ffn_w_in_2"][l - DEPTH, :, x], KD, 256)]
            if l < DEPTH:
                if n in cols:
                    a, b = cols[n]
                    return [(win[l, :, a:b], KD, b - a)]
                if n in ("qup0", "qup1"):
                    h = int(n[3]) * 384
                    return [(io["w_q_up"][l, :, h:h + 384], 3, 384)]
                if n in ("uk", "uv"):
                    return [(io["w_" + n][l], 2, 512)]
                if n.startswith("wo"):
                    i = int(n[2])
                    return [(io["w_o"][l, 256 * i:256 * (i + 1), :], 2, 1024)]
                m, e, i = n[0], int(n[1]), int(n[2])
                x = bass.ds(2 * p + e, 1) if p is not None else slice(e, e + 1)
                if m == "w":
                    src = io["w_down"][l, x, 256 * i:256 * (i + 1), :]
                    return [(src.rearrange("o r n -> (o r) n"), 2, 1024)]
                src = io["w_gate" if m == "g" else "w_up"][l, x, 512 * i:512 * (i + 1), :]
                return [(src.rearrange("o r n -> (o r) n"), 4, 512)]
            raise KeyError(name)

        skew = nc.dram_tensor("skew", [P, SWQ * NK], F32, kind="Internal").ap()

        @block.sync
        def _(sp):
            last = {}

            def stream(name, i=None):
                u = W[name]
                if i is not None and isinstance(freed[name][0], str):
                    what, n, step = freed[name]
                    sp.wait_ge(sem(what), n + (i - 1) * step)
                elif i is not None:
                    f = J[freed[name]]
                    sp.wait_ge(bank_full[f.place], f.before + 1 + (i - 1) * f.step)
                elif u.place in last and isinstance(freed[last[u.place]][0], str):
                    what, n, step = freed[last[u.place]]
                    sp.wait_ge(sem(what), n + (W[last[u.place]].turns - 1) * step)
                elif u.place in last:
                    f = J[freed[last[u.place]]]
                    sp.wait_ge(bank_full[f.place], f.before + 1 + (f.turns - 1) * f.step)
                last[u.place] = name
                for src, k, n in w_src(name, i):
                    sp.dma_start(slot(u, k, n), src.rearrange("(k p) n -> p k n", p=P)).then_inc(slot_full[u.place], 16)

            def overflow(l, body):
                n_rounds = more_rounds(sp, l)
                with sp.If(n_rounds > 0):
                    with sp.Fori(0, n_rounds) as r:
                        with sp.Fori(0, PAIRS) as p:
                            sp.wait_ge(over(l, "added"), r * PAIRS + p + 1)
                            for name in body:
                                for src, k, n in w_src(name, p):
                                    sp.dma_start(slot(W[name], k, n), src.rearrange("(k p) n -> p k n", p=P)).then_inc(over(l, "loaded"), 16)
                    sp.wait_ge(over(l, "done"), 1)

            for entry in order:
                if isinstance(entry[0], int) and isinstance(entry[1], list):
                    turns, body = entry
                    for name in body:
                        stream(name)
                    with sp.Fori(1, turns) as i:
                        for name in body:
                            stream(name, i)
                    if body[0][0] < DEPTH:
                        overflow(body[0][0], body)
                else:
                    stream(entry)
            sp.wait_ge(sem("result_ready"), 1)
            sp.dma_start(out.rearrange("o (t p) d -> p (o t) d", p=P), x_tok[:, :, :]).then_inc(sem("stored"), 16)
            sp.wait_ge(sem("stored"), 16)

        @block.gpsimd
        def _(pool):
            pool.memset(ones[:, :], 1.0).then_inc(sem("pool_set"), 1)
            pool.memset(eps[:, 0:1], LN_EPS).then_inc(sem("pool_set"), 1)
            pool.memset(eps[:, 1:2], RMS_EPS).then_inc(sem("pool_set"), 1)
            pool.memset(A["kr_tok"], 0.0).then_inc(sem("pool_set"), 1)

            def norm_rows(k, g, b):
                if k:
                    pool.wait_ge(sem("ln_done"), 2 * k)
                pool.dma_start(ln_gb[:, 0, :], g.unsqueeze(0).to_broadcast([P, D])).then_inc(sem("ln_rows"), 16)
                pool.dma_start(ln_gb[:, 1, :], b.unsqueeze(0).to_broadcast([P, D])).then_inc(sem("ln_rows"), 16)

            pool.memset(gscore[:, :, :], NEG).then_inc(sem("pool_set2"), 1)
            pool.dma_start(router[:, :, :], io["router_w"].rearrange("(k p) n -> p k n", p=P)).then_inc(sem("router_in"), 16)
            pool.dma_start(rbias[:, :], io["router_bias"].unsqueeze(0).to_broadcast([P, E])).then_inc(sem("router_in"), 16)
            pool.dma_start(pos[:, :], io["c_pos"]).then_inc(sem("router_in"), 16)
            pool.dma_start(eidx[:, :], io["c_eidx"]).then_inc(sem("router_in"), 16)
            pool.dma_start(gidx[:, :], io["c_gidx"]).then_inc(sem("router_in"), 16)
            norm_rows(0, io["ln1_g"][0], io["ln1_b"][0])
            norm_rows(1, io["ln2_g"][0], io["ln2_b"][0])
            norm_rows(2, io["ln1_g"][1], io["ln1_b"][1])
            norm_rows(3, io["ln2_g"][1], io["ln2_b"][1])
            pool.dma_start(lb_rows[:, :], io["hgrn_lb_logits_2"].rearrange("a (c p) -> (a c) p", p=P)).then_inc(sem("lb_in"), 16)
            pool.dma_start(gnorm[:, :], io["hgrn_gnorm_w_2"].to_broadcast([P, P])).then_inc(sem("gnorm_in"), 16)
            pool.dma_start(sinks[:, 0, :], io["swa_sinks_2"].to_broadcast([P, SWQ])).then_inc(sem("sinks_in"), 16)
            pool.wait_ge(sem("ln_done"), 8)
            pool.dma_start(levels, io["c_levels"]).then_inc(sem("levels_in"), 16)
            norm_rows(4, io["ln_mix_g_2"][0], io["ln_mix_b_2"][0])
            pool.memset(C["Sd"], 1.0).then_inc(sem("recur_set"), 1)
            pool.memset(C["SA"], 0.0).then_inc(sem("recur_set"), 1)
            pool.memset(C["Qt"], 0.0).then_inc(sem("recur_set"), 1)
            pool.memset(C["Kt"], 0.0).then_inc(sem("recur_set"), 1)
            chain = Chain(pool, "pool_chain")
            for li, m in enumerate(LEVELS):
                for s in range(2):
                    Pd, Sd = (C[n][:, 4 * s:4 * s + 4, :].rearrange("p h n -> p (h n)").rearrange("p (b j m) -> p b j m", j=2, m=m) for n in ("Pd", "Sd"))
                    nb = 4 * T // (2 * m)
                    pool.wait_ge(sem("scaled"), 2 * li + s + 1)
                    chain(nc.gpsimd.tensor_tensor(Sd[:, :, 0, :], Sd[:, :, 0, :], Pd[:, :, 1, m - 1:m].to_broadcast([P, nb, m]), ALU.mult))
                    nc.gpsimd.tensor_tensor(Pd[:, :, 1, :], Pd[:, :, 1, :], Pd[:, :, 0, m - 1:m].to_broadcast([P, nb, m]), ALU.mult)\
                        .then_inc(sem("decays"), 1)
            norm_rows(5, io["ln_ffn_g_2"][0], io["ln_ffn_b_2"][0])
            pool.dma_start(F["band"], io["c_band"]).then_inc(sem("band_in"), 16)
            pool.dma_start(F["rel"][0:NBUCKET, :], io["rel_bias_2"]).then_inc(sem("rel_in"), 16)
            pool.dma_start(F["pick"][0:NBUCKET, :], io["c_pick"]).then_inc(sem("rel_in"), 16)

            def conv_rows(l):
                pool.dma_start(F["cw_rows"][0:88, 0, :], io["ffn_conv_w_2"][l].rearrange("k n -> (k n)").rearrange("(r p) -> r p", p=P)[0:88, :]).then_inc(sem("cw_in"), 16)
                pool.dma_start(F["cw_rows"][0:44, 1, :], io["ffn_conv_w_2"][l].rearrange("k n -> (k n)").rearrange("(r p) -> r p", p=P)[88:132, :]).then_inc(sem("cw_in"), 16)
                pool.dma_start(F["cw_rows"][44:88, 1, :], io["ffn_conv_b_2"][l].rearrange("(r p) -> r p", p=P)).then_inc(sem("cw_in"), 16)

            conv_rows(0)
            for i in range(SWQ - 8, SWQ):
                evacuated(pool, (2, f"rb{i}"))
            pool.dma_start(skew, F["bias"].rearrange("p h n -> p (h n)")).then_inc(sem("skew_out"), 16)
            pool.wait_ge(sem("skew_out"), 16)
            for t, o in ((0, P), (1, 0)):
                src = bass.AP(skew.tensor, P - 1 + o, [[SWQ * NK - 1, P], [NK, SWQ], [1, KEYS[t]]])
                pool.dma_start(F["bias"][:, :, K0[t]:K0[t] + KEYS[t]], src).then_inc(sem("skew_in"), 16)
            pool.wait_ge(sem("skew_in"), 32)
            pool.wait_ge(sem("band_in"), 16)
            nc.gpsimd.tensor_tensor(F["bias"], F["bias"], F["band"].unsqueeze(1).to_broadcast([P, SWQ, NK]), ALU.add).then_inc(sem("bias_ready"), 1)
            norm_rows(6, io["ln_mix_g_2"][1], io["ln_mix_b_2"][1])
            conv_rows(1)
            norm_rows(7, io["ln_ffn_g_2"][1], io["ln_ffn_b_2"][1])

        @block.scalar
        def _(act):
            link = Chain(act, "act_chain")
            x3 = io["x"].rearrange("o (t p) d -> p (o t) d", p=P)
            act.dma_start(x_tok[:, :, :], x3).then_inc(sem("x_in"), 16)
            act.dma_start(ident[:, :], io["c_ident"]).then_inc(sem("ident_in"), 16)
            act.dma_start(rep[:, :, :], io["c_rep"]).then_inc(sem("rep_in"), 16)
            for l in range(DEPTH):
                act.dma_start(gain_rows[5 * l:5 * l + 3, :], io["q_norm_g"][l].rearrange("(a p) -> a p", p=P)).then_inc(sem("gains_in"), 16)
                act.dma_start(gain_rows[5 * l + 3:5 * l + 5, :], io["kv_norm_g"][l].rearrange("(a p) -> a p", p=P)).then_inc(sem("gains_in"), 16)
            act.dma_start(causal, io["c_causal"]).then_inc(sem("masks_in"), 16)
            act.dma_start(negdist, io["c_negdist"]).then_inc(sem("masks_in"), 16)
            act.dma_start(rope_cs[:, :, :], io["c_rope"].rearrange("t p n -> p t n")).then_inc(sem("masks_in"), 16)
            act.dma_start(before, io["c_before"]).then_inc(sem("masks_in"), 16)

            def copy(dst, src):
                return nc.scalar.activation(dst, src, ACT.Copy)

            def transposed(l, y):
                for t in range(NT):
                    for g in range(2):
                        b = produced(act, (l, f"{y}xT{t}{g}"))
                        drained(copy(xT[:, 4 * g:4 * g + 4, P * t:P * (t + 1)],
                                     b[:, :].rearrange("p (c n) -> p c n", c=4)), (l, f"{y}xT{t}{g}"))

            def norm_std(k):
                for t in range(NT):
                    act.wait_ge(sem("ln_moments"), 2 * k + t + 1)
                    nc.scalar.activation(ln_std[:, t:t + 1], ln_mv[:, t, 1:2], ACT.Sqrt, bias=eps[:, 0:1]).then_inc(sem("ln_root"), 1)

            def softmax_heads(l, heads, probs, probsT, outT, sink=False):
                base = heads_before[l]
                for k in range(heads + 4):
                    if k < heads:
                        act.wait_ge(sem("max_ready"), base + k + 1)
                        if sink:
                            nc.scalar.activation(sinkexp[:, k, :], negmax[:, k, :], ACT.Exp, bias=sinks[:, 0, k:k + 1])
                        for t in range(NT):
                            w = probs[:, k % 3, K0[t]:K0[t] + KEYS[t]]
                            last = nc.scalar.activation(w, w, ACT.Exp, bias=negmax[:, k, t:t + 1], accum_out=rowsum[:, k, t:t + 1])
                        last.then_inc(sem("exp_done"), 1)
                    if 0 <= k - 2 < heads:
                        b = produced(act, (l, f"T{k - 2}"))
                        drained(copy(probsT[:, k % 2, :], b[:, 0:NK]), (l, f"T{k - 2}"))
                    if k >= 4 and k % 2 == 0:
                        j = (k - 4) // 2
                        b = produced(act, (l, f"O{j}"))
                        drained(copy(outT[:, j, :], b[:, 0:T]), (l, f"O{j}"))

            def mixer(l):
                b = produced(act, (l, "ikdk"))
                copy(A["ikdk"][0:IDX_DIM, 0, :], b[0:IDX_DIM, 0:T])
                drained(copy(A["ikdk"][0:HD, 1, :], b[0:HD, T:2 * T]), (l, "ikdk"))
                b = produced(act, (l, "iq"))
                drained(copy(A["iqT"], b[:, :].rearrange("p (c n) -> p c n", c=2)), (l, "iq"))
                b = produced(act, (l, "dviw"))
                copy(A["dv"], b[:, 0:2 * HD].rearrange("p (t n) -> p t n", t=NT))
                drained(nc.scalar.activation(A["iw"], b[:, 2 * HD:2 * HD + 2 * IDX_HEADS].rearrange("p (t n) -> p t n", t=NT),
                                             ACT.Copy, scale=IDX_HEADS ** -0.5), (l, "dviw"))
                b = produced(act, (l, "rep"))
                drained(copy(A["ikdkT"], b[:, :].rearrange("p (c n) -> p c n", c=2)), (l, "rep"))

                def squares(name, parts):
                    b = produced(act, (l, name))
                    for i, (dst, sq, g) in enumerate(parts):
                        src = b[:, T * i:T * (i + 1)]
                        nc.scalar.activation(A["sq"][:, sq, :], src, ACT.Square)
                        last = nc.scalar.activation(dst, src, ACT.Copy, scale=gains[:, 5 * l + g:5 * l + g + 1])
                    return b, last

                if l == 0:
                    evacuated(act, (0, "gains"))
                _, last = squares("a", [(A["qaT"][:, 0, :], 0, 0), (A["qaT"][:, 1, :], 1, 1)])
                drained(last, (l, "a"))
                for h in range(IDX_HEADS):
                    b = produced(act, (l, f"idx{h}"))
                    if h >= 2:
                        act.wait_ge(sem("idx_added"), IDX_HEADS * l + h - 1)
                    drained(nc.scalar.activation(A["relu"][:, h % 2, :], b[:, 0:NK], ACT.Relu, scale=IDX_DIM ** -0.5), (l, f"idx{h}"))
                _, last = squares("b", [(A["qaT"][:, 2, :], 2, 2), (A["kvaT"][:, 0, :], 3, 3)])
                drained(last, (l, "b"))
                b, _ = squares("c", [(A["kvaT"][:, 1, :], 4, 4)])
                drained(copy(A["krt"], b[:, T:T + 2 * ROPE].rearrange("p (t n) -> p t n", t=NT)), (l, "c"))
                b = produced(act, (l, "ms"))
                nc.scalar.activation(A["rstd"][:, 0, :], b[:, 0:T], ACT.Sqrt, bias=eps[:, 1:2], scale=1.0 / Q_LORA)
                drained(nc.scalar.activation(A["rstd"][:, 1, :], b[:, T:2 * T], ACT.Sqrt, bias=eps[:, 1:2], scale=1.0 / KV_LORA), (l, "ms"))
                for i, n in enumerate("de"):
                    b = produced(act, (l, n))
                    drained(copy(A["dqT"][:, 2 * i:2 * i + 2, :], b[:, :].rearrange("p (c n) -> p c n", c=2)), (l, n))
                for t in range(NT):
                    for h in range(2):
                        b = produced(act, (l, f"q{t}{h}"))
                        drained(copy(A["q_tok"][:, t, 384 * h:384 * (h + 1)], b[:, 0:384]), (l, f"q{t}{h}"))
                for j in range(4):
                    b = produced(act, (l, f"kn{j}"))
                    drained(copy(A["kT"][0:NOPE, 2 * j:2 * j + 2, :], b[0:NOPE, :].rearrange("p (c n) -> p c n", c=2)), (l, f"kn{j}"))
                for t in range(NT):
                    b = produced(act, (l, f"v{t}"))
                    drained(copy(A["v_tok"][:, t, :], b[:, :]), (l, f"v{t}"))
                for j in range(4):
                    b = produced(act, (l, f"qT{j}"))
                    drained(copy(A["qT"][0:QK, 2 * j:2 * j + 2, :], b[0:QK, :].rearrange("p (c n) -> p c n", c=2)), (l, f"qT{j}"))
                softmax_heads(l, 2 * HEADS, A["prob"], A["probT"], A["mixT"])

            def experts(l):
                b = produced(act, (l, "logit"))
                drained(nc.scalar.activation(aff[:, :, :], b[:, 0:NT * E].rearrange("p (t e) -> p t e", t=NT), ACT.Sigmoid), (l, "logit"))
                for q in range(4):
                    b = produced(act, (l, f"sgT{q}"))
                    drained(copy(B["sgT"][:, 2 * q:2 * q + 2, :], b[:, :].rearrange("p (c n) -> p c n", c=2)), (l, f"sgT{q}"))

                def tokens(i):
                    for g in range(2):
                        b = produced(act, (l, f"G{g}"), i)
                        drained(copy(B["xe"][:, 4 * g:4 * g + 4, :], b[:, :].rearrange("p (c n) -> p c n", c=4)), (l, f"G{g}"))

                def pair(i, last=False):
                    b = produced(act, (l, "Hg"), i)
                    drained(nc.scalar.activation(B["silu"], b[:, :], ACT.Silu), (l, "Hg"))
                    if not last:
                        tokens(i + 1)
                    b = produced(act, (l, "A"), i)
                    drained(copy(B["actT"], b[:, :].rearrange("p (c n) -> p c n", c=MF)), (l, "A"))
                    for g in range(2):
                        b = produced(act, (l, f"Y{g}"), i)
                        drained(copy(B["y"][:, 512 * g:512 * (g + 1)], b[:, :]), (l, f"Y{g}"))

                tokens(0)
                with act.Fori(0, PAIRS - 1) as i:
                    pair(i)
                pair(PAIRS - 1, last=True)

            def overflow(l):
                n_rounds = more_rounds(act, l)
                with act.If(n_rounds > 0):
                    with act.Fori(0, n_rounds) as r:
                        with act.Fori(0, PAIRS) as p:
                            n = r * PAIRS + p
                            act.wait_ge(over(l, "pe"), 5 * n + 1)
                            for g in range(2):
                                copy(B["xe"][:, 4 * g:4 * g + 4, :], bank[g][:, :].rearrange("p (c n) -> p c n", c=4))
                            copy(B["sgp"], bank[6][:, 0:T]).then_inc(over(l, "act"), 1)
                            act.wait_ge(over(l, "pe"), 5 * n + 2)
                            nc.scalar.activation(B["silu"], bank[2][:, :], ACT.Silu).then_inc(over(l, "act"), 1)
                            act.wait_ge(over(l, "pe"), 5 * n + 3)
                            copy(B["actT"], bank[4][:, :].rearrange("p (c n) -> p c n", c=MF)).then_inc(over(l, "act"), 1)
                            act.wait_ge(over(l, "pe"), 5 * n + 4)
                            for g in range(2):
                                last = copy(B["y"][:, 512 * g:512 * (g + 1)], bank[5 + g][:, :])
                            last.then_inc(over(l, "act"), 1)

            act.wait_ge(sem("pool_set"), 4)
            transposed(0, "in")
            for l in range(DEPTH):
                mixer(l)
                norm_std(2 * l)
                transposed(l, "y")
                experts(l)
                overflow(l)
                norm_std(2 * l + 1)
                transposed(l, "m")

            def recurrent():
                evacuated(act, (2, "lbT"))
                act.wait_ge(sem("lb_shifted"), 1)
                nc.scalar.activation(lb[:, 0:2, :], lb[:, 0:2, :], ACT.Exp).then_inc(sem("lb_exp"), 1)
                for i in range(4):
                    b = produced(act, (2, f"hq{i}"))
                    drained(nc.scalar.activation(C["Q"][:, 2 * i:2 * i + 2, :], b[:, :].rearrange("p (c n) -> p c n", c=2), ACT.Silu), (2, f"hq{i}"))
                for i in range(4):
                    b = produced(act, (2, f"hf{i}"))
                    drained(nc.scalar.activation(C["Pd"][:, 2 * i:2 * i + 2, :], b[:, :].rearrange("p (c n) -> p c n", c=2), ACT.Sigmoid), (2, f"hf{i}"))
                for li in range(len(LEVELS) + 1):
                    m, h, t = "iv"[li // 4], li % 4 // 2, li % 2
                    b = produced(act, (2, f"h{m}{t}{h}"))
                    c = slice(512 * h, 512 * (h + 1))
                    if m == "i":
                        drained(copy(C["V"][:, t, c], b[:, :]), (2, f"h{m}{t}{h}"))
                    else:
                        drained(nc.scalar.activation(res[:, t, c], b[:, :], ACT.Silu), (2, f"h{m}{t}{h}"))
                for s in range(2):
                    b = produced(act, (2, f"X{s}"))
                    drained(copy(C["SX"][:, 4 * s:4 * s + 4, :], b[:, :].rearrange("p (c n) -> p c n", c=4)), (2, f"X{s}"))
                for t in range(NT):
                    for s in range(2):
                        b = produced(act, (2, f"R{t}{s}"))
                        drained(copy(C["O"][:, t, 512 * s:512 * (s + 1)], b[:, :]), (2, f"R{t}{s}"))
                act.wait_ge(sem("head_sums"), 1)
                nc.scalar.activation(hsum[:, :], hsum[:, :], ACT.Sqrt, bias=eps[:, 1:2], scale=1.0 / HG_DIM).then_inc(sem("head_roots"), 1)
                for i in range(4):
                    b = produced(act, (2, f"hoT{i}"))
                    drained(copy(C["mixT"][:, 4 * (i % 2):4 * (i % 2) + 4, P * (i // 2):P * (i // 2 + 1)], b[:, :].rearrange("p (c n) -> p c n", c=4)), (2, f"hoT{i}"))

            def feed_forward(l):
                b = produced(act, (l, "cw"))
                drained(copy(F["cw"], b[:, 0:4 * CH].rearrange("p (k n) -> p k n", k=4)), (l, "cw"))

                def step(j, i):
                    base = (l - 2) * (FFN // 256) + (10 if i is None else j)
                    more = 0 if i is None else 2 * i
                    for c in range(2):
                        b = produced(act, (l, f"U{j}{c}"), i)
                        if c == 0:
                            act.wait_ge(sem("taps"), base + 1 + more)
                        for ab in range(2):
                            w = F["cws"][:, j % 2, :].rearrange("p (k a c) -> p k a c", k=4, a=2)
                            last = nc.scalar.activation(F["conv"][:, 2 * c + ab, :], b[:, T * ab:T * (ab + 1)], ACT.Identity,
                                                        bias=w[:, 3, ab, c:c + 1], scale=w[:, 2, ab, c:c + 1])
                        last.then_inc(sem("conv_begun"), 1)
                    for c in range(2):
                        act.wait_ge(sem("conv_done"), 2 * base + c + 1 + 2 * more)
                        nc.scalar.activation(F["gate"][:, c, :], F["conv"][:, 2 * c, :], ACT.Silu).then_inc(sem("gate_done"), 1)

                with act.Fori(0, FFN // 256 // 2) as i:
                    step(0, i)
                    step(1, i)
                step(2, None)

            recurrent()
            norm_std(4)
            transposed(2, "y")
            for i in range(SWQ):
                b = produced(act, (2, f"rb{i}"))
                drained(copy(F["bias"][:, i, :], b[:, 0:NK]), (2, f"rb{i}"))
            feed_forward(2)
            norm_std(5)
            transposed(2, "z")
            b = produced(act, (3, "kv0"))
            drained(copy(G["kraw"], b[:, :].rearrange("p (c n) -> p c n", c=2)), (3, "kv0"))
            b = produced(act, (3, "vv"))
            drained(copy(G["v"], b[:, :].rearrange("p (c n) -> p c n", c=2)), (3, "vv"))
            for i in range(SWKV):
                b = produced(act, (3, f"kR{i}"))
                drained(copy(G["kR"][:, i, :], b[:, 0:T]), (3, f"kR{i}"))
            for i in range(4):
                b = produced(act, (3, f"sq{i}"))
                drained(copy(G["qT"][:, 2 * i:2 * i + 2, :], b[:, :].rearrange("p (c n) -> p c n", c=2)), (3, f"sq{i}"))
            softmax_heads(3, SWQ, G["prob"], G["probT"], G["mixT"], sink=True)
            norm_std(6)
            transposed(3, "y")
            feed_forward(3)
            norm_std(7)

        @block.vector
        def _(dve):
            link = Chain(dve, "dve_chain")
            V = nc.vector
            b = produced(dve, (0, "gains"))
            drained(V.tensor_copy(gains[:, :], b[:, 0:10]), (0, "gains"))

            def norm(k, l, y, from_psum):
                for t in range(NT):
                    for h in range(2):
                        cols = slice(512 * h, 512 * (h + 1))
                        if from_psum:
                            b = produced(dve, (l, f"{y}{t}{h}"))
                            ins = V.scalar_tensor_tensor(res[:, t, cols], x_tok[:, t, cols], ALPHA, b[:, :], ALU.mult, ALU.add)
                            drained(ins, (l, f"{y}{t}{h}"))
                            evacuated(dve, (l, f"{y}{t}{h}"))
                        last = V.bn_stats(ln_stats[:, t, h, :], res[:, t, cols])
                    link(last)
                    V.bn_aggr(ln_mv[:, t, :], ln_stats[:, t, :, :].rearrange("p a b -> p (a b)")).then_inc(sem("ln_moments"), 1)
                if k == 0:
                    dve.wait_ge(sem("ln_rows"), 32)
                else:
                    dve.wait_ge(sem("ln_rows"), 32 * (k + 1))
                for t in range(NT):
                    dve.wait_ge(sem("ln_root"), 2 * k + t + 1)
                    link(V.reciprocal(ln_std[:, t:t + 1], ln_std[:, t:t + 1]))
                    link(V.tensor_scalar(res[:, t, :], res[:, t, :], ln_mv[:, t, 0:1], ln_std[:, t:t + 1], ALU.subtract, ALU.mult))
                    link(V.tensor_tensor(res[:, t, :], res[:, t, :], ln_gb[:, 0, :], ALU.mult))
                    V.tensor_tensor(x_tok[:, t, :], res[:, t, :], ln_gb[:, 1, :], ALU.add).then_inc(sem("ln_done"), 1)

            def softmax_head(l, k, probs, scale, bias, sink=False):
                base = heads_before[l]
                b = produced(dve, (l, f"S{k}"))
                if k >= 3:
                    produced(dve, (l, f"T{k - 3}"))
                ins = V.scalar_tensor_tensor(probs[:, k % 3, :], b[:, 0:NK], scale, bias, ALU.mult, ALU.add)
                drained(ins, (l, f"S{k}"))
                evacuated(dve, (l, f"S{k}"))
                for t in range(NT):
                    last = V.tensor_reduce(negmax[:, k, t:t + 1], probs[:, k % 3, K0[t]:K0[t] + KEYS[t]], AX.X, ALU.max, negate=True)
                if sink:
                    link(last)
                    last = V.tensor_scalar(negmax[:, k, :], negmax[:, k, :], sinks[:, 1, k:k + 1], None, ALU.min)
                last.then_inc(sem("max_ready"), 1)

            def normalise(l, k, probs, sink=False):
                dve.wait_ge(sem("exp_done"), heads_before[l] + k + 1)
                if sink:
                    link(V.tensor_tensor(rowsum[:, k, :], rowsum[:, k, :], sinkexp[:, k, :], ALU.add))
                link(V.reciprocal(rinv[:, k, :], rowsum[:, k, :]))
                for t in range(NT):
                    w = probs[:, k % 3, K0[t]:K0[t] + KEYS[t]]
                    last = V.tensor_scalar(w, w, rinv[:, k, t:t + 1], None, ALU.mult)
                last.then_inc(sem("probs_ready"), 1)

            def mixer(l):
                work, causal_, iw = A["work"], causal, A["iw"]
                if l == 0:
                    dve.wait_ge(sem("masks_in"), 64)
                evacuated(dve, (l, "dviw"))
                for h in range(IDX_HEADS):
                    evacuated(dve, (l, f"idx{h}"))
                    for t in range(NT):
                        c = slice(K0[t], K0[t] + KEYS[t])
                        prev = causal_[:, c] if h == 0 else work[:, c]
                        last = V.scalar_tensor_tensor(work[:, c], A["relu"][:, h % 2, c], iw[:, t, h:h + 1], prev, ALU.mult, ALU.add)
                    last.then_inc(sem("idx_added"), 1)
                    dve.wait_ge(sem("idx_added"), IDX_HEADS * l + h + 1)
                evacuated(dve, (l, "ms"))
                link(V.reciprocal(A["rstd"], A["rstd"]))
                V.tensor_tensor(A["qaT"], A["qaT"], A["rstd"][:, 0:1, :].to_broadcast([P, 3, T]), ALU.mult).then_inc(sem("latents"), 1)
                V.tensor_tensor(A["kvaT"], A["kvaT"], A["rstd"][:, 1:2, :].to_broadcast([P, 2, T]), ALU.mult).then_inc(sem("latents"), 1)
                half = ROPE // 2
                cos, sin = rope_cs[:, :, 0:half], rope_cs[:, :, half:ROPE]
                kr, tmp, dst = A["krt"], A["rt"][:, 0:2, :], A["kr_tok"]
                V.tensor_tensor(dst[:, :, NOPE:NOPE + half], kr[:, :, 0:half], cos, ALU.mult)
                V.tensor_tensor(dst[:, :, NOPE + half:QK], kr[:, :, 0:half], sin, ALU.mult)
                V.tensor_tensor(tmp[:, :, 0:half], kr[:, :, half:ROPE], sin, ALU.mult)
                link(V.tensor_tensor(tmp[:, :, half:ROPE], kr[:, :, half:ROPE], cos, ALU.mult))
                V.tensor_tensor(dst[:, :, NOPE:NOPE + half], dst[:, :, NOPE:NOPE + half], tmp[:, :, 0:half], ALU.subtract)
                V.tensor_tensor(dst[:, :, NOPE + half:QK], dst[:, :, NOPE + half:QK], tmp[:, :, half:ROPE], ALU.add).then_inc(sem("kr_roped"), 1)
                dve.wait_ge(sem("kr_roped"), l + 1)
                for t in range(NT):
                    for h in range(2):
                        evacuated(dve, (l, f"q{t}{h}"))
                for t in range(NT):
                    q = A["q_tok"][:, t, :].rearrange("p (h n) -> p h n", h=HEADS)
                    x1, x2 = q[:, :, NOPE:NOPE + half], q[:, :, NOPE + half:QK]
                    rt = A["rt"][:, :, :].rearrange("p a b -> p (a b)").rearrange("p (j h n) -> p j h n", j=4, h=HEADS)
                    c = rope_cs[:, t:t + 1, 0:half].to_broadcast([P, HEADS, half])
                    s = rope_cs[:, t:t + 1, half:ROPE].to_broadcast([P, HEADS, half])
                    V.tensor_tensor(rt[:, 0], x1, c, ALU.mult)
                    V.tensor_tensor(rt[:, 1], x2, s, ALU.mult)
                    V.tensor_tensor(rt[:, 2], x1, s, ALU.mult)
                    link(V.tensor_tensor(rt[:, 3], x2, c, ALU.mult))
                    V.tensor_tensor(x1, rt[:, 0], rt[:, 1], ALU.subtract)
                    last = V.tensor_tensor(x2, rt[:, 2], rt[:, 3], ALU.add)
                    if t == 0:
                        link(last)
                    else:
                        last.then_inc(sem("q_roped"), 1)
                        dve.wait_ge(sem("q_roped"), l + 1)
                b = produced(dve, (l, "krT"))
                drained(V.tensor_copy(A["kT"][NOPE:QK, :, :], b[NOPE:QK, 0:T].unsqueeze(1).to_broadcast([ROPE, HEADS, T])), (l, "krT"))
                pr = A["prob"]
                for k in range(2 * HEADS + 1):
                    if k < HEADS:
                        softmax_head(l, k, pr, QK ** -0.5, causal_)
                    elif k < 2 * HEADS:
                        j = k - HEADS
                        link(V.scalar_tensor_tensor(A["bias"][:, k % 2, :], negdist, SLOPES[j], A["msel"], ALU.mult, ALU.add))
                        softmax_head(l, k, pr, HD ** -0.5, A["bias"][:, k % 2, :])
                    if k >= 1:
                        normalise(l, k - 1, pr)
                    if k < HEADS:
                        for t in range(NT):
                            last = V.max(A["top8"][:, t, :], work[:, K0[t]:K0[t] + KEYS[t]])
                        link(last)
                        for t in range(NT):
                            c = slice(K0[t], K0[t] + KEYS[t])
                            last = V.match_replace(work[:, c], A["top8"][:, t, :], work[:, c], PICKED)
                        link(last)
                    if k == HEADS - 1:
                        link(V.tensor_scalar(work, work, PICKED / 2, 1.0, ALU.is_lt, ALU.subtract))
                        link(V.scalar_tensor_tensor(A["msel"], work, -NEG, causal_, ALU.mult, ALU.add))

            def route(l):
                if l == 0:
                    dve.wait_ge(sem("router_in"), 80)
                    dve.wait_ge(sem("pool_set2"), 1)
                evacuated(dve, (l, "logit"))
                link(V.tensor_tensor(biased[:, :, :], aff[:, :, :], rbias[:, :].unsqueeze(1).to_broadcast([P, NT, E]), ALU.add))
                v = biased[:, :, :].rearrange("p t (g k) -> p (t g) k", g=GROUPS)
                V.tensor_tensor(pairs2[:, :, 0:3], v[:, :, 0:3], v[:, :, 1:4], ALU.add)
                V.tensor_tensor(pairs2[:, :, 3:5], v[:, :, 0:2], v[:, :, 2:4], ALU.add)
                link(V.tensor_tensor(pairs2[:, :, 5:6], v[:, :, 0:1], v[:, :, 3:4], ALU.add))
                link(V.tensor_reduce(gscore[:, :, 0:GROUPS], pairs2[:, :, :].rearrange("p (t g) k -> p t g k", t=NT), AX.X, ALU.max))

                def argmax(src, n):
                    for t in range(NT):
                        last = V.max(best[:, t, :], src[:, t, :])
                    link(last)
                    for t in range(NT):
                        last = V.max_index(besti[:, t, :], best[:, t, :], src[:, t, :])
                    link(last)
                    link(V.tensor_copy(bestf[:, :, 0:n], besti[:, :, 0:n]))

                argmax(gscore, 1)
                for t in range(NT):
                    last = V.tensor_scalar(chosen[:, t, :], gidx[:, :], bestf[:, t, 0:1], 1.0, ALU.is_equal, ALU.subtract)
                link(last)
                link(V.scalar_tensor_tensor(biased[:, :, :], chosen[:, :, :], -NEG, biased[:, :, :], ALU.mult, ALU.add))
                argmax(biased, 2)
                for t in range(NT):
                    last = V.tensor_scalar(gates[:, t, :], eidx[:, :], bestf[:, t, 0:1], None, ALU.is_equal)
                link(last)
                for t in range(NT):
                    last = V.scalar_tensor_tensor(chosen[:, t, :], eidx[:, :], bestf[:, t, 1:2], gates[:, t, :], ALU.is_equal, ALU.add)
                last.then_inc(sem("chosen_ready"), 1)
                dve.wait_ge(sem("chosen_ready"), l + 1)
                link(V.tensor_tensor(gates[:, :, :], aff[:, :, :], chosen[:, :, :], ALU.mult))
                link(V.tensor_reduce(wsum[:, :], gates[:, :, :], AX.X, ALU.add))
                link(V.reciprocal(wsum[:, :], wsum[:, :]))
                link(V.tensor_tensor(gates[:, :, :], gates[:, :, :], wsum[:, :].unsqueeze(2).to_broadcast([P, NT, E]), ALU.mult))
                b = produced(dve, (l, "rank"))
                link(V.scalar_tensor_tensor(rank[:, :, :], b[:, 0:NT * E].rearrange("p (t e) -> p t e", t=NT), 1.0, chosen[:, :, :], ALU.add, ALU.mult))
                drained(V.tensor_reduce(most[:, 0:1], b[:, NT * E:NT * E + E], AX.X, ALU.max), (l, "rank"))
                link(V.tensor_scalar(rank[:, :, :], rank[:, :, :], 1.0, None, ALU.subtract))
                evacuated(dve, (l, "rank"))
                link(V.tensor_scalar(most[:, 1:2], most[:, 0:1], float(CAP), None, ALU.is_gt))
                for r in range(2, T // CAP):
                    link(V.scalar_tensor_tensor(most[:, 1:2], most[:, 0:1], float(r * CAP), most[:, 1:2], ALU.is_gt, ALU.add))
                V.tensor_copy(rounds[:, l:l + 1], most[:, 1:2]).then_inc(sem("rounds_ready"), 1)
                slot_of = B["S"].rearrange("p t (e s) -> p (t e) s", e=E)
                V.tensor_tensor(slot_of, rank[:, :, :].rearrange("p t e -> p (t e)").unsqueeze(2).to_broadcast([P, NT * E, CAP]),
                                pos[:, :].unsqueeze(1).to_broadcast([P, NT * E, CAP]), ALU.is_equal).then_inc(sem("slots_ready"), 1)
                dve.wait_ge(sem("slots_ready"), 2 * l + 1)
                V.tensor_tensor(B["SG"].rearrange("p t (e s) -> p (t e) s", e=E), slot_of,
                                gates[:, :, :].rearrange("p t e -> p (t e)").unsqueeze(2).to_broadcast([P, NT * E, CAP]), ALU.mult)\
                    .then_inc(sem("slots_ready"), 1)
                link(V.tensor_scalar(res[:, :, :], x_tok[:, :, :], ALPHA, None, ALU.mult))

            def experts(l):
                evacuated(dve, (l, "sgT3"))
                with dve.Fori(0, PAIRS) as i:
                    u = J[(l, "M11")]
                    dve.wait_ge(bank_full[u.place], u.before + 1 - u.step + i * u.step)
                    V.tensor_scalar(B["sgp"], B["sgT"][:, bass.ds(i, 1), :].rearrange("p o n -> p (o n)"), 1.0, None, ALU.mult)\
                        .then_inc(sem("gates_copied"), 1)
                    b = produced(dve, (l, "Hu"), i)
                    evacuated(dve, (l, "Hg"), i)
                    drained(V.tensor_tensor(B["act"], B["silu"], b[:, :], ALU.mult), (l, "Hu"))
                    for t in range(NT):
                        for h in range(2):
                            b = produced(dve, (l, f"M{t}{h}"), i)
                            r = res[:, t, 512 * h:512 * (h + 1)]
                            drained(V.tensor_tensor(r, r, b[:, :], ALU.add), (l, f"M{t}{h}"))
                for n in ("M10", "M11"):
                    evacuated(dve, (l, n), PAIRS - 1)

            def overflow(l):
                n_rounds = more_rounds(dve, l)
                with dve.If(n_rounds > 0):
                    V.tensor_copy(most[:, 2:3], most[:, 0:1]).then_inc(over(l, "added"), 1)
                    with dve.Fori(0, n_rounds) as r:
                        V.tensor_scalar(rank[:, :, :], rank[:, :, :], float(CAP), None, ALU.subtract).then_inc(over(l, "ranked"), 1)
                        with dve.Fori(0, PAIRS) as p:
                            n = r * PAIRS + p
                            dve.wait_ge(over(l, "ranked"), r + 1)
                            two = bass.ds(2 * p, 2)
                            for t in range(NT):
                                last = V.tensor_tensor(B["S"][:, t, 0:P].rearrange("p (e s) -> p e s", e=2),
                                                       rank[:, t, two].unsqueeze(2).to_broadcast([P, 2, CAP]),
                                                       pos[:, :].unsqueeze(1).to_broadcast([P, 2, CAP]), ALU.is_equal)
                            last.then_inc(over(l, "slots"), 1)
                            dve.wait_ge(over(l, "slots"), 2 * n + 1)
                            for t in range(NT):
                                last = V.tensor_tensor(B["SG"][:, t, 0:P].rearrange("p (e s) -> p e s", e=2),
                                                       B["S"][:, t, 0:P].rearrange("p (e s) -> p e s", e=2),
                                                       gates[:, t, two].unsqueeze(2).to_broadcast([P, 2, CAP]), ALU.mult)
                            last.then_inc(over(l, "slots"), 1)
                            dve.wait_ge(over(l, "act"), 4 * n + 2)
                            V.tensor_tensor(B["act"], B["silu"], bank[3][:, :], ALU.mult).then_inc(over(l, "hidden"), 1)
                            dve.wait_ge(over(l, "pe"), 5 * n + 5)
                            for t in range(NT):
                                for h in range(2):
                                    y = res[:, t, 512 * h:512 * (h + 1)]
                                    last = V.tensor_tensor(y, y, bank[out_banks[2 * t + h]][:, :], ALU.add)
                            last.then_inc(over(l, "added"), 1)
                            dve.wait_ge(over(l, "added"), n + 2)
                    V.tensor_copy(most[:, 3:4], most[:, 0:1]).then_inc(over(l, "done"), 1)

            for l in range(DEPTH):
                mixer(l)
                norm(2 * l, l, "y", True)
                route(l)
                experts(l)
                overflow(l)
                norm(2 * l + 1, l, "m", False)
            def recurrent():
                b = produced(dve, (2, "lbT"))
                drained(V.tensor_copy(lb[:, 0:2, :], b[:, 0:16].rearrange("p (a c) -> p a c", a=2)), (2, "lbT"))
                evacuated(dve, (2, "lbT"))
                link(V.tensor_tensor(lb[:, 2, :], lb[:, 0, :], lb[:, 1, :], ALU.max))
                V.tensor_tensor(lb[:, 0:2, :], lb[:, 0:2, :], lb[:, 2:3, :].to_broadcast([P, 2, 8]), ALU.subtract).then_inc(sem("lb_shifted"), 1)
                dve.wait_ge(sem("lb_exp"), 1)
                link(V.tensor_tensor(lb[:, 3, :], lb[:, 0, :], lb[:, 1, :], ALU.add))
                link(V.reciprocal(lb[:, 3, :], lb[:, 3, :]))
                link(V.tensor_tensor(lb[:, 2, :], lb[:, 0, :], lb[:, 3, :], ALU.mult))
                link(V.tensor_scalar(lb[:, 3, :], lb[:, 2, :], -1.0, 1.0, ALU.mult, ALU.add))
                for h in range(HG_HEADS):
                    if h % 2 == 0:
                        evacuated(dve, (2, f"hf{h // 2}"))
                    last = V.tensor_scalar(C["Pd"][:, h, :], C["Pd"][:, h, :], lb[:, 3, h:h + 1], lb[:, 2, h:h + 1], ALU.mult, ALU.add)
                link(last)
                V.tensor_scalar(C["K"], C["Pd"], -1.0, 1.0, ALU.mult, ALU.add).then_inc(sem("keys_ready"), 1)
                dve.wait_ge(sem("keys_ready"), 1)
                dve.wait_ge(sem("recur_set"), 4)
                dve.wait_ge(sem("levels_in"), 16)
                for i in range(4):
                    evacuated(dve, (2, f"hq{i}"))

                def merge(li):
                    for s in range(2):
                        for t in range(NT):
                            b = produced(dve, (2, f"L{li}{s}{t}"))
                            if li:
                                evacuated(dve, (2, f"L{li - 1}{s}{t}"))
                            drained(V.copy_predicated(C["SA"][:, 4 * s:4 * s + 4, P * t:P * (t + 1)],
                                                      levels[:, li:li + 1, :].to_broadcast([P, 4, P]),
                                                      b[:, :].rearrange("p (c n) -> p c n", c=4)), (2, f"L{li}{s}{t}"))

                for li, m in enumerate(LEVELS + [P]):
                    for s in range(2):
                        Pd, Sd, Q, K, Qt, Kt = (C[n][:, 4 * s:4 * s + 4, :].rearrange("p h n -> p (h n)").rearrange("p (b j m) -> p b j m", j=2, m=m)
                                                for n in ("Pd", "Sd", "Q", "K", "Qt", "Kt"))
                        if li:
                            dve.wait_ge(sem("decays"), 2 * (li - 1) + s + 1)
                            produced(dve, (2, f"L{li}{s}1"))
                        V.tensor_tensor(Kt[:, :, 0, :], K[:, :, 0, :], Sd[:, :, 0, :], ALU.mult)
                        V.tensor_tensor(Qt[:, :, 1, :], Q[:, :, 1, :], Pd[:, :, 1, :], ALU.mult).then_inc(sem("scaled"), 1)
                    merge(li)
                for t in range(NT):
                    for s in range(2):
                        evacuated(dve, (2, f"R{t}{s}"))
                link(V.tensor_tensor(C["O2"], C["O"], C["O"], ALU.mult))
                V.tensor_reduce(hsum[:, :], C["O2"].rearrange("p t (h n) -> p (t h) n", n=HG_DIM), AX.X, ALU.add).then_inc(sem("head_sums"), 1)
                O16 = C["O"].rearrange("p t (h n) -> p (t h) n", n=HG_DIM)
                G16 = res[:, :, :].rearrange("p t (h n) -> p (t h) n", n=HG_DIM)
                evacuated(dve, (2, "hv11"))
                dve.wait_ge(sem("gnorm_in"), 16)
                link(V.tensor_tensor(G16, G16, gnorm[:, :].unsqueeze(1).to_broadcast([P, 16, P]), ALU.mult))
                dve.wait_ge(sem("head_roots"), 1)
                link(V.reciprocal(hsum[:, :], hsum[:, :]))
                link(V.tensor_tensor(O16, O16, hsum[:, :].unsqueeze(2).to_broadcast([P, 16, P]), ALU.mult))
                for t in range(NT):
                    V.tensor_tensor(C["O"][:, t, :], C["O"][:, t, :], res[:, t, :], ALU.mult).then_inc(sem("recur_out"), 1)
                dve.wait_ge(sem("recur_out"), 2)

            def feed_forward(l):
                evacuated(dve, (l, "cw"))
                cw = F["cw"].rearrange("p k (a n) -> p k a n", a=2)

                def step(j, i):
                    base = (l - 2) * (FFN // 256) + (10 if i is None else j)
                    more = 0 if i is None else 2 * i
                    w = F["cws"][:, j % 2, :].rearrange("p (k a c) -> p k a c", k=4, a=2)
                    if i is None:
                        src = lambda a: cw[:, :, a, GC - 2:GC]
                    else:
                        src = lambda a: cw[:, :, a, bass.ds(4 * i + 2 * j, 2)]
                    V.tensor_scalar(w[:, :, 0, :], src(0), 1.0, None, ALU.mult)
                    V.tensor_scalar(w[:, :, 1, :], src(1), 1.0, None, ALU.mult).then_inc(sem("taps"), 1)
                    dve.wait_ge(sem("taps"), base + 1 + more)
                    for c in range(2):
                        b = produced(dve, (l, f"U{j}{c}"), i)
                        dve.wait_ge(sem("conv_begun"), 2 * base + c + 1 + 2 * more)
                        for ab in range(2):
                            y, x = F["conv"][:, 2 * c + ab, :], b[:, T * ab:T * (ab + 1)]
                            last = V.scalar_tensor_tensor(y[:, 1:T], x[:, 0:T - 1], w[:, 1, ab, c:c + 1], y[:, 1:T], ALU.mult, ALU.add)
                        last.then_inc(sem("tap_done"), 1)
                        dve.wait_ge(sem("tap_done"), 2 * base + c + 1 + 2 * more)
                        for ab in range(2):
                            y, x = F["conv"][:, 2 * c + ab, :], b[:, T * ab:T * (ab + 1)]
                            last = V.scalar_tensor_tensor(y[:, 2:T], x[:, 0:T - 2], w[:, 0, ab, c:c + 1], y[:, 2:T], ALU.mult, ALU.add)
                            if ab == 0:
                                last.then_inc(sem("conv_done"), 1)
                        drained(last, (l, f"U{j}{c}"))
                    for c in range(2):
                        dve.wait_ge(sem("gate_done"), 2 * base + c + 1 + 2 * more)
                        if c == 0:
                            evacuated(dve, (l, f"U{j}0"), i)
                            evacuated(dve, (l, f"U{j}1"), i)
                        if i is None:
                            g = F["gT"][:, GC - 2 + c, :]
                        else:
                            g = F["gT"][:, bass.ds(4 * i + (2 * j + c), 1), :].rearrange("p o n -> p (o n)")
                        V.tensor_tensor(g, F["gate"][:, c, :], F["conv"][:, 2 * c + 1, :], ALU.mult).then_inc(sem("gated"), 1)

                with dve.Fori(0, FFN // 256 // 2) as i:
                    step(0, i)
                    step(1, i)
                step(2, None)

            recurrent()
            norm(4, 2, "y", True)
            feed_forward(2)
            norm(5, 2, "z", True)
            dve.wait_ge(sem("sinks_in"), 16)
            link(V.tensor_scalar(sinks[:, 1, :], sinks[:, 0, :], -1.0, None, ALU.mult))
            dve.wait_ge(sem("bias_ready"), 1)
            for k in range(SWQ + 1):
                if k < SWQ:
                    softmax_head(3, k, G["prob"], SWD ** -0.5, G["bias"][:, k, :], sink=True)
                if k >= 1:
                    normalise(3, k - 1, G["prob"], sink=True)
            norm(6, 3, "y", True)
            feed_forward(3)
            norm(7, 3, "z", True)
            dve.wait_ge(sem("ln_done"), 16)
            V.tensor_copy(ln_std[:, :], ln_std[:, :]).then_inc(sem("result_ready"), 1)

        @block.tensor
        def _(pe):
            mm = nc.tensor.matmul

            def product(dst, lhs, rhs, n):
                for c in range(n):
                    last = mm(dst, lhs(c), rhs(c), start=(c == 0), stop=(c == n - 1))
                return last

            def tok(t):
                return slice(P * t, P * (t + 1))

            def transpose_x(l, y, ready):
                for t in range(NT):
                    ready(t)
                    for g in range(2):
                        b = reuse(pe, (l, f"{y}xT{t}{g}"))
                        for c in range(4):
                            last = nc.tensor.transpose(b[:, P * c:P * (c + 1)], x_tok[:, t, P * (4 * g + c):P * (4 * g + c + 1)], ident[:, :])
                        done(last, (l, f"{y}xT{t}{g}"))

            def heads(l, n, score, value, probs, probsT):
                base = heads_before[l]
                for k in range(n + 3):
                    if k < n:
                        b = reuse(pe, (l, f"S{k}"))
                        for t in range(NT):
                            last = score(k, t, b[:, K0[t]:K0[t] + KEYS[t]])
                        done(last, (l, f"S{k}"))
                    if 0 <= k - 2 < n:
                        j = k - 2
                        b = reuse(pe, (l, f"T{j}"))
                        pe.wait_ge(sem("probs_ready"), base + j + 1)
                        for c in range(3):
                            last = nc.tensor.transpose(b[:, tok(c)], probs[:, j % 3, tok(c)], ident[:, :])
                        done(last, (l, f"T{j}"))
                    if 0 <= k - 3 < n:
                        j = k - 3
                        o = f"O{j // 2}"
                        if j % 2 == 0:
                            reuse(pe, (l, o))
                        b = bank[J[(l, o)].place]
                        rows = slice(64 * (j % 2), 64 * (j % 2) + 64)
                        evacuated(pe, (l, f"T{j}"))
                        mm(b[rows, 0:P], value(j, 0), probsT[:, j % 2, 0:P], start=True, stop=True)
                        mm(b[rows, P:T], value(j, 0), probsT[:, j % 2, P:2 * P], start=True, stop=False)
                        last = mm(b[rows, P:T], value(j, 1), probsT[:, j % 2, 2 * P:3 * P], start=False, stop=True)
                        if j % 2:
                            done(last, (l, o))

            def project_out(l, y, mixT, names):
                us = [loaded(pe, (l, n)) for n in names]
                for t in range(NT):
                    for h in range(2):
                        b = reuse(pe, (l, f"{y}{t}{h}"))
                        done(product(b[:, :], lambda c: mixT[:, c, tok(t)],
                                     lambda c: slot(us[c // 2], 2, 1024)[:, c % 2, 512 * h:512 * (h + 1)], KD), (l, f"{y}{t}{h}"))

            def mixer(l):
                f1, f2 = loaded(pe, (l, "f1")), loaded(pe, (l, "f2"))
                s1, s2 = slot(f1, KD, C_IQ - C_DK), slot(f2, KD, IN_COLS - C_IK)
                b = reuse(pe, (l, "ikdk"))
                product(b[0:IDX_DIM, 0:T], lambda c: s2[:, c, 0:IDX_DIM], lambda c: xT[:, c, :], KD)
                done(product(b[0:HD, T:2 * T], lambda c: s1[:, c, 0:HD], lambda c: xT[:, c, :], KD), (l, "ikdk"))

                def pair(name):
                    u = loaded(pe, (l, name))
                    b = reuse(pe, (l, name))
                    s = slot(u, KD, 256)
                    for i in range(2):
                        last = product(b[:, T * i:T * (i + 1)], lambda c: s[:, c, P * i:P * (i + 1)], lambda c: xT[:, c, :], KD)
                    done(last, (l, name))

                pair("iq")
                b = reuse(pe, (l, "dviw"))
                for t in range(NT):
                    product(b[:, HD * t:HD * (t + 1)], lambda c: xT[:, c, tok(t)], lambda c: s1[:, c, HD:2 * HD], KD)
                for t in range(NT):
                    o = 2 * HD + IDX_HEADS * t
                    last = product(b[:, o:o + IDX_HEADS], lambda c: xT[:, c, tok(t)], lambda c: s2[:, c, IDX_DIM:IDX_DIM + IDX_HEADS], KD)
                done(last, (l, "dviw"))
                b = reuse(pe, (l, "rep"))
                evacuated(pe, (l, "ikdk"))
                mm(b[:, 0:T], rep[0:IDX_DIM, 0, :], A["ikdk"][0:IDX_DIM, 0, :], start=True, stop=True)
                done(mm(b[:, T:2 * T], rep[0:HD, 1, :], A["ikdk"][0:HD, 1, :], start=True, stop=True), (l, "rep"))
                pair("a")
                evacuated(pe, (l, "iq"))
                evacuated(pe, (l, "rep"))
                for h in range(IDX_HEADS):
                    b = reuse(pe, (l, f"idx{h}"))
                    r = slice(32 * (h % 4), 32 * (h % 4) + 32)
                    for t in range(NT):
                        last = mm(b[:, K0[t]:K0[t] + KEYS[t]], A["iqT"][r, h // 4, tok(t)], A["ikdkT"][r, 0, 0:KEYS[t]], start=True, stop=True)
                    done(last, (l, f"idx{h}"))
                pair("b")
                u = loaded(pe, (l, "c"))
                s = slot(u, KD, C_DQ - 512)
                b = reuse(pe, (l, "c"))
                product(b[:, 0:T], lambda c: s[:, c, 0:P], lambda c: xT[:, c, :], KD)
                for t in range(NT):
                    last = product(b[:, T + ROPE * t:T + ROPE * (t + 1)], lambda c: xT[:, c, tok(t)], lambda c: s[:, c, P:P + ROPE], KD)
                done(last, (l, "c"))
                b = reuse(pe, (l, "ms"))
                for n in "abc":
                    evacuated(pe, (l, n))
                product(b[:, 0:T], lambda c: ones[:, :], lambda c: A["sq"][:, c, :], 3)
                done(product(b[:, T:2 * T], lambda c: ones[:, :], lambda c: A["sq"][:, 3 + c, :], 2), (l, "ms"))
                pair("d")
                pair("e")
                pe.wait_ge(sem("latents"), 2 * l + 2)
                us = [loaded(pe, (l, "qup0")), loaded(pe, (l, "qup1"))]
                for t in range(NT):
                    for h in range(2):
                        b = reuse(pe, (l, f"q{t}{h}"))
                        done(product(b[:, 0:384], lambda c: A["qaT"][:, c, tok(t)], lambda c: slot(us[h], 3, 384)[:, c, :], 3), (l, f"q{t}{h}"))
                uk = slot(loaded(pe, (l, "uk")), 2, 512)
                for j in range(4):
                    b = reuse(pe, (l, f"kn{j}"))
                    for i in range(2):
                        h = 2 * j + i
                        last = product(b[0:NOPE, T * i:T * (i + 1)], lambda c: uk[:, c, NOPE * h:NOPE * (h + 1)], lambda c: A["kvaT"][:, c, :], 2)
                    done(last, (l, f"kn{j}"))
                uv = slot(loaded(pe, (l, "uv")), 2, 512)
                for t in range(NT):
                    b = reuse(pe, (l, f"v{t}"))
                    done(product(b[:, :], lambda c: A["kvaT"][:, c, tok(t)], lambda c: uv[:, c, :], 2), (l, f"v{t}"))
                b = reuse(pe, (l, "krT"))
                pe.wait_ge(sem("kr_roped"), l + 1)
                for t in range(NT):
                    last = nc.tensor.transpose(b[0:QK, tok(t)], A["kr_tok"][:, t, :], ident[:, :])
                done(last, (l, "krT"))
                pe.wait_ge(sem("q_roped"), l + 1)
                for j in range(4):
                    b = reuse(pe, (l, f"qT{j}"))
                    for i in range(4):
                        h, t = 2 * j + i // 2, i % 2
                        last = nc.tensor.transpose(b[0:QK, P * i:P * (i + 1)], A["q_tok"][:, t, QK * h:QK * (h + 1)], ident[:, :])
                    done(last, (l, f"qT{j}"))
                for n in ["d", "e", "kn0", "kn1", "kn2", "kn3", "v0", "v1", "krT", "qT0", "qT1", "qT2", "qT3"]:
                    evacuated(pe, (l, n))

                def score(k, t, dst):
                    if k < HEADS:
                        return mm(dst, A["qT"][0:QK, k, tok(t)], A["kT"][0:QK, k, 0:KEYS[t]], start=True, stop=True)
                    h = k - HEADS
                    r = slice(64 * (h % 2), 64 * (h % 2) + 64)
                    return mm(dst, A["dqT"][r, h // 2, tok(t)], A["ikdkT"][r, 1, 0:KEYS[t]], start=True, stop=True)

                def value(k, t):
                    return A["v_tok"][:, t, HD * k:HD * (k + 1)] if k < HEADS else A["dv"][:, t, :]

                heads(l, 2 * HEADS, score, value, A["prob"], A["probT"])
                for j in range(HEADS):
                    evacuated(pe, (l, f"O{j}"))
                project_out(l, "y", A["mixT"], ["wo0", "wo1", "wo2", "wo3"])

            pe.wait_ge(sem("pool_set"), 4)
            pe.wait_ge(sem("ident_in"), 16)
            pe.wait_ge(sem("rep_in"), 16)
            pe.wait_ge(sem("gains_in"), 64)
            b = reuse(pe, (0, "gains"))
            done(nc.tensor.transpose(b[:, 0:10], gain_rows[:, :], ident[0:10, 0:10]), (0, "gains"))
            pe.wait_ge(sem("x_in"), 16)
            transpose_x(0, "in", lambda t: None)
            for t in range(NT):
                for g in range(2):
                    evacuated(pe, (0, f"inxT{t}{g}"))
            def route(l):
                for t in range(NT):
                    for g in range(2):
                        evacuated(pe, (l, f"yxT{t}{g}"))
                if l == 0:
                    pe.wait_ge(sem("router_in"), 80)
                    pe.wait_ge(sem("masks_in"), 64)
                b = reuse(pe, (l, "logit"))
                for t in range(NT):
                    last = product(b[:, E * t:E * (t + 1)], lambda c: xT[:, c, tok(t)], lambda c: router[:, c, :], KD)
                done(last, (l, "logit"))
                b = reuse(pe, (l, "rank"))
                pe.wait_ge(sem("chosen_ready"), l + 1)
                mm(b[:, 0:E], before, chosen[:, 0, :], start=True, stop=True)
                mm(b[:, E:2 * E], before, chosen[:, 1, :], start=True, stop=False)
                mm(b[:, E:2 * E], ones[:, :], chosen[:, 0, :], start=False, stop=True)
                done(product(b[:, 2 * E:3 * E], lambda c: ones[:, :], lambda c: chosen[:, c, :], NT), (l, "rank"))
                pe.wait_ge(sem("slots_ready"), 2 * l + 2)
                for q in range(4):
                    b = reuse(pe, (l, f"sgT{q}"))
                    for i in range(4):
                        last = nc.tensor.transpose(b[:, tok(i)], B["SG"][:, i % 2, tok(2 * q + i // 2)], ident[:, :])
                    done(last, (l, f"sgT{q}"))

            def gate_up(l, banks_gu):
                for q, (m, half) in enumerate((m, half) for half in range(2) for m in "gu"):
                    ws = [slot(W[(l, f"{m}{e}{half}")], 4, 512) for e in range(2)]
                    for c in range(4):
                        for e in range(2):
                            rows = slice(CAP * e, CAP * (e + 1))
                            last = mm(banks_gu["gu".index(m)][rows, :], B["xe"][:, 4 * half + c, rows], ws[e][:, c, :],
                                      start=(half == 0 and c == 0), stop=(half == 1 and c == 3))
                        if c == 3:
                            yield q, last

            def down(l, out, half):
                for c in range(MF):
                    for e in range(2):
                        rows = slice(CAP * e, CAP * (e + 1))
                        last = mm(out[rows, :], B["actT"][:, c, rows], slot(W[(l, f"w{e}{c // 2}")], 2, 1024)[:, c % 2, 512 * half:512 * (half + 1)],
                                  start=(c == 0), stop=(c == MF - 1))
                return last

            def experts(l):
                def tokens(i):
                    for g in range(2):
                        b = reuse(pe, (l, f"G{g}"), i)
                        for c in range(4):
                            for t in range(NT):
                                last = mm(b[:, tok(c)], x_tok[:, t, tok(4 * g + c)], B["S"][:, t, bass.ds(i * P, P)], start=(t == 0), stop=(t == 1))
                        done(last, (l, f"G{g}"))

                def pair(i, last_pair=False):
                    evacuated(pe, (l, "G0"), i)
                    evacuated(pe, (l, "G1"), i)
                    bs = [reuse(pe, (l, "Hg"), i), reuse(pe, (l, "Hu"), i)]
                    for e in range(2):
                        loaded(pe, (l, f"g{e}0"), i)
                    for q, last in gate_up(l, bs):
                        if q < 2:
                            last.then_inc(sem("quarter_used"), 1)
                        elif q == 2:
                            done(last, (l, "Hg"))
                        else:
                            done(last, (l, "Hu"))
                        if q < 3:
                            m, half = "ugu"[q], (0, 1, 1)[q]
                            for e in range(2):
                                loaded(pe, (l, f"{m}{e}{half}"), i)
                    if not last_pair:
                        tokens(i + 1)
                    b = reuse(pe, (l, "A"), i)
                    evacuated(pe, (l, "Hu"), i)
                    for c in range(MF):
                        last = nc.tensor.transpose(b[:, tok(c)], B["act"][:, tok(c)], ident[:, :])
                    done(last, (l, "A"))
                    for e in range(2):
                        for n in range(2):
                            loaded(pe, (l, f"w{e}{n}"), i)
                    evacuated(pe, (l, "A"), i)
                    for h in range(2):
                        b = reuse(pe, (l, f"Y{h}"), i)
                        done(down(l, b, h), (l, f"Y{h}"))
                    pe.wait_ge(sem("gates_copied"), i + (PAIRS * l + 1))
                    for t in range(NT):
                        for h in range(2):
                            b = reuse(pe, (l, f"M{t}{h}"), i)
                            evacuated(pe, (l, f"Y{h}"), i)
                            done(mm(b[:, :], B["sgp"][:, tok(t)], B["y"][:, 512 * h:512 * (h + 1)], start=True, stop=True), (l, f"M{t}{h}"))

                tokens(0)
                with pe.Fori(0, PAIRS - 1) as i:
                    pair(i)
                pair(PAIRS - 1, last_pair=True)

            def overflow(l):
                n_rounds = more_rounds(pe, l)
                with pe.If(n_rounds > 0):
                    with pe.Fori(0, n_rounds) as r:
                        with pe.Fori(0, PAIRS) as p:
                            n = r * PAIRS + p
                            pe.wait_ge(over(l, "added"), n + 1)
                            pe.wait_ge(over(l, "slots"), 2 * n + 2)
                            for g in range(2):
                                for c in range(4):
                                    product(bank[g][:, tok(c)], lambda t: x_tok[:, t, tok(4 * g + c)], lambda t: B["S"][:, t, 0:P], NT)
                            for t in range(NT):
                                last = nc.tensor.transpose(bank[6][:, tok(t)], B["SG"][:, t, 0:P], ident[:, :])
                            last.then_inc(over(l, "pe"), 1)
                            pe.wait_ge(over(l, "act"), 4 * n + 1)
                            pe.wait_ge(over(l, "loaded"), 16 * 12 * (n + 1))
                            for q, last in gate_up(l, [bank[2], bank[3]]):
                                if q == 3:
                                    last.then_inc(over(l, "pe"), 1)
                            pe.wait_ge(over(l, "hidden"), n + 1)
                            for c in range(MF):
                                last = nc.tensor.transpose(bank[4][:, tok(c)], B["act"][:, tok(c)], ident[:, :])
                            last.then_inc(over(l, "pe"), 1)
                            pe.wait_ge(over(l, "act"), 4 * n + 3)
                            for h in range(2):
                                last = down(l, bank[5 + h], h)
                            last.then_inc(over(l, "pe"), 1)
                            pe.wait_ge(over(l, "act"), 4 * n + 4)
                            for t in range(NT):
                                for h in range(2):
                                    last = mm(bank[out_banks[2 * t + h]][:, :], B["sgp"][:, tok(t)], B["y"][:, 512 * h:512 * (h + 1)], start=True, stop=True)
                            last.then_inc(over(l, "pe"), 1)

            for l in range(DEPTH):
                mixer(l)
                transpose_x(l, "y", lambda t: pe.wait_ge(sem("ln_done"), 4 * l + t + 1))
                route(l)
                experts(l)
                overflow(l)
                transpose_x(l, "m", lambda t: pe.wait_ge(sem("ln_done"), 4 * l + 2 + t + 1))
                for t in range(NT):
                    for g in range(2):
                        evacuated(pe, (l, f"mxT{t}{g}"))

            def pair(l, name):
                u = loaded(pe, (l, name))
                b = reuse(pe, (l, name))
                for i in range(2):
                    last = product(b[:, T * i:T * (i + 1)], lambda c: slot(u, KD, 256)[:, c, P * i:P * (i + 1)], lambda c: xT[:, c, :], KD)
                done(last, (l, name))

            def recurrent():
                b = reuse(pe, (2, "lbT"))
                pe.wait_ge(sem("lb_in"), 16)
                done(nc.tensor.transpose(b[:, 0:16], lb_rows[:, :], ident[0:16, 0:16]), (2, "lbT"))
                for n in "qf":
                    for i in range(4):
                        pair(2, f"h{n}{i}")
                for li in range(len(LEVELS) + 1):
                    for s in range(2):
                        if li == 0:
                            pe.wait_ge(sem("keys_ready"), 1)
                            for i in range(4):
                                evacuated(pe, (2, f"hq{i}"))
                        else:
                            pe.wait_ge(sem("scaled"), 2 * (li - 1) + s + 1)
                        q, k = (C["Q"], C["K"]) if li == 0 else (C["Qt"], C["Kt"])
                        for t in range(NT):
                            b = reuse(pe, (2, f"L{li}{s}{t}"))
                            for h in range(4):
                                last = mm(b[:, tok(h)], k[:, 4 * s + h, tok(t)], q[:, 4 * s + h, tok(t)], start=True, stop=True)
                            done(last, (2, f"L{li}{s}{t}"))
                    m, h, t = "iv"[li // 4], li % 4 // 2, li % 2
                    us = [loaded(pe, (2, f"h{m}{h}{g}")) for g in range(2)]
                    b = reuse(pe, (2, f"h{m}{t}{h}"))
                    done(product(b[:, :], lambda c: xT[:, c, tok(t)], lambda c: slot(us[c // 4], 4, 512)[:, c % 4, :], KD), (2, f"h{m}{t}{h}"))
                for s in range(2):
                    pe.wait_ge(sem("scaled"), 2 * len(LEVELS) + s + 1)
                    b = reuse(pe, (2, f"X{s}"))
                    for h in range(4):
                        last = mm(b[:, tok(h)], C["Kt"][:, 4 * s + h, 0:P], C["Qt"][:, 4 * s + h, P:T], start=True, stop=True)
                    done(last, (2, f"X{s}"))
                for t in range(NT):
                    for s in range(2):
                        evacuated(pe, (2, f"X{s}"))
                        evacuated(pe, (2, f"L{len(LEVELS)}{s}{t}"))
                        b = reuse(pe, (2, f"R{t}{s}"))
                        if t == 0 and s == 0:
                            for h in range(2):
                                for tt in range(2):
                                    evacuated(pe, (2, f"hi{tt}{h}"))
                        for i in range(4):
                            h = 4 * s + i
                            if t:
                                mm(b[:, tok(i)], C["SX"][:, h, :], C["V"][:, 0, tok(h)], start=True, stop=False)
                            last = mm(b[:, tok(i)], C["SA"][:, h, tok(t)], C["V"][:, t, tok(h)], start=(t == 0), stop=True)
                        done(last, (2, f"R{t}{s}"))
                for i in range(4):
                    pe.wait_ge(sem("recur_out"), i // 2 + 1)
                    b = reuse(pe, (2, f"hoT{i}"))
                    for c in range(4):
                        last = nc.tensor.transpose(b[:, tok(c)], C["O"][:, i // 2, tok(4 * (i % 2) + c)], ident[:, :])
                    done(last, (2, f"hoT{i}"))
                for i in range(4):
                    evacuated(pe, (2, f"hoT{i}"))
                project_out(2, "y", C["mixT"], ["ho0", "ho1", "ho2", "ho3"])

            def next_x(l, y, k):
                transpose_x(l, y, lambda t: pe.wait_ge(sem("ln_done"), 2 * k + t + 1))
                for t in range(NT):
                    for g in range(2):
                        evacuated(pe, (l, f"{y}xT{t}{g}"))

            def feed_forward(l):
                b = reuse(pe, (l, "cw"))
                pe.wait_ge(sem("cw_in"), 48 * (l - 1))
                for i in range(2):
                    last = nc.tensor.transpose(b[:, 88 * i:88 * (i + 1)], F["cw_rows"][0:88, i, :], ident[0:88, 0:88])
                done(last, (l, "cw"))

                def step(j, i):
                    us = [slot(loaded(pe, (l, f"F{n}{j}"), i), KD, 256) for n in "ab"]
                    for c in range(2):
                        b = reuse(pe, (l, f"U{j}{c}"), i)
                        for ab in range(2):
                            last = product(b[:, T * ab:T * (ab + 1)], lambda k: us[ab][:, k, tok(c)], lambda k: xT[:, k, :], KD)
                        done(last, (l, f"U{j}{c}"))

                with pe.Fori(0, FFN // 256 // 2) as i:
                    step(0, i)
                    step(1, i)
                step(2, None)
                bs = [[reuse(pe, (l, f"z{t}{h}")) for h in range(2)] for t in range(NT)]
                for k in range(GC):
                    if k % 2 == 0:
                        w = slot(loaded(pe, (l, f"Fw{k // 2}")), 2, 1024)
                    pe.wait_ge(sem("gated"), (l - 2) * GC + k + 1)
                    for t in range(NT):
                        for h in range(2):
                            last = mm(bs[t][h][:, :], F["gT"][:, k, tok(t)], w[:, k % 2, 512 * h:512 * (h + 1)], start=(k == 0), stop=(k == GC - 1))
                            if k == GC - 1:
                                done(last, (l, f"z{t}{h}"))
                    if k % 2 and k < GC - 1:
                        last.then_inc(sem("down_used"), 1)

            recurrent()
            next_x(2, "y", 4)
            pe.wait_ge(sem("rel_in"), 32)
            for i in range(SWQ):
                b = reuse(pe, (2, f"rb{i}"))
                done(mm(b[:, 0:NK], F["rel"][0:NBUCKET, i:i + 1].to_broadcast([NBUCKET, P]), F["pick"][0:NBUCKET, :], start=True, stop=True), (2, f"rb{i}"))
            feed_forward(2)
            next_x(2, "z", 5)
            pair(3, "kv0")
            u = loaded(pe, (3, "kv1"))
            b = reuse(pe, (3, "vv"))
            for t in range(NT):
                last = product(b[:, T * t:T * (t + 1)], lambda c: xT[:, c, tok(t)], lambda c: slot(u, KD, 256)[:, c, :], KD)
            done(last, (3, "vv"))
            evacuated(pe, (3, "kv0"))
            for i in range(SWKV):
                b = reuse(pe, (3, f"kR{i}"))
                r = slice(64 * (i % 2), 64 * (i % 2) + 64)
                done(mm(b[:, 0:T], rep[r, 1, :], G["kraw"][r, i // 2, :], start=True, stop=True), (3, f"kR{i}"))
            for i in range(4):
                pair(3, f"sq{i}")
            for n in ("vv", "kR0", "kR1", "kR2", "kR3", "sq0", "sq1", "sq2", "sq3"):
                evacuated(pe, (3, n))

            def score(k, t, dst):
                r = slice(64 * (k % 2), 64 * (k % 2) + 64)
                return mm(dst, G["qT"][r, k // 2, tok(t)], G["kR"][r, k // 4, 0:KEYS[t]], start=True, stop=True)

            heads(3, SWQ, score, lambda k, t: G["v"][:, t, SWD * (k // 4):SWD * (k // 4 + 1)], G["prob"], G["probT"])
            for j in range(SWQ // 2):
                evacuated(pe, (3, f"O{j}"))
            project_out(3, "y", G["mixT"], ["so0", "so1", "so2", "so3"])
            next_x(3, "y", 6)
            feed_forward(3)



_NAMES = [
    "x", "w_in", "q_norm_g", "w_q_up", "kv_norm_g", "w_uk", "w_uv", "w_o", "ln1_g", "ln1_b", "router_w", "router_bias",
    "w_gate", "w_up", "w_down", "ln2_g", "ln2_b", "hgrn_w_in_2", "hgrn_lb_logits_2", "hgrn_gnorm_w_2",
    "hgrn_w_out_2", "swa_w_q_2", "swa_sinks_2", "swa_w_out_2", "shared_w_kv_2", "rel_bias_2", "ffn_w_in_2",
    "ffn_conv_w_2", "ffn_conv_b_2", "ffn_w_out_2", "ln_mix_g_2", "ln_mix_b_2", "ln_ffn_g_2", "ln_ffn_b_2",
]


def kernel(**inputs):
    import concourse.bacc as bacc
    from concourse.bass_utils import run_bass_kernel_spmd

    nc = bacc.Bacc("TRN2", target_bir_lowering=False, num_devices=1)
    arrays = {"in_" + n: np.ascontiguousarray(inputs[n]) for n in _NAMES}
    arrays.update({"in_" + n: a for n, a in const_arrays().items()})
    io = {n[3:]: nc.dram_tensor(n, a.shape, mybir.dt.from_np(a.dtype), kind="ExternalInput").ap() for n, a in arrays.items()}
    out = nc.dram_tensor("out_0", (1, T, D), F32, kind="ExternalOutput").ap()
    build(nc, io, out)
    r = run_bass_kernel_spmd(nc, [arrays], core_ids=[0])
    return r.results[0]["out_0"]
```

```python
from contextlib import ExitStack

import numpy as np

import concourse.bass as bass
from concourse import mybir
from concourse.alu_op_type import AluOpType as ALU

F32 = mybir.dt.float32
F32R = mybir.dt.float32r
I32 = mybir.dt.int32
U32 = mybir.dt.uint32
ACT = mybir.ActivationFunctionType
AX = mybir.AxisListType

P = 128
T = 256
NT = T // P
D = 1024
KD = D // P
DEPTH = 2
ALPHA = (2.0 * DEPTH) ** 0.25
LN_EPS, RMS_EPS = 1e-5, 1e-6
NEG = -1.0e30
PICKED = -3.0e38

Q_LORA, KV_LORA, ROPE, HEADS, HD, IDX_HEADS, IDX_DIM = 384, 256, 32, 8, 64, 8, 32
NOPE = 64
QK = NOPE + ROPE
C_QA = 0
C_KVA = C_QA + Q_LORA
C_KR = C_KVA + KV_LORA
C_DQ = C_KR + ROPE
C_DK = C_DQ + HEADS * HD
C_DV = C_DK + HD
C_IQ = C_DV + HD
C_IK = C_IQ + IDX_HEADS * IDX_DIM
C_IW = C_IK + IDX_DIM
IN_COLS = C_IW + IDX_HEADS
N_IKW = IDX_DIM + IDX_HEADS
O_KR = T + NT * N_IKW
TOPK = T // 4
KEYS = [P * (t + 1) for t in range(NT)]
K0 = [0, P]
NK = sum(KEYS)
SLOPES = [2.0 ** (-8.0 * (h + 1) / HEADS) for h in range(HEADS)]

E, GROUPS, EPG, FF = 16, 4, 4, 512
CAP = 64
PAIRS = E // 2
MF = FF // P

HG_HEADS, HG_DIM = 8, 128
LEVELS = [1, 2, 4, 8, 16, 32, 64]
SWQ, SWKV, SWD = 16, 4, 64
FFN = 2816
CH = 2 * FFN // P
GC = FFN // P
NBUCKET, MAXDIST = 32, 128

STEPS = FFN // 256
NSLOT = 12
SLOT = 2048
RAW_SLOTS = 6
KV_UNIT = 16 + 2 * STEPS
FFN_UNIT = {2: 16, 3: KV_UNIT + 5}


class Use:

    def __init__(self, place, before):
        self.place, self.before, self.step, self.turns = place, before, 0, 1


class Ring:

    def __init__(self, size):
        self.size, self.count, self.at = size, [0] * size, 0
        self.open = None

    def take(self, place=None):
        if place is None:
            place = self.at % self.size
            self.at += 1
        u = Use(place, self.count[place])
        self.count[place] += 1
        if self.open is not None:
            self.open.append(u)
        return u

    def begin_loop(self):
        self.open = []
        self.start = list(self.count)

    def end_loop(self, turns):
        for u in self.open:
            u.step, u.turns = self.count[u.place] - self.start[u.place], turns
        for p in range(self.size):
            self.count[p] = self.start[p] + turns * (self.count[p] - self.start[p])
        self.open = None


def const_arrays():
    t = np.arange(T, dtype=np.float32)
    half = ROPE // 2
    inv = (10000.0 ** (-np.arange(half, dtype=np.float32) / half)).astype(np.float32)
    ang = (t[:, None] * inv[None, :]).astype(np.float32)
    rope = np.stack([np.cos(ang), np.sin(ang)], 1).astype(np.float32).reshape(NT, P, 2 * half)
    ident = np.eye(P, dtype=np.float32)
    before = np.triu(np.ones((P, P), np.float32), 1)
    q = np.arange(P)
    causal = np.zeros((P, NK), np.float32)
    for i in range(NT):
        s = np.arange(KEYS[i])
        causal[:, K0[i]:K0[i] + KEYS[i]] = np.where(s[None, :] <= (q + i * P)[:, None], 0.0, NEG)
    negdist = np.zeros((P, NK), np.float32)
    for i in range(NT):
        negdist[:, K0[i]:K0[i] + KEYS[i]] = np.arange(KEYS[i])[None, :] - (q + i * P)[:, None]
    rep = np.zeros((P, 2, P), np.float32)
    rep[:IDX_DIM, 0] = np.tile(np.eye(IDX_DIM), (1, P // IDX_DIM))
    rep[:HD, 1] = np.tile(np.eye(HD), (1, P // HD))
    rep[HD:, 1] = rep[:HD, 1]
    pos = np.tile(np.arange(CAP, dtype=np.float32), (P, 1))
    eidx = np.tile(np.arange(E, dtype=np.float32), (P, 1))
    gidx = np.tile(np.repeat(np.arange(GROUPS, dtype=np.float32), EPG), (P, 1))
    s, tt = np.arange(P)[:, None], np.arange(P)[None, :]
    levels = [(s == tt)]
    for m in LEVELS:
        levels.append((s // (2 * m) == tt // (2 * m)) & ((s // m) % 2 == 0) & ((tt // m) % 2 == 1))
    levels = np.stack(levels, 1).astype(np.int32)
    dist = q[:, None] + P - np.arange(2 * P)[None, :]
    band = np.where((dist >= 0) & (dist < P), 0.0, NEG).astype(np.float32)
    band = np.concatenate([band[:, P:], band], 1)
    d = 2 * P - 1 - np.arange(3 * P)
    exact = NBUCKET // 2
    safe = np.maximum(d, 1).astype(np.float32)
    logb = exact + (np.log(safe / np.float32(exact)) / np.float32(np.log(MAXDIST / exact)) * (NBUCKET - exact)).astype(np.int32)
    bucket = np.where(d < exact, np.maximum(d, 0), np.minimum(logb, NBUCKET - 1))
    pick = (bucket[None, :] == np.arange(NBUCKET)[:, None]).astype(np.float32)
    return {
        "c_ident": ident, "c_before": before,
        "c_rope": rope, "c_causal": causal, "c_negdist": negdist,
         "c_rep": rep, "c_pos": pos, "c_eidx": eidx, "c_gidx": gidx,
        "c_levels": levels, "c_band": band, "c_pick": pick,
    }



def plan():
    ring, banks = Ring(NSLOT), Ring(8)
    W, J, freed, order = {}, {}, {}, []

    def load(name, by):
        W[name] = ring.take()
        freed[name] = by
        order.append(name)

    def job(*name, bank=None):
        J[name] = banks.take(bank)

    plan_norm(job, 0, "in", False)
    job(0, "gains")
    for l in range(DEPTH):
        for n, by in (("f1", "ikdk"), ("f2", "ikdk"), ("c", "c"), ("iq", "iq"), ("a", "a"), ("b", "b"), ("d", "d"),
                      ("e", "e"), ("qup0", "q10"), ("qup1", "q11"), ("uk", "kn3"), ("uv", "v1")):
            load((l, n), (l, by))
        for n in range(4):
            load((l, f"wo{n}"), (l, "y11"))
        for n in ["ikdk", "iq", "dviw", "rep", "a"] + [f"idx{h}" for h in range(IDX_HEADS)] + ["b", "c", "ms", "d", "e",
                  "q00", "q01", "q10", "q11", "kn0", "kn1", "kn2", "kn3", "v0", "v1", "krT", "qT0", "qT1", "qT2", "qT3"]:
            job(l, n)
        plan_heads(job, l, 2 * HEADS)
        plan_norm(job, l, "y", True)
        for n in ("logit", "rank"):
            job(l, n)
        for q in range(4):
            job(l, f"sgT{q}", bank=4 + q)
        ring.begin_loop()
        banks.begin_loop()
        body = []
        quarters = [(m, i) for i in range(2) for m in "gu"]
        for q, (m, i) in enumerate(quarters):
            for e in range(2):
                load((l, f"{m}{e}{i}"), ("quarter_used", 2 * PAIRS * l + q + 1, 2) if q < 2 else (l, ("Hg", "Hu")[q - 2]))
                body.append(order.pop())
        for i in range(2):
            for e in range(2):
                load((l, f"w{e}{i}"), (l, "Y1"))
                body.append(order.pop())
        order.append((PAIRS, body))
        for n, b in (("G0", 0), ("G1", 1), ("Hg", 2), ("Hu", 3), ("A", 4), ("Y0", 5), ("Y1", 6),
                     ("M00", 7), ("M01", 4), ("M10", 7), ("M11", 4)):
            job(l, n, bank=b)
        ring.end_loop(PAIRS)
        banks.end_loop(PAIRS)
        plan_norm(job, l, "m", False)
    ring.size, ring.at = RAW_SLOTS, 0
    job(2, "lbT")
    for i in range(4):
        load((2, f"hq{i}"), ("split", 2 * (i + 1), 0))
        job(2, f"hq{i}")
    for i in range(4):
        load((2, f"hf{i}"), ("split", 2 * (4 + i + 1), 0))
        job(2, f"hf{i}")
    for n in range(8):
        load((2, f"h{'iv'[n // 4]}{n % 4 // 2}{n % 2}"), ("split", 2 * (8 + n + 1), 0))
    for li in range(len(LEVELS) + 1):
        for s in range(2):
            for t in range(NT):
                job(2, f"L{li}{s}{t}")
        if li % 2 == 0:
            for t in range(NT):
                job(2, f"h{'iv'[li // 4]}{t}{li % 4 // 2}")
    for s in range(2):
        job(2, f"X{s}")
    for t in range(NT):
        for s in range(2):
            job(2, f"R{t}{s}")
    for i in range(4):
        job(2, f"hoT{i}")
    for i in range(4):
        load((2, f"ho{i}"), (2, "y11"))
    plan_norm(job, 2, "y", True)
    for i in range(SWQ):
        job(2, f"rb{i}")
    plan_ffn(load, job, ring, banks, order, 2)
    load((3, "kv0"), ("split", 2 * (KV_UNIT + 1), 0))
    load((3, "kv1"), (3, "vv"))
    for n in ("kv0", "vv", "kR0", "kR1", "kR2", "kR3"):
        job(3, n)
    for i in range(4):
        load((3, f"sq{i}"), ("split", 2 * (KV_UNIT + 1 + i + 1), 0))
        job(3, f"sq{i}")
    plan_heads(job, 3, SWQ)
    for i in range(4):
        load((3, f"so{i}"), (3, "y11"))
    plan_norm(job, 3, "y", True)
    plan_ffn(load, job, ring, banks, order, 3)
    return W, J, freed, order


def plan_ffn(load, job, ring, banks, order, l):
    job(l, "cw")
    ring.begin_loop()
    banks.begin_loop()
    body = []
    for j in range(2):
        for n in "ab":
            load((l, f"F{n}{j}"), ("split", 2 * (FFN_UNIT[l] + 2 * (j + 1)), 8))
            body.append(order.pop())
        for c in range(2):
            job(l, f"U{j}{c}", bank=2 * j + c)
    order.append((STEPS // 2, body))
    ring.end_loop(STEPS // 2)
    banks.end_loop(STEPS // 2)
    for n in "ab":
        load((l, f"F{n}2"), ("split", 2 * (FFN_UNIT[l] + 2 * STEPS), 0))
    for c in range(2):
        job(l, f"U2{c}", bank=c)
    for i in range(GC // 2):
        load((l, f"Fw{i}"), ("down_used", (l - 2) * (GC // 2 - 1) + i + 1, 0) if i < GC // 2 - 1 else (l, "z11"))
    for n, b in (("00", 4), ("01", 5), ("10", 6), ("11", 7)):
        job(l, "z" + n, bank=b)
    if l < 3:
        plan_norm(job, l, "z", False)


def plan_heads(job, l, heads):
    for k in range(heads + 3):
        if k < heads:
            job(l, f"S{k}")
        if 0 <= k - 2 < heads:
            job(l, f"T{k - 2}")
        if 0 <= k - 3 < heads and (k - 3) % 2 == 0:
            job(l, f"O{(k - 3) // 2}")


def plan_norm(job, l, y, with_y):
    if with_y:
        for n in ("00", "01", "10", "11"):
            job(l, y + n)
    for n in ("00", "01", "10", "11"):
        job(l, y + "xT" + n)



def build(nc, io, out):
    W, J, freed, order = plan()
    with ExitStack() as ctx:
        def sb(name, shape, dt=F32):
            return ctx.enter_context(nc.sbuf_tensor(name, shape, dt))

        sems = {}

        def sem(name):
            if name not in sems:
                sems[name] = ctx.enter_context(nc.semaphore(name))
            return sems[name]

        bank_full = [sem(f"bank_full{b}") for b in range(8)]
        bank_free = [sem(f"bank_free{b}") for b in range(8)]
        slot_full = [sem(f"slot_full{s}") for s in range(NSLOT)]
        bank = [ctx.enter_context(nc.psum_tensor(f"bank{b}", [P, 512], F32)) for b in range(8)]

        slots = [sb(f"slot{s}", [P, SLOT]) for s in range(RAW_SLOTS)]
        with ExitStack() as first_block:
            slots += [first_block.enter_context(nc.sbuf_tensor(f"slot{s}", [P, SLOT], F32)) for s in range(RAW_SLOTS, NSLOT)]
        x_high = sb("x_high", [P, KD, T], F32R)
        x_low = sb("x_low", [P, KD, T], F32R)
        w_high = [sb(f"w_high{c}", [P, 2, KD, P], F32R) for c in range(2)]
        w_low = [sb(f"w_low{c}", [P, 2, KD, P], F32R) for c in range(2)]
        x_tok = sb("x_tok", [P, NT, D])
        xT = sb("xT", [P, KD, T])
        res = sb("res", [P, NT, D])
        ln_gb = sb("ln_gb", [P, 2, D])
        ident = sb("ident", [P, P])
        ones = sb("ones", [P, P])
        rope_cs = sb("rope_cs", [P, NT, ROPE])
        tables = sb("tables", [P, (len(LEVELS) + 1) * P])
        causal, negdist, before = tables[:, 0:NK], tables[:, NK:2 * NK], tables[:, 2 * NK:2 * NK + P]
        levels = tables[:, :].bitcast(I32).rearrange("p (l t) -> p l t", t=P)
        rep = sb("rep", [P, 2, P])
        eps = sb("eps", [P, 2])
        gains = sb("gains", [P, 10])
        gain_rows = sb("gain_rows", [10, P])
        ln_stats = sb("ln_stats", [P, NT, 2, 6])
        ln_mv = sb("ln_mv", [P, NT, 2])
        ln_std = sb("ln_std", [P, NT])
        negmax = sb("negmax", [P, 2 * HEADS, NT])
        rowsum = sb("rowsum", [P, 2 * HEADS, NT])
        rinv = sb("rinv", [P, 2 * HEADS, NT])

        router = sb("router", [P, KD, E])
        rbias = sb("rbias", [P, E])
        pos = sb("pos", [P, CAP])
        eidx = sb("eidx", [P, E])
        gidx = sb("gidx", [P, E])
        aff = sb("aff", [P, NT, E])
        biased = sb("biased", [P, NT, E])
        chosen = sb("chosen", [P, NT, E])
        gates = sb("gates", [P, NT, E])
        rank = sb("rank", [P, NT, E])
        pairs2 = sb("pairs2", [P, NT * GROUPS, 6])
        gscore = sb("gscore", [P, NT, 8])
        best = sb("best", [P, NT, 8])
        besti = sb("besti", [P, NT, 8], U32)
        bestf = sb("bestf", [P, NT, 2])
        wsum = sb("wsum", [P, NT])
        most = sb("most", [P, 4])
        rounds = sb("rounds", [P, DEPTH], I32)

        lb_rows = sb("lb_rows", [16, P])
        lb = sb("lb", [P, 4, 8])
        gnorm = sb("gnorm", [P, P])
        hsum = sb("hsum", [P, NT * HG_HEADS])
        sinks = sb("sinks", [P, 2, SWQ])
        sinkexp = sb("sinkexp", [P, SWQ, NT])

        ARENA = 17450
        arena = sb("arena", [P, ARENA])

        def carve(spec):
            got, at = {}, 0
            for name, *shape in spec:
                n = int(np.prod(shape))
                v = arena[:, at:at + n]
                if len(shape) == 2:
                    v = v.rearrange("p (a b) -> p a b", a=shape[0])
                elif len(shape) == 3:
                    v = v.rearrange("p (a b c) -> p a b c", a=shape[0], b=shape[1])
                got[name] = v
                at += n
            assert at <= ARENA, (at, spec)
            return got

        A = carve([("ikdk", 2, T), ("ikdkT", 2, T), ("iqT", 2, T), ("dqT", 4, T), ("qaT", 3, T), ("kvaT", 2, T),
                   ("sq", 5, T), ("rstd", 2, T), ("q_tok", NT, HEADS * QK), ("rt", NT * HEADS, 2 * 16), ("krt", NT, ROPE), ("kr_tok", NT, QK),
                   ("qT", HEADS, T), ("kT", HEADS, T), ("v_tok", NT, HEADS * HD), ("dv", NT, HD), ("iw", NT, IDX_HEADS),
                   ("relu", 2, NK), ("work", NK), ("top8", NT, 8), ("msel", NK), ("bias", 2, NK),
                   ("prob", 3, NK), ("probT", 2, NK)])
        A["mixT"] = carve([("latents", 10, T), ("mixT", 8, T)])["mixT"]

        B = carve([("S", NT, E * CAP), ("SG", NT, E * CAP), ("sgT", PAIRS, T), ("sgp", T), ("xe", KD, 2 * CAP),
                   ("silu", FF), ("act", FF), ("actT", MF, 2 * CAP), ("y", D)])

        C = carve([("Qt", HG_HEADS, T), ("Kt", HG_HEADS, T), ("SX", HG_HEADS, P), ("SA", HG_HEADS, NT * P), ("Pd", HG_HEADS, T), ("Sd", HG_HEADS, T),
                   ("Q", HG_HEADS, T), ("K", HG_HEADS, T), ("V", NT, D)])
        C["mixT"] = C["Qt"]
        C["O"] = C["Q"].rearrange("p h t -> p (h t)").rearrange("p (t n) -> p t n", t=NT)
        C["O2"] = C["K"].rearrange("p h t -> p (h t)").rearrange("p (t n) -> p t n", t=NT)
        F = carve([("gT", GC, T), ("conv", 4, T), ("gate", 2, T), ("cw_rows", 2, P), ("cw", 4, CH), ("cws", 2, 16), ("bias", SWQ, NK),
                   ("band", NK), ("rel", SWQ), ("pick", NK)])
        G = carve([("qT", 8, T), ("kraw", 2, T), ("kR", SWKV, T), ("v", NT, T), ("probT", 2, NK), ("prob", 3, NK)])
        G["bias"] = F["bias"]
        G["mixT"] = carve([("used", 54, T), ("mixT", 8, T)])["mixT"]

        def slot(u, k, n):
            return slots[u.place][:, 0:k * n].rearrange("p (k n) -> p k n", k=k)

        def at(u, i, more=0):
            v = u.before + more
            return v if i is None or u.step == 0 else v + i * u.step

        def loaded(eng, name, i=None):
            u = W[name]
            v = 16 * (u.before + 1)
            eng.wait_ge(slot_full[u.place], v if i is None else v + i * (16 * u.step))
            return u

        def reuse(pe, name, i=None):
            u = J[name]
            if u.before > 0:
                pe.wait_ge(bank_free[u.place], at(u, i))
            return bank[u.place]

        def done(ins, name):
            ins.then_inc(bank_full[J[name].place], 1)

        def produced(eng, name, i=None):
            eng.wait_ge(bank_full[J[name].place], at(J[name], i, 1))
            return bank[J[name].place]

        def drained(ins, name):
            ins.then_inc(bank_free[J[name].place], 1)

        def evacuated(eng, name, i=None):
            eng.wait_ge(bank_free[J[name].place], at(J[name], i, 1))

        class Chain:

            def __init__(self, eng, name):
                self.eng, self.sem, self.n, self.base = eng, sem(name), 0, None

            def __call__(self, ins):
                self.n += 1
                ins.then_inc(self.sem, 1)
                self.eng.wait_ge(self.sem, self.n if self.base is None else self.base + self.n)

        out_banks = [6, 7, 2, 4]

        def over(l, name):
            return sem(f"over_{name}{l}")

        def more_rounds(eng, l):
            eng.wait_ge(sem("rounds_ready"), l + 1)
            return eng.value_load(rounds[0:1, l:l + 1], min_val=0, max_val=T // CAP - 1)

        def flat(w):
            return w[:, :, :, :].rearrange("p a k n -> p (a k n)")

        def rows_name(n):
            return f"h{'iv'[n // 4]}{n % 4 // 2}{n % 2}"

        block = ctx.enter_context(nc.Block())
        heads_before = {0: 0, 1: 2 * HEADS, 3: 4 * HEADS}

        def w_src(name, p=None):
            l, n = name
            win = io["w_in"]
            cols = {"f1": (C_DK, C_IQ), "f2": (C_IK, IN_COLS), "iq": (C_IQ, C_IK), "a": (0, 256), "b": (256, 512),
                    "c": (512, C_DQ), "d": (C_DQ, C_DQ + 256), "e": (C_DQ + 256, C_DK)}
            if l >= DEPTH:
                i = int(n[-1])
                if n[:2] in ("hq", "hf"):
                    o = (0 if n[1] == "q" else D) + 256 * i
                    return [(io["hgrn_w_in_2"][0, :, o:o + 256], KD, 256)]
                if n[:2] in ("hi", "hv"):
                    o = (2 if n[1] == "i" else 3) * D + 512 * int(n[2])
                    return [(io["hgrn_w_in_2"][0, 512 * i:512 * (i + 1), o:o + 512], 4, 512)]
                if n[:2] == "ho":
                    return [(io["hgrn_w_out_2"][0, 256 * i:256 * (i + 1), :], 2, 1024)]
                if n[:2] == "so":
                    return [(io["swa_w_out_2"][0, 256 * i:256 * (i + 1), :], 2, 1024)]
                if n[:2] == "sq":
                    return [(io["swa_w_q_2"][0, :, 256 * i:256 * (i + 1)], KD, 256)]
                if n[:2] == "kv":
                    return [(io["shared_w_kv_2"][:, 256 * i:256 * (i + 1)], KD, 256)]
                if n[:2] == "Fw":
                    i = int(n[2:])
                    return [(io["ffn_w_out_2"][l - DEPTH, 256 * i:256 * (i + 1), :], 2, 1024)]
                if n[0] == "F":
                    j = STEPS - 1 if i == 2 else 2 * (0 if p is None else p) + i
                    o = FFN * (n[1] == "b") + 256 * j
                    x = slice(o, o + 256) if isinstance(o, int) else bass.ds(o, 256)
                    return [(io["ffn_w_in_2"][l - DEPTH, :, x], KD, 256)]
            if l < DEPTH:
                if n in cols:
                    a, b = cols[n]
                    return [(win[l, :, a:b], KD, b - a)]
                if n in ("qup0", "qup1"):
                    h = int(n[3]) * 384
                    return [(io["w_q_up"][l, :, h:h + 384], 3, 384)]
                if n in ("uk", "uv"):
                    return [(io["w_" + n][l], 2, 512)]
                if n.startswith("wo"):
                    i = int(n[2])
                    return [(io["w_o"][l, 256 * i:256 * (i + 1), :], 2, 1024)]
                m, e, i = n[0], int(n[1]), int(n[2])
                x = bass.ds(2 * p + e, 1) if p is not None else slice(e, e + 1)
                if m == "w":
                    src = io["w_down"][l, x, 256 * i:256 * (i + 1), :]
                    return [(src.rearrange("o r n -> (o r) n"), 2, 1024)]
                src = io["w_gate" if m == "g" else "w_up"][l, x, 512 * i:512 * (i + 1), :]
                return [(src.rearrange("o r n -> (o r) n"), 4, 512)]
            raise KeyError(name)

        skew = nc.dram_tensor("skew", [P, SWQ * NK], F32, kind="Internal").ap()

        @block.sync
        def _(sp):
            last = {}
            sp.dma_start(ident[:, :], io["c_ident"]).then_inc(sem("ident_in"), 16)
            for t in range(NT):
                sp.dma_start(x_tok[:, t, :], io["x"][0, P * t:P * (t + 1), :]).then_inc(sem(f"x_in{t}"), 16)

            def stream(name, i=None):
                u = W[name]
                if i is not None and isinstance(freed[name][0], str):
                    what, n, step = freed[name]
                    sp.wait_ge(sem(what), n + (i - 1) * step)
                elif i is not None:
                    f = J[freed[name]]
                    sp.wait_ge(bank_full[f.place], f.before + 1 + (i - 1) * f.step)
                elif u.place in last and isinstance(freed[last[u.place]][0], str):
                    what, n, step = freed[last[u.place]]
                    sp.wait_ge(sem(what), n + (W[last[u.place]].turns - 1) * step)
                elif u.place in last:
                    f = J[freed[last[u.place]]]
                    sp.wait_ge(bank_full[f.place], f.before + 1 + (f.turns - 1) * f.step)
                last[u.place] = name
                for src, k, n in w_src(name, i):
                    sp.dma_start(slot(u, k, n), src.rearrange("(k p) n -> p k n", p=P)).then_inc(slot_full[u.place], 16)

            def overflow(l, body):
                n_rounds = more_rounds(sp, l)
                with sp.If(n_rounds > 0):
                    with sp.Fori(0, n_rounds) as r:
                        with sp.Fori(0, PAIRS) as p:
                            sp.wait_ge(over(l, "added"), r * PAIRS + p + 1)
                            for name in body:
                                for src, k, n in w_src(name, p):
                                    sp.dma_start(slot(W[name], k, n), src.rearrange("(k p) n -> p k n", p=P)).then_inc(over(l, "loaded"), 16)
                    sp.wait_ge(over(l, "done"), 1)

            for entry in order:
                if isinstance(entry[0], int) and isinstance(entry[1], list):
                    turns, body = entry
                    for name in body:
                        stream(name)
                    with sp.Fori(1, turns) as i:
                        for name in body:
                            stream(name, i)
                    if body[0][0] < DEPTH:
                        overflow(body[0][0], body)
                else:
                    stream(entry)
            norms = 2 * DEPTH * 2 * NT
            for t in range(NT):
                sp.wait_ge(sem("ln_done"), norms - NT + t + 1)
                sp.dma_start(out[0, P * t:P * (t + 1), :], x_tok[:, t, :]).then_inc(sem("stored"), 16)
            sp.wait_ge(sem("stored"), 16 * NT)

        @block.gpsimd
        def _(pool):
            pool.memset(ones[:, :], 1.0).then_inc(sem("pool_set"), 1)
            pool.memset(eps[:, 0:1], LN_EPS).then_inc(sem("pool_set"), 1)
            pool.memset(eps[:, 1:2], RMS_EPS).then_inc(sem("pool_set"), 1)
            pool.memset(A["kr_tok"], 0.0).then_inc(sem("pool_set"), 1)

            def norm_rows(k, g, b):
                if k:
                    pool.wait_ge(sem("ln_done"), 2 * k)
                pool.dma_start(ln_gb[:, 0, :], g.unsqueeze(0).to_broadcast([P, D])).then_inc(sem("ln_rows"), 16)
                pool.dma_start(ln_gb[:, 1, :], b.unsqueeze(0).to_broadcast([P, D])).then_inc(sem("ln_rows"), 16)

            pool.memset(gscore[:, :, :], NEG).then_inc(sem("pool_set2"), 1)
            pool.dma_start(router[:, :, :], io["router_w"].rearrange("(k p) n -> p k n", p=P)).then_inc(sem("router_in"), 16)
            pool.dma_start(rbias[:, :], io["router_bias"].unsqueeze(0).to_broadcast([P, E])).then_inc(sem("router_in"), 16)
            pool.dma_start(pos[:, :], io["c_pos"]).then_inc(sem("router_in"), 16)
            pool.dma_start(eidx[:, :], io["c_eidx"]).then_inc(sem("router_in"), 16)
            pool.dma_start(gidx[:, :], io["c_gidx"]).then_inc(sem("router_in"), 16)
            norm_rows(0, io["ln1_g"][0], io["ln1_b"][0])
            norm_rows(1, io["ln2_g"][0], io["ln2_b"][0])
            norm_rows(2, io["ln1_g"][1], io["ln1_b"][1])
            norm_rows(3, io["ln2_g"][1], io["ln2_b"][1])
            pool.dma_start(lb_rows[:, :], io["hgrn_lb_logits_2"].rearrange("a (c p) -> (a c) p", p=P)).then_inc(sem("lb_in"), 16)
            pool.dma_start(gnorm[:, :], io["hgrn_gnorm_w_2"].to_broadcast([P, P])).then_inc(sem("gnorm_in"), 16)
            pool.dma_start(sinks[:, 0, :], io["swa_sinks_2"].to_broadcast([P, SWQ])).then_inc(sem("sinks_in"), 16)
            pool.wait_ge(sem("ln_done"), 8)
            pool.dma_start(levels, io["c_levels"]).then_inc(sem("levels_in"), 16)
            norm_rows(4, io["ln_mix_g_2"][0], io["ln_mix_b_2"][0])
            pool.memset(C["Sd"], 1.0).then_inc(sem("recur_set"), 1)
            pool.memset(C["SA"], 0.0).then_inc(sem("recur_set"), 1)
            pool.memset(C["Qt"], 0.0).then_inc(sem("recur_set"), 1)
            pool.memset(C["Kt"], 0.0).then_inc(sem("recur_set"), 1)
            chain = Chain(pool, "pool_chain")
            for li, m in enumerate(LEVELS):
                for s in range(2):
                    Pd, Sd = (C[n][:, 4 * s:4 * s + 4, :].rearrange("p h n -> p (h n)").rearrange("p (b j m) -> p b j m", j=2, m=m) for n in ("Pd", "Sd"))
                    nb = 4 * T // (2 * m)
                    pool.wait_ge(sem("scaled"), 2 * li + s + 1)
                    chain(nc.gpsimd.tensor_tensor(Sd[:, :, 0, :], Sd[:, :, 0, :], Pd[:, :, 1, m - 1:m].to_broadcast([P, nb, m]), ALU.mult))
                    nc.gpsimd.tensor_tensor(Pd[:, :, 1, :], Pd[:, :, 1, :], Pd[:, :, 0, m - 1:m].to_broadcast([P, nb, m]), ALU.mult)\
                        .then_inc(sem("decays"), 1)
            norm_rows(5, io["ln_ffn_g_2"][0], io["ln_ffn_b_2"][0])
            pool.dma_start(F["band"], io["c_band"]).then_inc(sem("band_in"), 16)
            pool.dma_start(F["rel"][0:NBUCKET, :], io["rel_bias_2"]).then_inc(sem("rel_in"), 16)
            pool.dma_start(F["pick"][0:NBUCKET, :], io["c_pick"]).then_inc(sem("rel_in"), 16)

            def conv_rows(l):
                pool.dma_start(F["cw_rows"][0:88, 0, :], io["ffn_conv_w_2"][l].rearrange("k n -> (k n)").rearrange("(r p) -> r p", p=P)[0:88, :]).then_inc(sem("cw_in"), 16)
                pool.dma_start(F["cw_rows"][0:44, 1, :], io["ffn_conv_w_2"][l].rearrange("k n -> (k n)").rearrange("(r p) -> r p", p=P)[88:132, :]).then_inc(sem("cw_in"), 16)
                pool.dma_start(F["cw_rows"][44:88, 1, :], io["ffn_conv_b_2"][l].rearrange("(r p) -> r p", p=P)).then_inc(sem("cw_in"), 16)

            conv_rows(0)
            for i in range(SWQ - 8, SWQ):
                evacuated(pool, (2, f"rb{i}"))
            pool.dma_start(skew, F["bias"].rearrange("p h n -> p (h n)")).then_inc(sem("skew_out"), 16)
            pool.wait_ge(sem("skew_out"), 16)
            for t, o in ((0, P), (1, 0)):
                src = bass.AP(skew.tensor, P - 1 + o, [[SWQ * NK - 1, P], [NK, SWQ], [1, KEYS[t]]])
                pool.dma_start(F["bias"][:, :, K0[t]:K0[t] + KEYS[t]], src).then_inc(sem("skew_in"), 16)
            pool.wait_ge(sem("skew_in"), 32)
            pool.wait_ge(sem("band_in"), 16)
            nc.gpsimd.tensor_tensor(F["bias"], F["bias"], F["band"].unsqueeze(1).to_broadcast([P, SWQ, NK]), ALU.add).then_inc(sem("bias_ready"), 1)
            norm_rows(6, io["ln_mix_g_2"][1], io["ln_mix_b_2"][1])
            conv_rows(1)
            norm_rows(7, io["ln_ffn_g_2"][1], io["ln_ffn_b_2"][1])

        @block.scalar
        def _(act):
            link = Chain(act, "act_chain")
            act.dma_start(rep[:, :, :], io["c_rep"]).then_inc(sem("rep_in"), 16)
            for l in range(DEPTH):
                act.dma_start(gain_rows[5 * l:5 * l + 3, :], io["q_norm_g"][l].rearrange("(a p) -> a p", p=P)).then_inc(sem("gains_in"), 16)
                act.dma_start(gain_rows[5 * l + 3:5 * l + 5, :], io["kv_norm_g"][l].rearrange("(a p) -> a p", p=P)).then_inc(sem("gains_in"), 16)
            act.dma_start(causal, io["c_causal"]).then_inc(sem("masks_in"), 16)
            act.dma_start(negdist, io["c_negdist"]).then_inc(sem("masks_in"), 16)
            act.dma_start(rope_cs[:, :, :], io["c_rope"].rearrange("t p n -> p t n")).then_inc(sem("masks_in"), 16)
            act.dma_start(before, io["c_before"]).then_inc(sem("masks_in"), 16)

            def copy(dst, src):
                return nc.scalar.activation(dst, src, ACT.Copy)

            def transposed(l, y):
                for t in range(NT):
                    for g in range(2):
                        b = produced(act, (l, f"{y}xT{t}{g}"))
                        drained(copy(xT[:, 4 * g:4 * g + 4, P * t:P * (t + 1)],
                                     b[:, :].rearrange("p (c n) -> p c n", c=4)), (l, f"{y}xT{t}{g}"))

            def split_slot(l, name, n):
                raw = slot(loaded(act, (l, name)), KD, 256)
                for ab in range(2):
                    copy(w_high[n % 2][:, ab, :, :], raw[:, :, P * ab:P * (ab + 1)]).then_inc(sem("high_ready"), 1)

            def transposed_split(l, y, whole=False):
                for t in range(NT):
                    for g in range(2):
                        b = produced(act, (l, f"{y}xT{t}{g}"))
                        if whole:
                            copy(xT[:, 4 * g:4 * g + 4, P * t:P * (t + 1)], b[:, :].rearrange("p (c n) -> p c n", c=4))
                        copy(x_high[:, 4 * g:4 * g + 4, P * t:P * (t + 1)], b[:, :].rearrange("p (c n) -> p c n", c=4)).then_inc(sem("x_high_ready"), 1)

            def norm_std(k):
                for t in range(NT):
                    act.wait_ge(sem("ln_moments"), 2 * k + t + 1)
                    nc.scalar.activation(ln_std[:, t:t + 1], ln_mv[:, t, 1:2], ACT.Sqrt, bias=eps[:, 0:1]).then_inc(sem("ln_root"), 1)

            def softmax_heads(l, heads, probs, probsT, outT, sink=False, scaled_here=0):
                base = heads_before[l]
                for k in range(heads + 4):
                    if k < heads:
                        act.wait_ge(sem("max_ready"), base + k + 1)
                        if sink:
                            nc.scalar.activation(sinkexp[:, k, :], negmax[:, k, :], ACT.Exp, bias=sinks[:, 0, k:k + 1])
                        for t in range(NT):
                            w = probs[:, k % 3, K0[t]:K0[t] + KEYS[t]]
                            last = nc.scalar.activation(w, w, ACT.Exp, bias=negmax[:, k, t:t + 1], accum_out=rowsum[:, k, t:t + 1])
                        last.then_inc(sem("exp_done"), 1)
                    if 1 <= k <= scaled_here:
                        j = k - 1
                        act.wait_ge(sem("rinv_ready"), l * scaled_here + j + 1)
                        for t in range(NT):
                            w = probs[:, j % 3, K0[t]:K0[t] + KEYS[t]]
                            last = nc.scalar.activation(w, w, ACT.Copy, scale=rinv[:, j, t:t + 1])
                        last.then_inc(sem("probs_scaled"), 1)
                    if 0 <= k - 2 < heads:
                        b = produced(act, (l, f"T{k - 2}"))
                        drained(copy(probsT[:, k % 2, :], b[:, 0:NK]), (l, f"T{k - 2}"))
                    if k >= 4 and k % 2 == 0:
                        j = (k - 4) // 2
                        b = produced(act, (l, f"O{j}"))
                        drained(copy(outT[:, j, :], b[:, 0:T]), (l, f"O{j}"))

            def mixer(l):
                b = produced(act, (l, "ikdk"))
                copy(A["ikdk"][0:N_IKW, 0, :], b[0:N_IKW, 0:T])
                copy(A["ikdk"][64:64 + ROPE, 0, :], b[64:64 + ROPE, 0:T])
                drained(copy(A["ikdk"][:, 1, :], b[:, T:2 * T]), (l, "ikdk"))
                b = produced(act, (l, "iq"))
                drained(copy(A["iqT"], b[:, :].rearrange("p (c n) -> p c n", c=2)), (l, "iq"))
                b = produced(act, (l, "dviw"))
                copy(A["dv"], b[:, 0:T].rearrange("p (t n) -> p t n", t=NT)[:, :, HD:2 * HD])
                copy(A["krt"], b[:, O_KR:O_KR + NT * ROPE].rearrange("p (t n) -> p t n", t=NT))
                drained(nc.scalar.activation(A["iw"], b[:, T:T + NT * N_IKW].rearrange("p (t n) -> p t n", t=NT)[:, :, IDX_DIM:N_IKW],
                                             ACT.Copy, scale=IDX_HEADS ** -0.5), (l, "dviw"))
                b = produced(act, (l, "rep"))
                drained(copy(A["ikdkT"], b[:, :].rearrange("p (c n) -> p c n", c=2)), (l, "rep"))

                def squares(name, parts):
                    b = produced(act, (l, name))
                    for i, (dst, sq, g) in enumerate(parts):
                        src = b[:, T * i:T * (i + 1)]
                        nc.scalar.activation(A["sq"][:, sq, :], src, ACT.Square)
                        last = nc.scalar.activation(dst, src, ACT.Copy, scale=gains[:, 5 * l + g:5 * l + g + 1])
                    return b, last

                if l == 0:
                    evacuated(act, (0, "gains"))
                _, last = squares("a", [(A["qaT"][:, 0, :], 0, 0), (A["qaT"][:, 1, :], 1, 1)])
                drained(last, (l, "a"))
                for h in range(IDX_HEADS):
                    b = produced(act, (l, f"idx{h}"))
                    if h >= 2:
                        act.wait_ge(sem("idx_added"), IDX_HEADS * l + h - 1)
                    drained(nc.scalar.activation(A["relu"][:, h % 2, :], b[:, 0:NK], ACT.Relu, scale=IDX_DIM ** -0.5), (l, f"idx{h}"))
                _, last = squares("b", [(A["qaT"][:, 2, :], 2, 2), (A["kvaT"][:, 0, :], 3, 3)])
                drained(last, (l, "b"))
                _, last = squares("c", [(A["kvaT"][:, 1, :], 4, 4)])
                drained(last, (l, "c"))
                b = produced(act, (l, "ms"))
                nc.scalar.activation(A["rstd"][:, 0, :], b[:, 0:T], ACT.Sqrt, bias=eps[:, 1:2], scale=1.0 / Q_LORA)
                drained(nc.scalar.activation(A["rstd"][:, 1, :], b[:, T:2 * T], ACT.Sqrt, bias=eps[:, 1:2], scale=1.0 / KV_LORA), (l, "ms"))
                for i, n in enumerate("de"):
                    b = produced(act, (l, n))
                    drained(copy(A["dqT"][:, 2 * i:2 * i + 2, :], b[:, :].rearrange("p (c n) -> p c n", c=2)), (l, n))
                for t in range(NT):
                    for h in range(2):
                        b = produced(act, (l, f"q{t}{h}"))
                        drained(copy(A["q_tok"][:, t, 384 * h:384 * (h + 1)], b[:, 0:384]), (l, f"q{t}{h}"))
                for j in range(4):
                    b = produced(act, (l, f"kn{j}"))
                    drained(copy(A["kT"][0:NOPE, 2 * j:2 * j + 2, :], b[0:NOPE, :].rearrange("p (c n) -> p c n", c=2)), (l, f"kn{j}"))
                for t in range(NT):
                    b = produced(act, (l, f"v{t}"))
                    drained(copy(A["v_tok"][:, t, :], b[:, :]), (l, f"v{t}"))
                for j in range(4):
                    b = produced(act, (l, f"qT{j}"))
                    drained(copy(A["qT"][0:QK, 2 * j:2 * j + 2, :], b[0:QK, :].rearrange("p (c n) -> p c n", c=2)), (l, f"qT{j}"))
                softmax_heads(l, 2 * HEADS, A["prob"], A["probT"], A["mixT"], scaled_here=HEADS)

            def experts(l):
                b = produced(act, (l, "logit"))
                drained(nc.scalar.activation(aff[:, :, :], b[:, 0:NT * E].rearrange("p (t e) -> p t e", t=NT), ACT.Sigmoid), (l, "logit"))

                def tokens(i):
                    for g in range(2):
                        b = produced(act, (l, f"G{g}"), i)
                        drained(copy(B["xe"][:, 4 * g:4 * g + 4, :], b[:, :].rearrange("p (c n) -> p c n", c=4)), (l, f"G{g}"))

                def pair(i, last=False):
                    b = produced(act, (l, "Hg"), i)
                    drained(nc.scalar.activation(B["silu"], b[:, :], ACT.Silu), (l, "Hg"))
                    if not last:
                        tokens(i + 1)
                    b = produced(act, (l, "A"), i)
                    drained(copy(B["actT"], b[:, :].rearrange("p (c n) -> p c n", c=MF)), (l, "A"))
                    for g in range(2):
                        b = produced(act, (l, f"Y{g}"), i)
                        drained(copy(B["y"][:, 512 * g:512 * (g + 1)], b[:, :]), (l, f"Y{g}"))

                tokens(0)
                for q in range(4):
                    b = produced(act, (l, f"sgT{q}"))
                    drained(copy(B["sgT"][:, 2 * q:2 * q + 2, :], b[:, :].rearrange("p (c n) -> p c n", c=2)), (l, f"sgT{q}"))
                with act.Fori(0, PAIRS - 1) as i:
                    pair(i)
                pair(PAIRS - 1, last=True)

            def overflow(l):
                n_rounds = more_rounds(act, l)
                with act.If(n_rounds > 0):
                    with act.Fori(0, n_rounds) as r:
                        with act.Fori(0, PAIRS) as p:
                            n = r * PAIRS + p
                            act.wait_ge(over(l, "pe"), 5 * n + 1)
                            for g in range(2):
                                copy(B["xe"][:, 4 * g:4 * g + 4, :], bank[g][:, :].rearrange("p (c n) -> p c n", c=4))
                            copy(B["sgp"], bank[6][:, 0:T]).then_inc(over(l, "act"), 1)
                            act.wait_ge(over(l, "pe"), 5 * n + 2)
                            nc.scalar.activation(B["silu"], bank[2][:, :], ACT.Silu).then_inc(over(l, "act"), 1)
                            act.wait_ge(over(l, "pe"), 5 * n + 3)
                            copy(B["actT"], bank[4][:, :].rearrange("p (c n) -> p c n", c=MF)).then_inc(over(l, "act"), 1)
                            act.wait_ge(over(l, "pe"), 5 * n + 4)
                            for g in range(2):
                                last = copy(B["y"][:, 512 * g:512 * (g + 1)], bank[5 + g][:, :])
                            last.then_inc(over(l, "act"), 1)

            act.wait_ge(sem("pool_set"), 4)
            transposed(0, "in")
            for l in range(DEPTH):
                mixer(l)
                norm_std(2 * l)
                transposed(l, "y")
                experts(l)
                overflow(l)
                norm_std(2 * l + 1)
                if l < DEPTH - 1:
                    transposed(l, "m")
                else:
                    transposed_split(l, "m")

            def recurrent():
                names = [f"h{n}{i}" for n in "qf" for i in range(4)]

                def split_rows(n):
                    u = loaded(act, (2, rows_name(n)))
                    for ab in range(2):
                        half = slice(SLOT // 2 * ab, SLOT // 2 * (ab + 1))
                        copy(flat(w_high[n % 2])[:, half], slots[u.place][:, half]).then_inc(sem("high_ready"), 1)

                for n in range(2):
                    split_slot(2, names[n], n)
                evacuated(act, (2, "lbT"))
                act.wait_ge(sem("lb_shifted"), 1)
                nc.scalar.activation(lb[:, 0:2, :], lb[:, 0:2, :], ACT.Exp).then_inc(sem("lb_exp"), 1)
                for i in range(4):
                    b = produced(act, (2, f"hq{i}"))
                    split_slot(2, names[i + 2], i + 2)
                    drained(nc.scalar.activation(C["Q"][:, 2 * i:2 * i + 2, :], b[:, :].rearrange("p (c n) -> p c n", c=2), ACT.Silu), (2, f"hq{i}"))
                for i in range(4):
                    b = produced(act, (2, f"hf{i}"))
                    if i < 2:
                        split_slot(2, names[i + 6], i + 6)
                    else:
                        split_rows(i - 2)
                    drained(nc.scalar.activation(C["Pd"][:, 2 * i:2 * i + 2, :], b[:, :].rearrange("p (c n) -> p c n", c=2), ACT.Sigmoid), (2, f"hf{i}"))
                for li in range(len(LEVELS) + 1):
                    m, h = "iv"[li // 4], li % 4 // 2
                    c = slice(512 * h, 512 * (h + 1))
                    for t in range(NT if li % 2 else 0):
                        b = produced(act, (2, f"h{m}{t}{h}"))
                        if m == "i":
                            drained(copy(C["V"][:, t, c], b[:, :]), (2, f"h{m}{t}{h}"))
                        else:
                            drained(nc.scalar.activation(res[:, t, c], b[:, :], ACT.Silu), (2, f"h{m}{t}{h}"))
                    if li + 2 <= len(LEVELS):
                        produced(act, (2, f"L{li + 1}00"))
                        split_rows(li + 2)
                for s in range(2):
                    b = produced(act, (2, f"X{s}"))
                    drained(copy(C["SX"][:, 4 * s:4 * s + 4, :], b[:, :].rearrange("p (c n) -> p c n", c=4)), (2, f"X{s}"))
                for t in range(NT):
                    for s in range(2):
                        b = produced(act, (2, f"R{t}{s}"))
                        drained(copy(C["O"][:, t, 512 * s:512 * (s + 1)], b[:, :]), (2, f"R{t}{s}"))
                for t in range(NT):
                    act.wait_ge(sem("head_sums"), t + 1)
                    sums = hsum[:, HG_HEADS * t:HG_HEADS * (t + 1)]
                    nc.scalar.activation(sums, sums, ACT.Sqrt, bias=eps[:, 1:2], scale=1.0 / HG_DIM).then_inc(sem("head_roots"), 1)
                for i in range(4):
                    b = produced(act, (2, f"hoT{i}"))
                    drained(copy(C["mixT"][:, 4 * (i % 2):4 * (i % 2) + 4, P * (i // 2):P * (i // 2 + 1)], b[:, :].rearrange("p (c n) -> p c n", c=4)), (2, f"hoT{i}"))

            def feed_forward(l):
                b = produced(act, (l, "cw"))
                drained(copy(F["cw"], b[:, 0:4 * CH].rearrange("p (k n) -> p k n", k=4)), (l, "cw"))

                def split(j, i, c):
                    for ab, n in enumerate("ab"):
                        raw = slot(loaded(act, (l, f"F{n}{j}"), i), KD, 256)
                        copy(w_high[c][:, ab, :, :], raw[:, :, P * c:P * (c + 1)]).then_inc(sem("high_ready"), 1)

                def step(j, i, following):
                    base = (l - 2) * STEPS + (STEPS - 1 if i is None else j)
                    more = 0 if i is None else 2 * i
                    for c in range(2):
                        b = produced(act, (l, f"U{j}{c}"), i)
                        if following:
                            split(*following, c)
                        if c == 0:
                            act.wait_ge(sem("taps"), base + 1 + more)
                        for ab in range(2):
                            w = F["cws"][:, j % 2, :].rearrange("p (k a c) -> p k a c", k=4, a=2)
                            last = nc.scalar.activation(F["conv"][:, 2 * c + ab, :], b[:, T * ab:T * (ab + 1)], ACT.Identity,
                                                        bias=w[:, 3, ab, c:c + 1], scale=w[:, 2, ab, c:c + 1])
                        last.then_inc(sem("conv_begun"), 1)
                    for c in range(2):
                        act.wait_ge(sem("conv_done"), 2 * base + c + 1 + 2 * more)
                        nc.scalar.activation(F["gate"][:, c, :], F["conv"][:, 2 * c, :], ACT.Silu).then_inc(sem("gate_done"), 1)

                for c in range(2):
                    split(0, 0, c)
                with act.Fori(0, STEPS // 2 - 1) as i:
                    step(0, i, (1, i))
                    step(1, i, (0, i + 1))
                i = STEPS // 2 - 1
                step(0, i, (1, i))
                step(1, i, (2, None))
                step(2, None, None)

            recurrent()
            norm_std(4)
            transposed_split(2, "y")
            for i in range(SWQ):
                b = produced(act, (2, f"rb{i}"))
                drained(copy(F["bias"][:, i, :], b[:, 0:NK]), (2, f"rb{i}"))
            feed_forward(2)
            norm_std(5)
            transposed_split(2, "z", whole=True)
            names = ["kv0"] + [f"sq{i}" for i in range(4)]
            for n in range(2):
                split_slot(3, names[n], KV_UNIT + n)
            b = produced(act, (3, "kv0"))
            split_slot(3, names[2], KV_UNIT + 2)
            drained(copy(G["kraw"], b[:, :].rearrange("p (c n) -> p c n", c=2)), (3, "kv0"))
            b = produced(act, (3, "vv"))
            drained(copy(G["v"], b[:, :].rearrange("p (c n) -> p c n", c=2)), (3, "vv"))
            for i in range(SWKV):
                b = produced(act, (3, f"kR{i}"))
                drained(copy(G["kR"][:, i, :], b[:, 0:T]), (3, f"kR{i}"))
            for i in range(4):
                b = produced(act, (3, f"sq{i}"))
                if i < 2:
                    split_slot(3, names[i + 3], KV_UNIT + i + 3)
                drained(copy(G["qT"][:, 2 * i:2 * i + 2, :], b[:, :].rearrange("p (c n) -> p c n", c=2)), (3, f"sq{i}"))
            softmax_heads(3, SWQ, G["prob"], G["probT"], G["mixT"], sink=True)
            norm_std(6)
            transposed_split(3, "y")
            feed_forward(3)
            norm_std(7)

        @block.vector
        def _(dve):
            link = Chain(dve, "dve_chain")
            V = nc.vector
            b = produced(dve, (0, "gains"))
            drained(V.tensor_copy(gains[:, :], b[:, 0:10]), (0, "gains"))

            def norm(k, l, y, from_psum):
                for t in range(NT):
                    for h in range(2):
                        cols = slice(512 * h, 512 * (h + 1))
                        if from_psum:
                            b = produced(dve, (l, f"{y}{t}{h}"))
                            ins = V.scalar_tensor_tensor(res[:, t, cols], x_tok[:, t, cols], ALPHA, b[:, :], ALU.mult, ALU.add)
                            drained(ins, (l, f"{y}{t}{h}"))
                            evacuated(dve, (l, f"{y}{t}{h}"))
                        last = V.bn_stats(ln_stats[:, t, h, :], res[:, t, cols])
                    link(last)
                    V.bn_aggr(ln_mv[:, t, :], ln_stats[:, t, :, :].rearrange("p a b -> p (a b)")).then_inc(sem("ln_moments"), 1)
                    dve.wait_ge(sem("ln_moments"), 2 * k + t + 1)
                    dve.wait_ge(sem("ln_rows"), 32 * (k + 1))
                    link(V.scalar_tensor_tensor(res[:, t, :], res[:, t, :], ln_mv[:, t, 0:1], ln_gb[:, 0, :], ALU.subtract, ALU.mult))
                    dve.wait_ge(sem("ln_root"), 2 * k + t + 1)
                    link(V.reciprocal(ln_std[:, t:t + 1], ln_std[:, t:t + 1]))
                    V.scalar_tensor_tensor(x_tok[:, t, :], res[:, t, :], ln_std[:, t:t + 1], ln_gb[:, 1, :], ALU.mult, ALU.add)\
                        .then_inc(sem("ln_done"), 1)

            def softmax_head(l, k, probs, scale, bias, sink=False):
                base = heads_before[l]
                b = produced(dve, (l, f"S{k}"))
                if k >= 3:
                    produced(dve, (l, f"T{k - 3}"))
                ins = V.scalar_tensor_tensor(probs[:, k % 3, :], b[:, 0:NK], scale, bias, ALU.mult, ALU.add)
                drained(ins, (l, f"S{k}"))
                evacuated(dve, (l, f"S{k}"))
                for t in range(NT):
                    last = V.tensor_reduce(negmax[:, k, t:t + 1], probs[:, k % 3, K0[t]:K0[t] + KEYS[t]], AX.X, ALU.max, negate=True)
                if sink:
                    link(last)
                    last = V.tensor_scalar(negmax[:, k, :], negmax[:, k, :], sinks[:, 1, k:k + 1], None, ALU.min)
                last.then_inc(sem("max_ready"), 1)

            def normalise(l, k, probs, sink=False):
                dve.wait_ge(sem("exp_done"), heads_before[l] + k + 1)
                if sink:
                    link(V.tensor_tensor(rowsum[:, k, :], rowsum[:, k, :], sinkexp[:, k, :], ALU.add))
                if l < DEPTH and k < HEADS:
                    V.reciprocal(rinv[:, k, :], rowsum[:, k, :]).then_inc(sem("rinv_ready"), 1)
                    return
                link(V.reciprocal(rinv[:, k, :], rowsum[:, k, :]))
                for t in range(NT):
                    w = probs[:, k % 3, K0[t]:K0[t] + KEYS[t]]
                    last = V.tensor_scalar(w, w, rinv[:, k, t:t + 1], None, ALU.mult)
                last.then_inc(sem("probs_ready"), 1)

            def mixer(l):
                work, causal_, iw = A["work"], causal, A["iw"]
                if l == 0:
                    dve.wait_ge(sem("masks_in"), 64)
                evacuated(dve, (l, "dviw"))
                for h in range(IDX_HEADS):
                    evacuated(dve, (l, f"idx{h}"))
                    for t in range(NT):
                        c = slice(K0[t], K0[t] + KEYS[t])
                        prev = causal_[:, c] if h == 0 else work[:, c]
                        last = V.scalar_tensor_tensor(work[:, c], A["relu"][:, h % 2, c], iw[:, t, h:h + 1], prev, ALU.mult, ALU.add)
                    last.then_inc(sem("idx_added"), 1)
                    dve.wait_ge(sem("idx_added"), IDX_HEADS * l + h + 1)
                evacuated(dve, (l, "ms"))
                link(V.reciprocal(A["rstd"], A["rstd"]))
                V.tensor_tensor(A["qaT"], A["qaT"], A["rstd"][:, 0:1, :].to_broadcast([P, 3, T]), ALU.mult).then_inc(sem("latents"), 1)
                V.tensor_tensor(A["kvaT"], A["kvaT"], A["rstd"][:, 1:2, :].to_broadcast([P, 2, T]), ALU.mult).then_inc(sem("latents"), 1)
                half = ROPE // 2
                cos, sin = rope_cs[:, :, 0:half], rope_cs[:, :, half:ROPE]
                kr, tmp, dst = A["krt"], A["rt"][:, 0:2, :], A["kr_tok"]
                V.tensor_tensor(dst[:, :, NOPE:NOPE + half], kr[:, :, 0:half], cos, ALU.mult)
                V.tensor_tensor(dst[:, :, NOPE + half:QK], kr[:, :, 0:half], sin, ALU.mult)
                V.tensor_tensor(tmp[:, :, 0:half], kr[:, :, half:ROPE], sin, ALU.mult)
                link(V.tensor_tensor(tmp[:, :, half:ROPE], kr[:, :, half:ROPE], cos, ALU.mult))
                V.tensor_tensor(dst[:, :, NOPE:NOPE + half], dst[:, :, NOPE:NOPE + half], tmp[:, :, 0:half], ALU.subtract)
                V.tensor_tensor(dst[:, :, NOPE + half:QK], dst[:, :, NOPE + half:QK], tmp[:, :, half:ROPE], ALU.add).then_inc(sem("kr_roped"), 1)
                dve.wait_ge(sem("kr_roped"), l + 1)
                for t in range(NT):
                    for h in range(2):
                        evacuated(dve, (l, f"q{t}{h}"))
                for t in range(NT):
                    q = A["q_tok"][:, t, :].rearrange("p (h n) -> p h n", h=HEADS)
                    x1, x2 = q[:, :, NOPE:NOPE + half], q[:, :, NOPE + half:QK]
                    rt = A["rt"][:, :, :].rearrange("p a b -> p (a b)").rearrange("p (j h n) -> p j h n", j=4, h=HEADS)
                    c = rope_cs[:, t:t + 1, 0:half].to_broadcast([P, HEADS, half])
                    s = rope_cs[:, t:t + 1, half:ROPE].to_broadcast([P, HEADS, half])
                    V.tensor_tensor(rt[:, 0], x1, c, ALU.mult)
                    V.tensor_tensor(rt[:, 1], x2, s, ALU.mult)
                    V.tensor_tensor(rt[:, 2], x1, s, ALU.mult)
                    link(V.tensor_tensor(rt[:, 3], x2, c, ALU.mult))
                    V.tensor_tensor(x1, rt[:, 0], rt[:, 1], ALU.subtract)
                    last = V.tensor_tensor(x2, rt[:, 2], rt[:, 3], ALU.add)
                    if t == 0:
                        link(last)
                    else:
                        last.then_inc(sem("q_roped"), 1)
                        dve.wait_ge(sem("q_roped"), l + 1)
                b = produced(dve, (l, "krT"))
                drained(V.tensor_copy(A["kT"][NOPE:QK, :, :], b[NOPE:QK, 0:T].unsqueeze(1).to_broadcast([ROPE, HEADS, T])), (l, "krT"))
                pr = A["prob"]
                for k in range(2 * HEADS + 1):
                    if k < HEADS:
                        softmax_head(l, k, pr, QK ** -0.5, causal_)
                    elif k < 2 * HEADS:
                        j = k - HEADS
                        link(V.scalar_tensor_tensor(A["bias"][:, k % 2, :], negdist, SLOPES[j], A["msel"], ALU.mult, ALU.add))
                        softmax_head(l, k, pr, HD ** -0.5, A["bias"][:, k % 2, :])
                    if k >= 1:
                        normalise(l, k - 1, pr)
                    if k < HEADS:
                        for t in range(NT):
                            last = V.max(A["top8"][:, t, :], work[:, K0[t]:K0[t] + KEYS[t]])
                        link(last)
                        for t in range(NT):
                            c = slice(K0[t], K0[t] + KEYS[t])
                            last = V.match_replace(work[:, c], A["top8"][:, t, :], work[:, c], PICKED)
                        link(last)
                    if k == HEADS - 1:
                        link(V.tensor_scalar(work, work, PICKED / 2, 1.0, ALU.is_lt, ALU.subtract))
                        link(V.scalar_tensor_tensor(A["msel"], work, -NEG, causal_, ALU.mult, ALU.add))

            def route(l):
                if l == 0:
                    dve.wait_ge(sem("router_in"), 80)
                    dve.wait_ge(sem("pool_set2"), 1)
                evacuated(dve, (l, "logit"))
                link(V.tensor_tensor(biased[:, :, :], aff[:, :, :], rbias[:, :].unsqueeze(1).to_broadcast([P, NT, E]), ALU.add))
                v = biased[:, :, :].rearrange("p t (g k) -> p (t g) k", g=GROUPS)
                V.tensor_tensor(pairs2[:, :, 0:3], v[:, :, 0:3], v[:, :, 1:4], ALU.add)
                V.tensor_tensor(pairs2[:, :, 3:5], v[:, :, 0:2], v[:, :, 2:4], ALU.add)
                link(V.tensor_tensor(pairs2[:, :, 5:6], v[:, :, 0:1], v[:, :, 3:4], ALU.add))
                link(V.tensor_reduce(gscore[:, :, 0:GROUPS], pairs2[:, :, :].rearrange("p (t g) k -> p t g k", t=NT), AX.X, ALU.max))

                def argmax(src, n):
                    for t in range(NT):
                        last = V.max(best[:, t, :], src[:, t, :])
                    link(last)
                    for t in range(NT):
                        last = V.max_index(besti[:, t, :], best[:, t, :], src[:, t, :])
                    link(last)
                    link(V.tensor_copy(bestf[:, :, 0:n], besti[:, :, 0:n]))

                argmax(gscore, 1)
                for t in range(NT):
                    last = V.tensor_scalar(chosen[:, t, :], gidx[:, :], bestf[:, t, 0:1], 1.0, ALU.is_equal, ALU.subtract)
                link(last)
                link(V.scalar_tensor_tensor(biased[:, :, :], chosen[:, :, :], -NEG, biased[:, :, :], ALU.mult, ALU.add))
                argmax(biased, 2)
                for t in range(NT):
                    last = V.tensor_scalar(gates[:, t, :], eidx[:, :], bestf[:, t, 0:1], None, ALU.is_equal)
                link(last)
                for t in range(NT):
                    last = V.scalar_tensor_tensor(chosen[:, t, :], eidx[:, :], bestf[:, t, 1:2], gates[:, t, :], ALU.is_equal, ALU.add)
                last.then_inc(sem("chosen_ready"), 1)
                dve.wait_ge(sem("chosen_ready"), l + 1)
                link(V.tensor_tensor(gates[:, :, :], aff[:, :, :], chosen[:, :, :], ALU.mult))
                link(V.tensor_reduce(wsum[:, :], gates[:, :, :], AX.X, ALU.add))
                link(V.reciprocal(wsum[:, :], wsum[:, :]))
                link(V.tensor_tensor(gates[:, :, :], gates[:, :, :], wsum[:, :].unsqueeze(2).to_broadcast([P, NT, E]), ALU.mult))
                b = produced(dve, (l, "rank"))
                link(V.scalar_tensor_tensor(rank[:, :, :], b[:, 0:NT * E].rearrange("p (t e) -> p t e", t=NT), 1.0, chosen[:, :, :], ALU.add, ALU.mult))
                drained(V.tensor_reduce(most[:, 0:1], b[:, NT * E:NT * E + E], AX.X, ALU.max), (l, "rank"))
                link(V.tensor_scalar(rank[:, :, :], rank[:, :, :], 1.0, None, ALU.subtract))
                evacuated(dve, (l, "rank"))
                link(V.tensor_scalar(most[:, 1:2], most[:, 0:1], float(CAP), None, ALU.is_gt))
                for r in range(2, T // CAP):
                    link(V.scalar_tensor_tensor(most[:, 1:2], most[:, 0:1], float(r * CAP), most[:, 1:2], ALU.is_gt, ALU.add))
                V.tensor_copy(rounds[:, l:l + 1], most[:, 1:2]).then_inc(sem("rounds_ready"), 1)
                slot_of = B["S"].rearrange("p t (e s) -> p (t e) s", e=E)
                V.tensor_tensor(slot_of, rank[:, :, :].rearrange("p t e -> p (t e)").unsqueeze(2).to_broadcast([P, NT * E, CAP]),
                                pos[:, :].unsqueeze(1).to_broadcast([P, NT * E, CAP]), ALU.is_equal).then_inc(sem("slots_ready"), 1)
                dve.wait_ge(sem("slots_ready"), 2 * l + 1)
                V.tensor_tensor(B["SG"].rearrange("p t (e s) -> p (t e) s", e=E), slot_of,
                                gates[:, :, :].rearrange("p t e -> p (t e)").unsqueeze(2).to_broadcast([P, NT * E, CAP]), ALU.mult)\
                    .then_inc(sem("slots_ready"), 1)
                link(V.tensor_scalar(res[:, :, :], x_tok[:, :, :], ALPHA, None, ALU.mult))

            def experts(l):
                evacuated(dve, (l, "sgT3"))
                with dve.Fori(0, PAIRS) as i:
                    u = J[(l, "M11")]
                    dve.wait_ge(bank_full[u.place], u.before + 1 - u.step + i * u.step)
                    V.tensor_scalar(B["sgp"], B["sgT"][:, bass.ds(i, 1), :].rearrange("p o n -> p (o n)"), 1.0, None, ALU.mult)\
                        .then_inc(sem("gates_copied"), 1)
                    b = produced(dve, (l, "Hu"), i)
                    evacuated(dve, (l, "Hg"), i)
                    drained(V.tensor_tensor(B["act"], B["silu"], b[:, :], ALU.mult), (l, "Hu"))
                    for t in range(NT):
                        for h in range(2):
                            b = produced(dve, (l, f"M{t}{h}"), i)
                            r = res[:, t, 512 * h:512 * (h + 1)]
                            drained(V.tensor_tensor(r, r, b[:, :], ALU.add), (l, f"M{t}{h}"))
                for n in ("M10", "M11"):
                    evacuated(dve, (l, n), PAIRS - 1)

            def overflow(l):
                n_rounds = more_rounds(dve, l)
                with dve.If(n_rounds > 0):
                    V.tensor_copy(most[:, 2:3], most[:, 0:1]).then_inc(over(l, "added"), 1)
                    with dve.Fori(0, n_rounds) as r:
                        V.tensor_scalar(rank[:, :, :], rank[:, :, :], float(CAP), None, ALU.subtract).then_inc(over(l, "ranked"), 1)
                        with dve.Fori(0, PAIRS) as p:
                            n = r * PAIRS + p
                            dve.wait_ge(over(l, "ranked"), r + 1)
                            two = bass.ds(2 * p, 2)
                            for t in range(NT):
                                last = V.tensor_tensor(B["S"][:, t, 0:P].rearrange("p (e s) -> p e s", e=2),
                                                       rank[:, t, two].unsqueeze(2).to_broadcast([P, 2, CAP]),
                                                       pos[:, :].unsqueeze(1).to_broadcast([P, 2, CAP]), ALU.is_equal)
                            last.then_inc(over(l, "slots"), 1)
                            dve.wait_ge(over(l, "slots"), 2 * n + 1)
                            for t in range(NT):
                                last = V.tensor_tensor(B["SG"][:, t, 0:P].rearrange("p (e s) -> p e s", e=2),
                                                       B["S"][:, t, 0:P].rearrange("p (e s) -> p e s", e=2),
                                                       gates[:, t, two].unsqueeze(2).to_broadcast([P, 2, CAP]), ALU.mult)
                            last.then_inc(over(l, "slots"), 1)
                            dve.wait_ge(over(l, "act"), 4 * n + 2)
                            V.tensor_tensor(B["act"], B["silu"], bank[3][:, :], ALU.mult).then_inc(over(l, "hidden"), 1)
                            dve.wait_ge(over(l, "pe"), 5 * n + 5)
                            for t in range(NT):
                                for h in range(2):
                                    y = res[:, t, 512 * h:512 * (h + 1)]
                                    last = V.tensor_tensor(y, y, bank[out_banks[2 * t + h]][:, :], ALU.add)
                            last.then_inc(over(l, "added"), 1)
                            dve.wait_ge(over(l, "added"), n + 2)
                    V.tensor_copy(most[:, 3:4], most[:, 0:1]).then_inc(over(l, "done"), 1)

            for l in range(DEPTH):
                mixer(l)
                norm(2 * l, l, "y", True)
                route(l)
                experts(l)
                overflow(l)
                norm(2 * l + 1, l, "m", False)
            def low_tokens(l, y, times_before):
                for n, (t, g) in enumerate((t, g) for t in range(NT) for g in range(2)):
                    dve.wait_ge(sem("x_high_ready"), 4 * times_before + n + 1)
                    x = (slice(None), slice(4 * g, 4 * g + 4), slice(P * t, P * (t + 1)))
                    b = produced(dve, (l, f"{y}xT{t}{g}"))
                    drained(V.tensor_tensor(x_low[x], b[:, :].rearrange("p (c n) -> p c n", c=4), x_high[x].bitcast(F32), ALU.subtract), (l, f"{y}xT{t}{g}"))

            def low_slot(l, name, n):
                raw = slot(W[(l, name)], KD, 256)
                for ab in range(2):
                    dve.wait_ge(sem("high_ready"), 2 * n + ab + 1)
                    V.tensor_tensor(w_low[n % 2][:, ab, :, :], raw[:, :, P * ab:P * (ab + 1)], w_high[n % 2][:, ab, :, :].bitcast(F32), ALU.subtract)\
                        .then_inc(sem("split"), 1)

            def recurrent():
                low_tokens(1, "m", 0)
                names = [f"h{n}{i}" for n in "qf" for i in range(4)]
                for n in range(2):
                    low_slot(2, names[n], n)
                b = produced(dve, (2, "lbT"))
                drained(V.tensor_copy(lb[:, 0:2, :], b[:, 0:16].rearrange("p (a c) -> p a c", a=2)), (2, "lbT"))
                evacuated(dve, (2, "lbT"))
                link(V.tensor_tensor(lb[:, 2, :], lb[:, 0, :], lb[:, 1, :], ALU.max))
                V.tensor_tensor(lb[:, 0:2, :], lb[:, 0:2, :], lb[:, 2:3, :].to_broadcast([P, 2, 8]), ALU.subtract).then_inc(sem("lb_shifted"), 1)
                dve.wait_ge(sem("lb_exp"), 1)
                link(V.tensor_tensor(lb[:, 3, :], lb[:, 0, :], lb[:, 1, :], ALU.add))
                link(V.reciprocal(lb[:, 3, :], lb[:, 3, :]))
                link(V.tensor_tensor(lb[:, 2, :], lb[:, 0, :], lb[:, 3, :], ALU.mult))
                link(V.tensor_scalar(lb[:, 3, :], lb[:, 2, :], -1.0, 1.0, ALU.mult, ALU.add))
                for n in range(2, 8):
                    low_slot(2, names[n], n)

                def low_rows(n):
                    u = W[(2, rows_name(n))]
                    for ab in range(2):
                        half = slice(SLOT // 2 * ab, SLOT // 2 * (ab + 1))
                        dve.wait_ge(sem("high_ready"), 2 * (8 + n) + ab + 1)
                        V.tensor_tensor(flat(w_low[n % 2])[:, half], slots[u.place][:, half], flat(w_high[n % 2])[:, half].bitcast(F32), ALU.subtract)\
                            .then_inc(sem("split"), 1)

                low_rows(0)
                for h in range(HG_HEADS):
                    if h % 2 == 0:
                        evacuated(dve, (2, f"hf{h // 2}"))
                    last = V.tensor_scalar(C["Pd"][:, h, :], C["Pd"][:, h, :], lb[:, 3, h:h + 1], lb[:, 2, h:h + 1], ALU.mult, ALU.add)
                link(last)
                V.tensor_scalar(C["K"], C["Pd"], -1.0, 1.0, ALU.mult, ALU.add).then_inc(sem("keys_ready"), 1)
                dve.wait_ge(sem("keys_ready"), 1)
                low_rows(1)
                dve.wait_ge(sem("recur_set"), 4)
                dve.wait_ge(sem("levels_in"), 16)
                for i in range(4):
                    evacuated(dve, (2, f"hq{i}"))

                def merge(li):
                    for s in range(2):
                        for t in range(NT):
                            b = produced(dve, (2, f"L{li}{s}{t}"))
                            if li:
                                evacuated(dve, (2, f"L{li - 1}{s}{t}"))
                            drained(V.copy_predicated(C["SA"][:, 4 * s:4 * s + 4, P * t:P * (t + 1)],
                                                      levels[:, li:li + 1, :].to_broadcast([P, 4, P]),
                                                      b[:, :].rearrange("p (c n) -> p c n", c=4)), (2, f"L{li}{s}{t}"))

                for li, m in enumerate(LEVELS + [P]):
                    for s in range(2):
                        Pd, Sd, Q, K, Qt, Kt = (C[n][:, 4 * s:4 * s + 4, :].rearrange("p h n -> p (h n)").rearrange("p (b j m) -> p b j m", j=2, m=m)
                                                for n in ("Pd", "Sd", "Q", "K", "Qt", "Kt"))
                        if li:
                            dve.wait_ge(sem("decays"), 2 * (li - 1) + s + 1)
                            produced(dve, (2, f"L{li}{s}1"))
                        V.tensor_tensor(Kt[:, :, 0, :], K[:, :, 0, :], Sd[:, :, 0, :], ALU.mult)
                        V.tensor_tensor(Qt[:, :, 1, :], Q[:, :, 1, :], Pd[:, :, 1, :], ALU.mult).then_inc(sem("scaled"), 1)
                    merge(li)
                    if 1 <= li < len(LEVELS):
                        low_rows(li + 1)
                evacuated(dve, (2, "hv11"))
                dve.wait_ge(sem("gnorm_in"), 16)
                G16 = res[:, :, :].rearrange("p t (h n) -> p (t h) n", n=HG_DIM)
                link(V.tensor_tensor(G16, G16, gnorm[:, :].unsqueeze(1).to_broadcast([P, NT * HG_HEADS, P]), ALU.mult))
                for t in range(NT):
                    for s in range(2):
                        evacuated(dve, (2, f"R{t}{s}"))
                    sums = hsum[:, HG_HEADS * t:HG_HEADS * (t + 1)]
                    o = C["O"][:, t, :].rearrange("p (h n) -> p h n", n=HG_DIM)
                    link(V.tensor_tensor(C["O2"][:, t, :], C["O"][:, t, :], C["O"][:, t, :], ALU.mult))
                    V.tensor_reduce(sums, C["O2"][:, t, :].rearrange("p (h n) -> p h n", n=HG_DIM), AX.X, ALU.add).then_inc(sem("head_sums"), 1)
                    dve.wait_ge(sem("head_roots"), t + 1)
                    link(V.reciprocal(sums, sums))
                    link(V.tensor_tensor(o, o, sums.unsqueeze(2).to_broadcast([P, HG_HEADS, P]), ALU.mult))
                    V.tensor_tensor(C["O"][:, t, :], C["O"][:, t, :], res[:, t, :], ALU.mult).then_inc(sem("recur_out"), 1)
                dve.wait_ge(sem("recur_out"), 2)

            def feed_forward(l):
                low_tokens(l, "y", 2 * (l - DEPTH) + 1)
                evacuated(dve, (l, "cw"))
                cw = F["cw"].rearrange("p k (a n) -> p k a n", a=2)

                def split(j, i, c):
                    before_ = 2 * (FFN_UNIT[l] + c + (2 * STEPS - 2 if i is None else 2 * j)) + (0 if i is None else 8 * i)
                    for ab, n in enumerate("ab"):
                        raw = slot(W[(l, f"F{n}{j}")], KD, 256)
                        dve.wait_ge(sem("high_ready"), before_ + (ab + 1))
                        V.tensor_tensor(w_low[c][:, ab, :, :], raw[:, :, P * c:P * (c + 1)], w_high[c][:, ab, :, :].bitcast(F32), ALU.subtract)\
                            .then_inc(sem("split"), 1)

                def step(j, i, following):
                    base = (l - 2) * STEPS + (STEPS - 1 if i is None else j)
                    more = 0 if i is None else 2 * i
                    w = F["cws"][:, j % 2, :].rearrange("p (k a c) -> p k a c", k=4, a=2)
                    if i is None:
                        src = lambda a: cw[:, :, a, GC - 2:GC]
                    else:
                        src = lambda a: cw[:, :, a, bass.ds(4 * i + 2 * j, 2)]
                    V.tensor_scalar(w[:, :, 0, :], src(0), 1.0, None, ALU.mult)
                    V.tensor_scalar(w[:, :, 1, :], src(1), 1.0, None, ALU.mult).then_inc(sem("taps"), 1)
                    dve.wait_ge(sem("taps"), base + 1 + more)
                    for c in range(2):
                        b = produced(dve, (l, f"U{j}{c}"), i)
                        if following:
                            split(*following, c)
                        dve.wait_ge(sem("conv_begun"), 2 * base + c + 1 + 2 * more)
                        for ab in range(2):
                            y, x = F["conv"][:, 2 * c + ab, :], b[:, T * ab:T * (ab + 1)]
                            last = V.scalar_tensor_tensor(y[:, 1:T], x[:, 0:T - 1], w[:, 1, ab, c:c + 1], y[:, 1:T], ALU.mult, ALU.add)
                        last.then_inc(sem("tap_done"), 1)
                        dve.wait_ge(sem("tap_done"), 2 * base + c + 1 + 2 * more)
                        for ab in range(2):
                            y, x = F["conv"][:, 2 * c + ab, :], b[:, T * ab:T * (ab + 1)]
                            last = V.scalar_tensor_tensor(y[:, 2:T], x[:, 0:T - 2], w[:, 0, ab, c:c + 1], y[:, 2:T], ALU.mult, ALU.add)
                            if ab == 0:
                                last.then_inc(sem("conv_done"), 1)
                        drained(last, (l, f"U{j}{c}"))
                    for c in range(2):
                        dve.wait_ge(sem("gate_done"), 2 * base + c + 1 + 2 * more)
                        if c == 0:
                            evacuated(dve, (l, f"U{j}0"), i)
                            evacuated(dve, (l, f"U{j}1"), i)
                        if i is None:
                            g = F["gT"][:, GC - 2 + c, :]
                        else:
                            g = F["gT"][:, bass.ds(4 * i + (2 * j + c), 1), :].rearrange("p o n -> p (o n)")
                        V.tensor_tensor(g, F["gate"][:, c, :], F["conv"][:, 2 * c + 1, :], ALU.mult).then_inc(sem("gated"), 1)

                for c in range(2):
                    split(0, 0, c)
                with dve.Fori(0, STEPS // 2 - 1) as i:
                    step(0, i, (1, i))
                    step(1, i, (0, i + 1))
                i = STEPS // 2 - 1
                step(0, i, (1, i))
                step(1, i, (2, None))
                step(2, None, None)

            recurrent()
            norm(4, 2, "y", True)
            feed_forward(2)
            norm(5, 2, "z", True)
            dve.wait_ge(sem("sinks_in"), 16)
            link(V.tensor_scalar(sinks[:, 1, :], sinks[:, 0, :], -1.0, None, ALU.mult))
            low_tokens(2, "z", 2)
            for n, name in enumerate(["kv0"] + [f"sq{i}" for i in range(4)]):
                low_slot(3, name, KV_UNIT + n)
            dve.wait_ge(sem("bias_ready"), 1)
            for k in range(SWQ + 1):
                if k < SWQ:
                    softmax_head(3, k, G["prob"], SWD ** -0.5, G["bias"][:, k, :], sink=True)
                if k >= 1:
                    normalise(3, k - 1, G["prob"], sink=True)
            norm(6, 3, "y", True)
            feed_forward(3)
            norm(7, 3, "z", True)

        @block.tensor
        def _(pe):
            mm = nc.tensor.matmul

            def product(dst, lhs, rhs, n):
                for c in range(n):
                    last = mm(dst, lhs(c), rhs(c), start=(c == 0), stop=(c == n - 1))
                return last

            def tok(t):
                return slice(P * t, P * (t + 1))

            def transpose_x(l, y, ready):
                for t in range(NT):
                    ready(t)
                    for g in range(2):
                        b = reuse(pe, (l, f"{y}xT{t}{g}"))
                        for c in range(4):
                            last = nc.tensor.transpose(b[:, P * c:P * (c + 1)], x_tok[:, t, P * (4 * g + c):P * (4 * g + c + 1)], ident[:, :])
                        done(last, (l, f"{y}xT{t}{g}"))

            def heads(l, n, score, value, probs, probsT):
                for k in range(n + 3):
                    if k < n:
                        b = reuse(pe, (l, f"S{k}"))
                        for t in range(NT):
                            last = score(k, t, b[:, K0[t]:K0[t] + KEYS[t]])
                        done(last, (l, f"S{k}"))
                    if 0 <= k - 2 < n:
                        j = k - 2
                        b = reuse(pe, (l, f"T{j}"))
                        if l < DEPTH and j < HEADS:
                            pe.wait_ge(sem("probs_scaled"), HEADS * l + j + 1)
                        else:
                            pe.wait_ge(sem("probs_ready"), HEADS * l + j - HEADS + 1 if l < DEPTH else HEADS * DEPTH + j + 1)
                        for c in range(3):
                            last = nc.tensor.transpose(b[:, tok(c)], probs[:, j % 3, tok(c)], ident[:, :])
                        done(last, (l, f"T{j}"))
                    if 0 <= k - 3 < n:
                        j = k - 3
                        o = f"O{j // 2}"
                        if j % 2 == 0:
                            reuse(pe, (l, o))
                        b = bank[J[(l, o)].place]
                        rows = slice(64 * (j % 2), 64 * (j % 2) + 64)
                        evacuated(pe, (l, f"T{j}"))
                        mm(b[rows, 0:P], value(j, 0), probsT[:, j % 2, 0:P], start=True, stop=True)
                        mm(b[rows, P:T], value(j, 0), probsT[:, j % 2, P:2 * P], start=True, stop=False)
                        last = mm(b[rows, P:T], value(j, 1), probsT[:, j % 2, 2 * P:3 * P], start=False, stop=True)
                        if j % 2:
                            done(last, (l, o))

            def project_out(l, y, mixT, names):
                us = [loaded(pe, (l, n)) for n in names]
                for t in range(NT):
                    for h in range(2):
                        b = reuse(pe, (l, f"{y}{t}{h}"))
                        done(product(b[:, :], lambda c: mixT[:, c, tok(t)],
                                     lambda c: slot(us[c // 2], 2, 1024)[:, c % 2, 512 * h:512 * (h + 1)], KD), (l, f"{y}{t}{h}"))

            def mixer(l):
                f1, f2 = loaded(pe, (l, "f1")), loaded(pe, (l, "f2"))
                s1, s2 = slot(f1, KD, C_IQ - C_DK), slot(f2, KD, IN_COLS - C_IK)
                s3 = slot(loaded(pe, (l, "c")), KD, C_DQ - 512)
                b = reuse(pe, (l, "ikdk"))
                for c in range(KD):
                    mm(b[0:N_IKW, 0:T], s2[:, c, :], xT[:, c, :], start=(c == 0), stop=(c == KD - 1))
                    mm(b[64:64 + ROPE, 0:T], s3[:, c, P:P + ROPE], xT[:, c, :], start=(c == 0), stop=(c == KD - 1))
                done(product(b[:, T:2 * T], lambda c: s1[:, c, :], lambda c: xT[:, c, :], KD), (l, "ikdk"))

                def pair(name):
                    u = loaded(pe, (l, name))
                    b = reuse(pe, (l, name))
                    s = slot(u, KD, 256)
                    for i in range(2):
                        last = product(b[:, T * i:T * (i + 1)], lambda c: s[:, c, P * i:P * (i + 1)], lambda c: xT[:, c, :], KD)
                    done(last, (l, name))

                pair("iq")
                b = reuse(pe, (l, "dviw"))
                evacuated(pe, (l, "ikdk"))
                for t in range(NT):
                    nc.tensor.transpose(b[:, tok(t)], A["ikdk"][:, 1, tok(t)], ident[:, :])
                for t in range(NT):
                    o = T + N_IKW * t
                    nc.tensor.transpose(b[:, o:o + N_IKW], A["ikdk"][0:N_IKW, 0, tok(t)], ident[0:N_IKW, 0:N_IKW])
                for t in range(NT):
                    o = O_KR + ROPE * t
                    last = nc.tensor.transpose(b[:, o:o + ROPE], A["ikdk"][64:64 + ROPE, 0, tok(t)], ident[64:64 + ROPE, 64:64 + ROPE])
                done(last, (l, "dviw"))
                if l == 0:
                    pe.wait_ge(sem("rep_in"), 16)
                    pe.wait_ge(sem("pool_set"), 4)
                b = reuse(pe, (l, "rep"))
                mm(b[:, 0:T], rep[0:IDX_DIM, 0, :], A["ikdk"][0:IDX_DIM, 0, :], start=True, stop=True)
                done(mm(b[:, T:2 * T], rep[0:HD, 1, :], A["ikdk"][0:HD, 1, :], start=True, stop=True), (l, "rep"))
                pair("a")
                evacuated(pe, (l, "iq"))
                evacuated(pe, (l, "rep"))
                for h in range(IDX_HEADS):
                    b = reuse(pe, (l, f"idx{h}"))
                    r = slice(32 * (h % 4), 32 * (h % 4) + 32)
                    for t in range(NT):
                        last = mm(b[:, K0[t]:K0[t] + KEYS[t]], A["iqT"][r, h // 4, tok(t)], A["ikdkT"][r, 0, 0:KEYS[t]], start=True, stop=True)
                    done(last, (l, f"idx{h}"))
                pair("b")
                b = reuse(pe, (l, "c"))
                done(product(b[:, 0:T], lambda c: s3[:, c, 0:P], lambda c: xT[:, c, :], KD), (l, "c"))
                b = reuse(pe, (l, "ms"))
                for n in "abc":
                    evacuated(pe, (l, n))
                product(b[:, 0:T], lambda c: ones[:, :], lambda c: A["sq"][:, c, :], 3)
                done(product(b[:, T:2 * T], lambda c: ones[:, :], lambda c: A["sq"][:, 3 + c, :], 2), (l, "ms"))
                pair("d")
                pair("e")
                pe.wait_ge(sem("latents"), 2 * l + 2)
                us = [loaded(pe, (l, "qup0")), loaded(pe, (l, "qup1"))]
                for t in range(NT):
                    for h in range(2):
                        b = reuse(pe, (l, f"q{t}{h}"))
                        done(product(b[:, 0:384], lambda c: A["qaT"][:, c, tok(t)], lambda c: slot(us[h], 3, 384)[:, c, :], 3), (l, f"q{t}{h}"))
                uk = slot(loaded(pe, (l, "uk")), 2, 512)
                for j in range(4):
                    b = reuse(pe, (l, f"kn{j}"))
                    for i in range(2):
                        h = 2 * j + i
                        last = product(b[0:NOPE, T * i:T * (i + 1)], lambda c: uk[:, c, NOPE * h:NOPE * (h + 1)], lambda c: A["kvaT"][:, c, :], 2)
                    done(last, (l, f"kn{j}"))
                uv = slot(loaded(pe, (l, "uv")), 2, 512)
                for t in range(NT):
                    b = reuse(pe, (l, f"v{t}"))
                    done(product(b[:, :], lambda c: A["kvaT"][:, c, tok(t)], lambda c: uv[:, c, :], 2), (l, f"v{t}"))
                b = reuse(pe, (l, "krT"))
                pe.wait_ge(sem("kr_roped"), l + 1)
                for t in range(NT):
                    last = nc.tensor.transpose(b[0:QK, tok(t)], A["kr_tok"][:, t, :], ident[:, :])
                done(last, (l, "krT"))
                pe.wait_ge(sem("q_roped"), l + 1)
                for j in range(4):
                    b = reuse(pe, (l, f"qT{j}"))
                    for i in range(4):
                        h, t = 2 * j + i // 2, i % 2
                        last = nc.tensor.transpose(b[0:QK, P * i:P * (i + 1)], A["q_tok"][:, t, QK * h:QK * (h + 1)], ident[:, :])
                    done(last, (l, f"qT{j}"))
                for n in ["d", "e", "kn0", "kn1", "kn2", "kn3", "v0", "v1", "krT", "qT0", "qT1", "qT2", "qT3"]:
                    evacuated(pe, (l, n))

                def score(k, t, dst):
                    if k < HEADS:
                        return mm(dst, A["qT"][0:QK, k, tok(t)], A["kT"][0:QK, k, 0:KEYS[t]], start=True, stop=True)
                    h = k - HEADS
                    r = slice(64 * (h % 2), 64 * (h % 2) + 64)
                    return mm(dst, A["dqT"][r, h // 2, tok(t)], A["ikdkT"][r, 1, 0:KEYS[t]], start=True, stop=True)

                def value(k, t):
                    return A["v_tok"][:, t, HD * k:HD * (k + 1)] if k < HEADS else A["dv"][:, t, :]

                heads(l, 2 * HEADS, score, value, A["prob"], A["probT"])
                for j in range(HEADS):
                    evacuated(pe, (l, f"O{j}"))
                project_out(l, "y", A["mixT"], ["wo0", "wo1", "wo2", "wo3"])

            pe.wait_ge(sem("ident_in"), 16)
            transpose_x(0, "in", lambda t: pe.wait_ge(sem(f"x_in{t}"), 16))
            pe.wait_ge(sem("gains_in"), 64)
            b = reuse(pe, (0, "gains"))
            done(nc.tensor.transpose(b[:, 0:10], gain_rows[:, :], ident[0:10, 0:10]), (0, "gains"))
            for t in range(NT):
                for g in range(2):
                    evacuated(pe, (0, f"inxT{t}{g}"))
            def route(l):
                for t in range(NT):
                    for g in range(2):
                        evacuated(pe, (l, f"yxT{t}{g}"))
                if l == 0:
                    pe.wait_ge(sem("router_in"), 80)
                    pe.wait_ge(sem("masks_in"), 64)
                b = reuse(pe, (l, "logit"))
                for t in range(NT):
                    last = product(b[:, E * t:E * (t + 1)], lambda c: xT[:, c, tok(t)], lambda c: router[:, c, :], KD)
                done(last, (l, "logit"))
                b = reuse(pe, (l, "rank"))
                pe.wait_ge(sem("chosen_ready"), l + 1)
                mm(b[:, 0:E], before, chosen[:, 0, :], start=True, stop=True)
                mm(b[:, E:2 * E], before, chosen[:, 1, :], start=True, stop=False)
                mm(b[:, E:2 * E], ones[:, :], chosen[:, 0, :], start=False, stop=True)
                done(product(b[:, 2 * E:3 * E], lambda c: ones[:, :], lambda c: chosen[:, c, :], NT), (l, "rank"))

            def gates_by_slot(l):
                pe.wait_ge(sem("slots_ready"), 2 * l + 2)
                for q in range(4):
                    b = reuse(pe, (l, f"sgT{q}"))
                    for i in range(4):
                        last = nc.tensor.transpose(b[:, tok(i)], B["SG"][:, i % 2, tok(2 * q + i // 2)], ident[:, :])
                    done(last, (l, f"sgT{q}"))

            def gate_up(l, banks_gu):
                for q, (m, half) in enumerate((m, half) for half in range(2) for m in "gu"):
                    ws = [slot(W[(l, f"{m}{e}{half}")], 4, 512) for e in range(2)]
                    for c in range(4):
                        for e in range(2):
                            rows = slice(CAP * e, CAP * (e + 1))
                            last = mm(banks_gu["gu".index(m)][rows, :], B["xe"][:, 4 * half + c, rows], ws[e][:, c, :],
                                      start=(half == 0 and c == 0), stop=(half == 1 and c == 3))
                        if c == 3:
                            yield q, last

            def down(l, out, half):
                for c in range(MF):
                    for e in range(2):
                        rows = slice(CAP * e, CAP * (e + 1))
                        last = mm(out[rows, :], B["actT"][:, c, rows], slot(W[(l, f"w{e}{c // 2}")], 2, 1024)[:, c % 2, 512 * half:512 * (half + 1)],
                                  start=(c == 0), stop=(c == MF - 1))
                return last

            def experts(l):
                def tokens(i):
                    for g in range(2):
                        b = reuse(pe, (l, f"G{g}"), i)
                        for c in range(4):
                            for t in range(NT):
                                last = mm(b[:, tok(c)], x_tok[:, t, tok(4 * g + c)], B["S"][:, t, bass.ds(i * P, P)], start=(t == 0), stop=(t == 1))
                        done(last, (l, f"G{g}"))

                def pair(i, last_pair=False):
                    evacuated(pe, (l, "G0"), i)
                    evacuated(pe, (l, "G1"), i)
                    bs = [reuse(pe, (l, "Hg"), i), reuse(pe, (l, "Hu"), i)]
                    for e in range(2):
                        loaded(pe, (l, f"g{e}0"), i)
                    for q, last in gate_up(l, bs):
                        if q < 2:
                            last.then_inc(sem("quarter_used"), 1)
                        elif q == 2:
                            done(last, (l, "Hg"))
                        else:
                            done(last, (l, "Hu"))
                        if q < 3:
                            m, half = "ugu"[q], (0, 1, 1)[q]
                            for e in range(2):
                                loaded(pe, (l, f"{m}{e}{half}"), i)
                    if not last_pair:
                        tokens(i + 1)
                    b = reuse(pe, (l, "A"), i)
                    evacuated(pe, (l, "Hu"), i)
                    for c in range(MF):
                        last = nc.tensor.transpose(b[:, tok(c)], B["act"][:, tok(c)], ident[:, :])
                    done(last, (l, "A"))
                    for e in range(2):
                        for n in range(2):
                            loaded(pe, (l, f"w{e}{n}"), i)
                    evacuated(pe, (l, "A"), i)
                    for h in range(2):
                        b = reuse(pe, (l, f"Y{h}"), i)
                        done(down(l, b, h), (l, f"Y{h}"))
                    pe.wait_ge(sem("gates_copied"), i + (PAIRS * l + 1))
                    for t in range(NT):
                        for h in range(2):
                            b = reuse(pe, (l, f"M{t}{h}"), i)
                            evacuated(pe, (l, f"Y{h}"), i)
                            done(mm(b[:, :], B["sgp"][:, tok(t)], B["y"][:, 512 * h:512 * (h + 1)], start=True, stop=True), (l, f"M{t}{h}"))

                pe.wait_ge(sem("slots_ready"), 2 * l + 1)
                tokens(0)
                gates_by_slot(l)
                with pe.Fori(0, PAIRS - 1) as i:
                    pair(i)
                pair(PAIRS - 1, last_pair=True)

            def overflow(l):
                n_rounds = more_rounds(pe, l)
                with pe.If(n_rounds > 0):
                    with pe.Fori(0, n_rounds) as r:
                        with pe.Fori(0, PAIRS) as p:
                            n = r * PAIRS + p
                            pe.wait_ge(over(l, "added"), n + 1)
                            pe.wait_ge(over(l, "slots"), 2 * n + 2)
                            for g in range(2):
                                for c in range(4):
                                    product(bank[g][:, tok(c)], lambda t: x_tok[:, t, tok(4 * g + c)], lambda t: B["S"][:, t, 0:P], NT)
                            for t in range(NT):
                                last = nc.tensor.transpose(bank[6][:, tok(t)], B["SG"][:, t, 0:P], ident[:, :])
                            last.then_inc(over(l, "pe"), 1)
                            pe.wait_ge(over(l, "act"), 4 * n + 1)
                            pe.wait_ge(over(l, "loaded"), 16 * 12 * (n + 1))
                            for q, last in gate_up(l, [bank[2], bank[3]]):
                                if q == 3:
                                    last.then_inc(over(l, "pe"), 1)
                            pe.wait_ge(over(l, "hidden"), n + 1)
                            for c in range(MF):
                                last = nc.tensor.transpose(bank[4][:, tok(c)], B["act"][:, tok(c)], ident[:, :])
                            last.then_inc(over(l, "pe"), 1)
                            pe.wait_ge(over(l, "act"), 4 * n + 3)
                            for h in range(2):
                                last = down(l, bank[5 + h], h)
                            last.then_inc(over(l, "pe"), 1)
                            pe.wait_ge(over(l, "act"), 4 * n + 4)
                            for t in range(NT):
                                for h in range(2):
                                    last = mm(bank[out_banks[2 * t + h]][:, :], B["sgp"][:, tok(t)], B["y"][:, 512 * h:512 * (h + 1)], start=True, stop=True)
                            last.then_inc(over(l, "pe"), 1)

            for l in range(DEPTH):
                mixer(l)
                transpose_x(l, "y", lambda t: pe.wait_ge(sem("ln_done"), 4 * l + t + 1))
                route(l)
                experts(l)
                overflow(l)
                transpose_x(l, "m", lambda t: pe.wait_ge(sem("ln_done"), 4 * l + 2 + t + 1))
                for t in range(NT):
                    for g in range(2):
                        evacuated(pe, (l, f"mxT{t}{g}"))

            def split_product(dst, high, low):
                for k in range(KD):
                    mm(dst, high[:, k, :], x_high[:, k, :], start=(k == 0), stop=False)
                    mm(dst, high[:, k, :], x_low[:, k, :], start=False, stop=False)
                    last = mm(dst, low[:, k, :], x_high[:, k, :], start=False, stop=(k == KD - 1))
                return last

            def pair(l, name, n):
                b = reuse(pe, (l, name))
                for i in range(2):
                    pe.wait_ge(sem("split"), 2 * n + i + 1)
                    last = split_product(b[:, T * i:T * (i + 1)], w_high[n % 2][:, i, :, :], w_low[n % 2][:, i, :, :])
                done(last, (l, name))

            def recurrent():
                b = reuse(pe, (2, "lbT"))
                pe.wait_ge(sem("lb_in"), 16)
                done(nc.tensor.transpose(b[:, 0:16], lb_rows[:, :], ident[0:16, 0:16]), (2, "lbT"))
                for j, n in enumerate("qf"):
                    for i in range(4):
                        pair(2, f"h{n}{i}", 4 * j + i)
                for li in range(len(LEVELS) + 1):
                    for s in range(2):
                        if li == 0:
                            pe.wait_ge(sem("keys_ready"), 1)
                            for i in range(4):
                                evacuated(pe, (2, f"hq{i}"))
                        else:
                            pe.wait_ge(sem("scaled"), 2 * (li - 1) + s + 1)
                        q, k = (C["Q"], C["K"]) if li == 0 else (C["Qt"], C["Kt"])
                        for t in range(NT):
                            b = reuse(pe, (2, f"L{li}{s}{t}"))
                            for h in range(4):
                                last = mm(b[:, tok(h)], k[:, 4 * s + h, tok(t)], q[:, 4 * s + h, tok(t)], start=True, stop=True)
                            done(last, (2, f"L{li}{s}{t}"))
                    m, h, g = "iv"[li // 4], li % 4 // 2, li % 2
                    names = [(2, f"h{m}{t}{h}") for t in range(NT)]
                    if g == 0:
                        for name in names:
                            reuse(pe, name)
                    high, low = (flat(w[li % 2]).rearrange("p (c n) -> p c n", c=4) for w in (w_high, w_low))
                    for c in range(4):
                        if c % 2 == 0:
                            pe.wait_ge(sem("split"), 2 * (8 + li) + c // 2 + 1)
                        for t in range(NT):
                            dst, k = bank[J[names[t]].place][:, :], 4 * g + c
                            mm(dst, x_high[:, k, tok(t)], high[:, c, :], start=(k == 0), stop=False)
                            mm(dst, x_low[:, k, tok(t)], high[:, c, :], start=False, stop=False)
                            last = mm(dst, x_high[:, k, tok(t)], low[:, c, :], start=False, stop=(k == KD - 1))
                            if k == KD - 1:
                                done(last, names[t])
                for s in range(2):
                    pe.wait_ge(sem("scaled"), 2 * len(LEVELS) + s + 1)
                    b = reuse(pe, (2, f"X{s}"))
                    for h in range(4):
                        last = mm(b[:, tok(h)], C["Kt"][:, 4 * s + h, 0:P], C["Qt"][:, 4 * s + h, P:T], start=True, stop=True)
                    done(last, (2, f"X{s}"))
                for t in range(NT):
                    for s in range(2):
                        evacuated(pe, (2, f"X{s}"))
                        evacuated(pe, (2, f"L{len(LEVELS)}{s}{t}"))
                        b = reuse(pe, (2, f"R{t}{s}"))
                        if t == 0 and s == 0:
                            for h in range(2):
                                for tt in range(2):
                                    evacuated(pe, (2, f"hi{tt}{h}"))
                        for i in range(4):
                            h = 4 * s + i
                            if t:
                                mm(b[:, tok(i)], C["SX"][:, h, :], C["V"][:, 0, tok(h)], start=True, stop=False)
                            last = mm(b[:, tok(i)], C["SA"][:, h, tok(t)], C["V"][:, t, tok(h)], start=(t == 0), stop=True)
                        done(last, (2, f"R{t}{s}"))
                for i in range(4):
                    pe.wait_ge(sem("recur_out"), i // 2 + 1)
                    b = reuse(pe, (2, f"hoT{i}"))
                    for c in range(4):
                        last = nc.tensor.transpose(b[:, tok(c)], C["O"][:, i // 2, tok(4 * (i % 2) + c)], ident[:, :])
                    done(last, (2, f"hoT{i}"))
                for i in range(4):
                    evacuated(pe, (2, f"hoT{i}"))
                project_out(2, "y", C["mixT"], ["ho0", "ho1", "ho2", "ho3"])

            def next_x(l, y, k):
                transpose_x(l, y, lambda t: pe.wait_ge(sem("ln_done"), 2 * k + t + 1))
                for t in range(NT):
                    for g in range(2):
                        evacuated(pe, (l, f"{y}xT{t}{g}"))

            def feed_forward(l):
                b = reuse(pe, (l, "cw"))
                pe.wait_ge(sem("cw_in"), 48 * (l - 1))
                for i in range(2):
                    last = nc.tensor.transpose(b[:, 88 * i:88 * (i + 1)], F["cw_rows"][0:88, i, :], ident[0:88, 0:88])
                done(last, (l, "cw"))

                def step(j, i):
                    for c in range(2):
                        before_ = 2 * (FFN_UNIT[l] + c + (2 * STEPS - 2 if i is None else 2 * j)) + (0 if i is None else 8 * i)
                        b = reuse(pe, (l, f"U{j}{c}"), i)
                        for ab in range(2):
                            pe.wait_ge(sem("split"), before_ + (ab + 1))
                            last = split_product(b[:, T * ab:T * (ab + 1)], w_high[c][:, ab, :, :], w_low[c][:, ab, :, :])
                        done(last, (l, f"U{j}{c}"))

                with pe.Fori(0, STEPS // 2) as i:
                    step(0, i)
                    step(1, i)
                step(2, None)
                bs = [[reuse(pe, (l, f"z{t}{h}")) for h in range(2)] for t in range(NT)]
                for k in range(GC):
                    if k % 2 == 0:
                        w = slot(loaded(pe, (l, f"Fw{k // 2}")), 2, 1024)
                    pe.wait_ge(sem("gated"), (l - 2) * GC + k + 1)
                    for t in range(NT):
                        for h in range(2):
                            last = mm(bs[t][h][:, :], F["gT"][:, k, tok(t)], w[:, k % 2, 512 * h:512 * (h + 1)], start=(k == 0), stop=(k == GC - 1))
                            if k == GC - 1:
                                done(last, (l, f"z{t}{h}"))
                    if k % 2 and k < GC - 1:
                        last.then_inc(sem("down_used"), 1)

            recurrent()
            next_x(2, "y", 4)
            pe.wait_ge(sem("rel_in"), 32)
            for i in range(SWQ):
                b = reuse(pe, (2, f"rb{i}"))
                done(mm(b[:, 0:NK], F["rel"][0:NBUCKET, i:i + 1].to_broadcast([NBUCKET, P]), F["pick"][0:NBUCKET, :], start=True, stop=True), (2, f"rb{i}"))
            feed_forward(2)
            next_x(2, "z", 5)
            pair(3, "kv0", KV_UNIT)
            u = loaded(pe, (3, "kv1"))
            b = reuse(pe, (3, "vv"))
            for t in range(NT):
                last = product(b[:, T * t:T * (t + 1)], lambda c: xT[:, c, tok(t)], lambda c: slot(u, KD, 256)[:, c, :], KD)
            done(last, (3, "vv"))
            evacuated(pe, (3, "kv0"))
            for i in range(SWKV):
                b = reuse(pe, (3, f"kR{i}"))
                r = slice(64 * (i % 2), 64 * (i % 2) + 64)
                done(mm(b[:, 0:T], rep[r, 1, :], G["kraw"][r, i // 2, :], start=True, stop=True), (3, f"kR{i}"))
            for i in range(4):
                pair(3, f"sq{i}", KV_UNIT + 1 + i)
            for n in ("vv", "kR0", "kR1", "kR2", "kR3", "sq0", "sq1", "sq2", "sq3"):
                evacuated(pe, (3, n))

            def score(k, t, dst):
                r = slice(64 * (k % 2), 64 * (k % 2) + 64)
                return mm(dst, G["qT"][r, k // 2, tok(t)], G["kR"][r, k // 4, 0:KEYS[t]], start=True, stop=True)

            heads(3, SWQ, score, lambda k, t: G["v"][:, t, SWD * (k // 4):SWD * (k // 4 + 1)], G["prob"], G["probT"])
            for j in range(SWQ // 2):
                evacuated(pe, (3, f"O{j}"))
            project_out(3, "y", G["mixT"], ["so0", "so1", "so2", "so3"])
            next_x(3, "y", 6)
            feed_forward(3)



_NAMES = [
    "x", "w_in", "q_norm_g", "w_q_up", "kv_norm_g", "w_uk", "w_uv", "w_o", "ln1_g", "ln1_b", "router_w", "router_bias",
    "w_gate", "w_up", "w_down", "ln2_g", "ln2_b", "hgrn_w_in_2", "hgrn_lb_logits_2", "hgrn_gnorm_w_2",
    "hgrn_w_out_2", "swa_w_q_2", "swa_sinks_2", "swa_w_out_2", "shared_w_kv_2", "rel_bias_2", "ffn_w_in_2",
    "ffn_conv_w_2", "ffn_conv_b_2", "ffn_w_out_2", "ln_mix_g_2", "ln_mix_b_2", "ln_ffn_g_2", "ln_ffn_b_2",
]


def kernel(**inputs):
    import concourse.bacc as bacc
    from concourse.bass_utils import run_bass_kernel_spmd

    nc = bacc.Bacc("TRN2", target_bir_lowering=False, num_devices=1)
    arrays = {"in_" + n: np.ascontiguousarray(inputs[n]) for n in _NAMES}
    arrays.update({"in_" + n: a for n, a in const_arrays().items()})
    io = {n[3:]: nc.dram_tensor(n, a.shape, mybir.dt.from_np(a.dtype), kind="ExternalInput").ap() for n, a in arrays.items()}
    out = nc.dram_tensor("out_0", (1, T, D), F32, kind="ExternalOutput").ap()
    build(nc, io, out)
    r = run_bass_kernel_spmd(nc, [arrays], core_ids=[0])
    return r.results[0]["out_0"]
```
